# Optimizing a Trainium2 kernel written in Bass

```python
import jax, jax.numpy as jnp
from jax import lax
import numpy as np
import jax
import jax.numpy as jnp

D_MODEL = 1024
BATCH = 1
SEQ = 512
DEPTH = 2

GLA_HEADS = 4
GLA_DK = D_MODEL // 2 // GLA_HEADS
GLA_DV = D_MODEL // GLA_HEADS
GLA_GATE_RANK = 16
GLA_TAU = 16.0
GLA_CHUNK = 64

NSA_HEADS = 16
NSA_GROUPS = 4
NSA_HPG = NSA_HEADS // NSA_GROUPS
NSA_HEAD_DIM = D_MODEL // NSA_HEADS
CMP_BLOCK = 32
CMP_STRIDE = 16
CMP_HIDDEN = 256
SLC_BLOCK = 64
SLC_TOP_N = 16
WINDOW = 512
Q_BLOCK = 128

ROPE_THETA = 500000.0
ROT_DIM = NSA_HEAD_DIM // 4

N_EXPERTS = 16
N_EXPERT_GROUPS = 4
EXPERTS_PER_GROUP = N_EXPERTS // N_EXPERT_GROUPS
TOP_K = 2
D_FF_EXPERT = D_MODEL // 4

DN_ALPHA = (2 * DEPTH) ** 0.25
DN_BETA = (8 * DEPTH) ** -0.25
LN_EPS = 1e-5
NEG = -1e30
BIG = 1e30

N_GLA_LAYERS = (DEPTH + 1) // 2
N_NSA_LAYERS = DEPTH // 2
GLA_IN = 2 * GLA_HEADS * GLA_DK + 2 * GLA_HEADS * GLA_DV + GLA_GATE_RANK
NSA_IN = NSA_HEADS * NSA_HEAD_DIM + 6 * NSA_GROUPS * NSA_HEAD_DIM + 3 * NSA_HEADS


def layer_norm(x, g, b):
    xf = x.astype(jnp.float32)
    mu = jnp.mean(xf, axis=-1, keepdims=True)
    var = jnp.mean(jnp.square(xf - mu), axis=-1, keepdims=True)
    y = (xf - mu) * lax.rsqrt(var + LN_EPS) * g.astype(jnp.float32) + b.astype(jnp.float32)
    return y.astype(x.dtype)

def partial_rope(t, pos):
    half = ROT_DIM // 2
    inv_freq = jnp.power(ROPE_THETA, -jnp.arange(half, dtype=jnp.float32) * (2.0 / ROT_DIM))
    ang = pos.astype(jnp.float32)[:, None] * inv_freq[None, :]
    cos = jnp.cos(ang).astype(t.dtype)
    sin = jnp.sin(ang).astype(t.dtype)
    x1 = t[..., :half]
    x2 = t[..., half:ROT_DIM]
    return jnp.concatenate([x1 * cos - x2 * sin, x2 * cos + x1 * sin, t[..., ROT_DIM:]], axis=-1)

def masked_softmax(scores, mask):
    return jax.nn.softmax(jnp.where(mask, scores.astype(jnp.float32), NEG), axis=-1)

def gla_mixer(x, w_in, w_gate_up, b_gate, norm_g, w_out):
    B, S, _ = x.shape
    H, DK, DV, C = GLA_HEADS, GLA_DK, GLA_DV, GLA_CHUNK
    N = S // C
    f32 = jnp.float32
    proj = x @ w_in
    cuts = np.cumsum([H * DK, H * DK, H * DV, GLA_GATE_RANK]).tolist()
    q, k, v, g_low, r = jnp.split(proj, cuts, axis=-1)
    log_a = jax.nn.log_sigmoid((g_low @ w_gate_up + b_gate).astype(f32)) / GLA_TAU

    def chunks(t, d):
        return t.reshape(B, N, C, H, d).transpose(0, 3, 1, 2, 4).astype(f32)

    q = chunks(q, DK) * (DK ** -0.5)
    k = chunks(k, DK)
    v = chunks(v, DV)
    b = jnp.cumsum(chunks(log_a, DK), axis=3)
    b_last = b[:, :, :, -1:, :]
    q_dec = q * jnp.exp(b)
    causal = jnp.tril(jnp.ones((C, C), dtype=bool))
    scores = jnp.einsum('bhnid,bhnjd->bhnij', q_dec, k * jnp.exp(-b))
    o_intra = jnp.einsum('bhnij,bhnjv->bhniv', jnp.where(causal, scores, 0.0), v)
    kv = jnp.einsum('bhncd,bhncv->bhndv', k * jnp.exp(b_last - b), v)
    decay = jnp.exp(b_last[:, :, :, 0, :])

    def step(state, inp):
        dec, kv_n = inp
        return dec[..., None] * state + kv_n, state

    _, states = lax.scan(step, jnp.zeros((B, H, DK, DV), f32),
                         (jnp.moveaxis(decay, 2, 0), jnp.moveaxis(kv, 2, 0)))
    o_inter = jnp.einsum('bhncd,nbhdv->bhncv', q_dec, states)
    o = (o_intra + o_inter).transpose(0, 2, 3, 1, 4).reshape(B, S, H, DV)
    o = o * lax.rsqrt(jnp.mean(jnp.square(o), axis=-1, keepdims=True) + LN_EPS) * norm_g.astype(f32)
    o = o.reshape(B, S, H * DV) * jax.nn.silu(r.astype(f32))
    return o.astype(x.dtype) @ w_out

def compress(t, w1, w2, pe):
    B, G, S, Dh = t.shape
    n_chunk = S // CMP_STRIDE
    span = CMP_BLOCK // CMP_STRIDE
    nc = n_chunk - span + 1
    ch = t.reshape(B, G, n_chunk, CMP_STRIDE, Dh)
    blocks = jnp.concatenate([ch[:, :, i:i + nc] for i in range(span)], axis=3)
    blocks = (blocks + pe).reshape(B, G, nc, CMP_BLOCK * Dh)
    return jax.nn.silu(blocks @ w1) @ w2

def nsa_mixer(x, w_in, w_ck1, w_ck2, w_cv1, w_cv2, cmp_pe, w_out):
    B, S, _ = x.shape
    H, G, HPG, Dh = NSA_HEADS, NSA_GROUPS, NSA_HPG, NSA_HEAD_DIM
    f32 = jnp.float32
    proj = x @ w_in
    cuts = np.cumsum([H * Dh] + [G * Dh] * 6).tolist()
    q, kc, vc, ks, vs, kw, vw, gates = jnp.split(proj, cuts, axis=-1)
    pos = jnp.arange(S, dtype=jnp.int32)

    def kv_heads(t):
        return t.reshape(B, S, G, Dh).transpose(0, 2, 1, 3)

    q = partial_rope(q.reshape(B, S, G, HPG, Dh).transpose(0, 2, 3, 1, 4), pos) * (Dh ** -0.5)
    gates = jax.nn.sigmoid(gates.astype(f32)).reshape(B, S, G, HPG, 3).transpose(0, 2, 3, 1, 4)

    span = CMP_BLOCK // CMP_STRIDE
    nc = S // CMP_STRIDE - span + 1
    cmp_end = jnp.arange(nc, dtype=jnp.int32) * CMP_STRIDE + (CMP_BLOCK - 1)
    k_cmp = partial_rope(compress(kv_heads(kc), w_ck1, w_ck2, cmp_pe), cmp_end)
    v_cmp = compress(kv_heads(vc), w_cv1, w_cv2, cmp_pe).astype(f32)

    ns = S // SLC_BLOCK
    n_sel = min(SLC_TOP_N, ns)
    k_slc = partial_rope(kv_heads(ks), pos).reshape(B, G, ns, SLC_BLOCK, Dh)
    v_slc = kv_heads(vs).reshape(B, G, ns, SLC_BLOCK, Dh)
    ratio = SLC_BLOCK // CMP_STRIDE
    pad_amt = ratio * ns + span - 1 - nc

    pad = ((0, 0), (0, 0), (WINDOW, 0), (0, 0))
    k_win = jnp.pad(partial_rope(kv_heads(kw), pos), pad)
    v_win = jnp.pad(kv_heads(vw), pad)

    bi = jnp.arange(B)[:, None, None, None]
    gi = jnp.arange(G)[None, :, None, None]
    blk_ids = jnp.arange(ns)
    in_blk = jnp.arange(SLC_BLOCK)
    win_off = jnp.arange(WINDOW + Q_BLOCK) - WINDOW

    def query_block(qi):
        s0 = qi * Q_BLOCK
        qpos = s0 + jnp.arange(Q_BLOCK)
        qb = lax.dynamic_slice_in_dim(q, s0, Q_BLOCK, axis=3)
        gb = lax.dynamic_slice_in_dim(gates, s0, Q_BLOCK, axis=3)

        cmask = cmp_end[None, :] <= qpos[:, None]
        p_cmp = masked_softmax(jnp.einsum('bghqd,bgcd->bghqc', qb, k_cmp), cmask)
        p_cmp = p_cmp * jnp.any(cmask, axis=-1)[:, None]
        o_cmp = jnp.einsum('bghqc,bgcd->bghqd', p_cmp, v_cmp)

        p_grp = jnp.pad(p_cmp.sum(axis=2), ((0, 0), (0, 0), (0, 0), (0, pad_amt)))
        imp = p_grp[..., 0:ratio * ns:ratio]
        for m in range(ratio):
            for n in range(span):
                if m + n > 0:
                    imp = imp + p_grp[..., m + n:m + n + ratio * ns:ratio]
        cur = (qpos // SLC_BLOCK)[:, None]
        forced = (blk_ids == 0) | (blk_ids == cur) | (blk_ids == cur - 1)
        imp = jnp.where(blk_ids <= cur, jnp.where(forced, BIG, imp), NEG)
        _, sel = lax.top_k(imp, n_sel)
        k_sel = k_slc[bi, gi, sel].reshape(B, G, Q_BLOCK, n_sel * SLC_BLOCK, Dh)
        v_sel = v_slc[bi, gi, sel].reshape(B, G, Q_BLOCK, n_sel * SLC_BLOCK, Dh)
        kpos = (sel[..., None] * SLC_BLOCK + in_blk).reshape(B, G, Q_BLOCK, n_sel * SLC_BLOCK)
        smask = (kpos <= qpos[:, None])[:, :, None]
        p_slc = masked_softmax(jnp.einsum('bghqd,bgqkd->bghqk', qb, k_sel), smask)
        o_slc = jnp.einsum('bghqk,bgqkd->bghqd', p_slc, v_sel.astype(f32))

        kw_b = lax.dynamic_slice_in_dim(k_win, s0, WINDOW + Q_BLOCK, axis=2)
        vw_b = lax.dynamic_slice_in_dim(v_win, s0, WINDOW + Q_BLOCK, axis=2)
        kwpos = s0 + win_off
        rel = qpos[:, None] - kwpos[None, :]
        wmask = (rel >= 0) & (rel < WINDOW) & (kwpos[None, :] >= 0)
        p_win = masked_softmax(jnp.einsum('bghqd,bgkd->bghqk', qb, kw_b), wmask)
        o_win = jnp.einsum('bghqk,bgkd->bghqd', p_win, vw_b.astype(f32))

        o = gb[..., 0:1] * o_cmp + gb[..., 1:2] * o_slc + gb[..., 2:3] * o_win
        return o.astype(x.dtype)

    outs = lax.map(query_block, jnp.arange(S // Q_BLOCK))
    o = outs.transpose(1, 0, 4, 2, 3, 5).reshape(B, S, H * Dh)
    return o @ w_out

def moe_ffn(x, w_router, b_router, w_gate, w_up, w_down):
    B, S, D = x.shape
    xt = x.reshape(B * S, D)
    n = xt.shape[0]
    s = jax.nn.sigmoid((xt @ w_router).astype(jnp.float32))
    biased = s + b_router.astype(jnp.float32)
    grp_score = lax.top_k(biased.reshape(n, N_EXPERT_GROUPS, EXPERTS_PER_GROUP), TOP_K)[0].sum(-1)
    grp = jnp.argmax(grp_score, axis=-1)
    in_grp = (jnp.arange(N_EXPERTS) // EXPERTS_PER_GROUP)[None, :] == grp[:, None]
    _, top_e = lax.top_k(jnp.where(in_grp, biased, NEG), TOP_K)
    w = jnp.take_along_axis(s, top_e, axis=-1)
    w = w / jnp.sum(w, axis=-1, keepdims=True)
    gate = jnp.zeros((n, N_EXPERTS), jnp.float32).at[jnp.arange(n)[:, None], top_e].set(w)
    h = jax.nn.silu(jnp.einsum('nd,edf->nef', xt, w_gate)) * jnp.einsum('nd,edf->nef', xt, w_up)
    h = h * gate[:, :, None].astype(h.dtype)
    return jnp.einsum('nef,efd->nd', h, w_down).reshape(B, S, D)

def first_inputs(seed: int = 0) -> dict:
    key = jax.random.key(seed)
    ks = jax.random.split(key, 20)
    f32 = jnp.float32

    def nrm(k, shape, scale):
        return jax.random.normal(k, shape, f32) * scale

    D = D_MODEL
    nG, nN = N_GLA_LAYERS, N_NSA_LAYERS
    cmp_in = CMP_BLOCK * NSA_HEAD_DIM
    return {
        'x': nrm(ks[0], (BATCH, SEQ, D), 1.0),
        'gla_w_in': nrm(ks[1], (nG, D, GLA_IN), D ** -0.5),
        'gla_w_gate_up': nrm(ks[2], (nG, GLA_GATE_RANK, GLA_HEADS * GLA_DK), GLA_GATE_RANK ** -0.5),
        'gla_b_gate': nrm(ks[3], (nG, GLA_HEADS * GLA_DK), 0.1),
        'gla_norm_g': 1.0 + nrm(ks[4], (nG, GLA_DV), 0.02),
        'gla_w_out': nrm(ks[5], (nG, GLA_HEADS * GLA_DV, D), DN_BETA * (GLA_HEADS * GLA_DV) ** -0.5),
        'nsa_w_in': nrm(ks[6], (nN, D, NSA_IN), D ** -0.5),
        'nsa_w_cmp_k1': nrm(ks[7], (nN, cmp_in, CMP_HIDDEN), cmp_in ** -0.5),
        'nsa_w_cmp_k2': nrm(ks[8], (nN, CMP_HIDDEN, NSA_HEAD_DIM), CMP_HIDDEN ** -0.5),
        'nsa_w_cmp_v1': nrm(ks[9], (nN, cmp_in, CMP_HIDDEN), cmp_in ** -0.5),
        'nsa_w_cmp_v2': nrm(ks[10], (nN, CMP_HIDDEN, NSA_HEAD_DIM), CMP_HIDDEN ** -0.5),
        'nsa_cmp_pe': nrm(ks[11], (nN, CMP_BLOCK, NSA_HEAD_DIM), 0.1),
        'nsa_w_out': nrm(ks[12], (nN, NSA_HEADS * NSA_HEAD_DIM, D), DN_BETA * (NSA_HEADS * NSA_HEAD_DIM) ** -0.5),
        'moe_w_router': nrm(ks[13], (D, N_EXPERTS), D ** -0.5),
        'moe_b_router': nrm(ks[14], (N_EXPERTS,), 0.01),
        'moe_w_gate': nrm(ks[15], (DEPTH, N_EXPERTS, D, D_FF_EXPERT), D ** -0.5),
        'moe_w_up': nrm(ks[16], (DEPTH, N_EXPERTS, D, D_FF_EXPERT), D ** -0.5),
        'moe_w_down': nrm(ks[17], (DEPTH, N_EXPERTS, D_FF_EXPERT, D), DN_BETA * D_FF_EXPERT ** -0.5),
        'ln_g': 1.0 + nrm(ks[18], (DEPTH, 2, D), 0.02),
        'ln_b': nrm(ks[19], (DEPTH, 2, D), 0.02),
    }

def first_block(x, gla_w_in, gla_w_gate_up, gla_b_gate, gla_norm_g, gla_w_out,
              nsa_w_in, nsa_w_cmp_k1, nsa_w_cmp_k2, nsa_w_cmp_v1, nsa_w_cmp_v2, nsa_cmp_pe, nsa_w_out,
              moe_w_router, moe_b_router, moe_w_gate, moe_w_up, moe_w_down, ln_g, ln_b):
    for i in range(DEPTH):
        j = i // 2
        if i % 2 == 0:
            h = gla_mixer(x, gla_w_in[j], gla_w_gate_up[j], gla_b_gate[j], gla_norm_g[j], gla_w_out[j])
        else:
            h = nsa_mixer(x, nsa_w_in[j], nsa_w_cmp_k1[j], nsa_w_cmp_k2[j], nsa_w_cmp_v1[j],
                          nsa_w_cmp_v2[j], nsa_cmp_pe[j], nsa_w_out[j])
        x = layer_norm(DN_ALPHA * x + h, ln_g[i, 0], ln_b[i, 0])
        f = moe_ffn(x, moe_w_router, moe_b_router, moe_w_gate[i], moe_w_up[i], moe_w_down[i])
        x = layer_norm(DN_ALPHA * x + f, ln_g[i, 1], ln_b[i, 1])
    return x


HEAD_DIM = 64
ROT_DIM_2 = HEAD_DIM // 4
BLOCK = 128
RMS_EPS = 1e-6

A_HEADS = (D_MODEL // 2) // HEAD_DIM
A_KV_HEADS = 2
A_WINDOW = 128
CONV_CH = D_MODEL // 2
CONV_WIDTH = 31
C_HEADS = (D_MODEL // 2) // HEAD_DIM
DILATED_PAIRS = ((128, 1), (512, 4), (2048, 16))
D_CH = D_MODEL // 2
D_GROUPS = D_CH // HEAD_DIM
CHUNK = 128
D_FF = ((8 * D_MODEL // 3 + 255) // 256) * 256

A_Q = A_HEADS * HEAD_DIM
A_KV = A_KV_HEADS * HEAD_DIM
EVEN_IN = A_Q + 2 * A_KV + 2 * CONV_CH
EVEN_OUT = A_Q + CONV_CH
C_W = C_HEADS * HEAD_DIM
ODD_IN = 3 * C_W + 2 * D_CH
ODD_OUT = C_W + D_CH
N_EVEN = (DEPTH + 1) // 2
N_ODD = DEPTH // 2


def rms_norm(x, g):
    xf = x.astype(jnp.float32)
    y = xf * lax.rsqrt(jnp.mean(xf * xf, axis=-1, keepdims=True) + RMS_EPS)
    return (y * g.astype(jnp.float32)).astype(x.dtype)

def layer_norm_2(x, g, b):
    xf = x.astype(jnp.float32)
    mu = jnp.mean(xf, axis=-1, keepdims=True)
    xc = xf - mu
    var = jnp.mean(xc * xc, axis=-1, keepdims=True)
    y = xc * lax.rsqrt(var + LN_EPS) * g.astype(jnp.float32) + b.astype(jnp.float32)
    return y.astype(x.dtype)

def rotary(x, pos):
    half = ROT_DIM_2 // 2
    inv_freq = ROPE_THETA ** (-jnp.arange(half, dtype=jnp.float32) * (2.0 / ROT_DIM_2))
    ang = pos.astype(jnp.float32)[:, None] * inv_freq[None, :]
    cos = jnp.cos(ang)[None, :, None, :]
    sin = jnp.sin(ang)[None, :, None, :]
    xr = x[..., :ROT_DIM_2].astype(jnp.float32)
    x1, x2 = xr[..., :half], xr[..., half:]
    rot = jnp.concatenate([x1 * cos - x2 * sin, x2 * cos + x1 * sin], axis=-1).astype(x.dtype)
    return jnp.concatenate([rot, x[..., ROT_DIM_2:]], axis=-1)

def band_attention(q, k, v, max_dist, sink=None):
    B, S, Hq, hd = q.shape
    Hkv = k.shape[2]
    G = Hq // Hkv
    n = S // BLOCK
    qb = q.reshape(B, n, BLOCK, Hkv, G, hd)
    kb = k.reshape(B, n, BLOCK, Hkv, hd)
    vb = v.reshape(B, n, BLOCK, Hkv, hd)
    prev = lambda t: jnp.pad(t, ((0, 0), (1, 0), (0, 0), (0, 0), (0, 0)))[:, :-1]
    kk = jnp.concatenate([prev(kb), kb], axis=2)
    vv = jnp.concatenate([prev(vb), vb], axis=2)
    s = jnp.einsum('bnqhgd,bnjhd->bnhgqj', qb, kk,
                   preferred_element_type=jnp.float32) * (hd ** -0.5)
    qi = jnp.arange(BLOCK)[:, None]
    kj = jnp.arange(2 * BLOCK)[None, :]
    dist = qi + BLOCK - kj
    key_pos = jnp.arange(n)[:, None, None] * BLOCK + kj[None] - BLOCK
    valid = (dist >= 0)[None] & (dist <= max_dist)[None] & (key_pos >= 0)
    s = jnp.where(valid[None, :, None, None], s, -jnp.inf)
    m = jnp.max(s, axis=-1)
    if sink is not None:
        sink_b = sink.astype(jnp.float32).reshape(Hkv, G)[None, None, :, :, None]
        m = jnp.maximum(m, sink_b)
    p = jnp.exp(s - m[..., None])
    l = jnp.sum(p, axis=-1)
    if sink is not None:
        l = l + jnp.exp(sink_b - m)
    o = jnp.einsum('bnhgqj,bnjhd->bnqhgd', p.astype(v.dtype), vv,
                   preferred_element_type=jnp.float32)
    o = o / jnp.transpose(l, (0, 1, 4, 2, 3))[..., None]
    lse = jnp.transpose(m + jnp.log(l), (0, 1, 4, 2, 3)).reshape(B, S, Hq)
    return o.reshape(B, S, Hq, hd).astype(q.dtype), lse

def dilated_window_attention(q, k, v, window, dilation):
    B, S, H, hd = q.shape
    span = dilation * BLOCK
    s_pad = -(-S // span) * span
    sub = s_pad // dilation

    def fold(t):
        t = jnp.pad(t, ((0, 0), (0, s_pad - S), (0, 0), (0, 0)))
        t = t.reshape(B, sub, dilation, t.shape[2], hd)
        return jnp.transpose(t, (0, 2, 1, 3, 4)).reshape(B * dilation, sub, t.shape[3], hd)

    o, lse = band_attention(fold(q), fold(k), fold(v), window // dilation)
    o = jnp.transpose(o.reshape(B, dilation, sub, H, hd), (0, 2, 1, 3, 4)).reshape(B, s_pad, H, hd)
    lse = jnp.transpose(lse.reshape(B, dilation, sub, H), (0, 2, 1, 3)).reshape(B, s_pad, H)
    return o[:, :S], lse[:, :S]

def causal_depthwise_conv(x, w, b):
    C = x.shape[-1]
    y = lax.conv_general_dilated(
        x, w[:, None, :].astype(x.dtype), window_strides=(1,),
        padding=[(CONV_WIDTH - 1, 0)], dimension_numbers=('NWC', 'WIO', 'NWC'),
        feature_group_count=C)
    return y + b.astype(x.dtype)

def even_mixer(h, w_in, sinks, conv_w, conv_b, ln_g, ln_b, w_out, pos):
    B, S, _ = h.shape
    proj = jnp.einsum('bsd,de->bse', h, w_in)
    q, k, v, glu = jnp.split(proj, [A_Q, A_Q + A_KV, A_Q + 2 * A_KV], axis=-1)
    q = rotary(q.reshape(B, S, A_HEADS, HEAD_DIM), pos)
    k = rotary(k.reshape(B, S, A_KV_HEADS, HEAD_DIM), pos)
    v = v.reshape(B, S, A_KV_HEADS, HEAD_DIM)
    a, _ = band_attention(q, k, v, A_WINDOW - 1, sinks)
    a = a.reshape(B, S, A_Q)
    g_a, g_b = jnp.split(glu, 2, axis=-1)
    c = g_a * jax.nn.sigmoid(g_b)
    c = causal_depthwise_conv(c, conv_w, conv_b)
    c = jax.nn.silu(layer_norm_2(c, ln_g, ln_b))
    return jnp.einsum('bse,ed->bsd', jnp.concatenate([a, c], axis=-1), w_out)

def odd_mixer(h, w_in, sgu_ln_g, sgu_ln_b, spatial_w, spatial_b, w_out, pos):
    B, S, _ = h.shape
    proj = jnp.einsum('bsd,de->bse', h, w_in)
    q, k, v, z = jnp.split(proj, [C_W, 2 * C_W, 3 * C_W], axis=-1)
    q = rotary(q.reshape(B, S, C_HEADS, HEAD_DIM), pos)
    k = rotary(k.reshape(B, S, C_HEADS, HEAD_DIM), pos)
    v = v.reshape(B, S, C_HEADS, HEAD_DIM)
    outs, lses = [], []
    for window, dilation in DILATED_PAIRS:
        o_r, lse_r = dilated_window_attention(q, k, v, window, dilation)
        outs.append(o_r)
        lses.append(lse_r)
    alpha = jax.nn.softmax(jnp.stack(lses, axis=0), axis=0)
    c_out = jnp.einsum('rbsh,rbshd->bshd', alpha, jnp.stack(outs, axis=0).astype(jnp.float32))
    c_out = c_out.astype(h.dtype).reshape(B, S, C_W)
    z = jax.nn.gelu(z)
    u, g = jnp.split(z, 2, axis=-1)
    g = layer_norm_2(g, sgu_ln_g, sgu_ln_b).reshape(B, S // CHUNK, CHUNK, D_GROUPS, HEAD_DIM)
    causal = jnp.tril(jnp.ones((CHUNK, CHUNK), dtype=bool))
    w_s = jnp.where(causal[None], spatial_w, 0).astype(g.dtype)
    mixed = jnp.einsum('gts,bcsgd->bctgd', w_s, g) + spatial_b.T.astype(g.dtype)[None, None, :, :, None]
    d_out = u * mixed.reshape(B, S, D_CH)
    return jnp.einsum('bse,ed->bsd', jnp.concatenate([c_out, d_out], axis=-1), w_out)

def swiglu(h, w_gate, w_up, w_down):
    gate = jnp.einsum('bsd,df->bsf', h, w_gate)
    up = jnp.einsum('bsd,df->bsf', h, w_up)
    return jnp.einsum('bsf,fd->bsd', jax.nn.silu(gate) * up, w_down)

def second_inputs(seed: int = 0) -> dict:
    key = jax.random.key(seed)
    ks = jax.random.split(key, 21)
    f32 = jnp.float32

    def nrm(k, shape, scale):
        return jax.random.normal(k, shape, f32) * scale

    return {
        'x': nrm(ks[0], (BATCH, SEQ, D_MODEL), 1.0),
        'ev_norm_g': 1.0 + nrm(ks[1], (N_EVEN, D_MODEL), 0.02),
        'ev_w_in': nrm(ks[2], (N_EVEN, D_MODEL, EVEN_IN), D_MODEL ** -0.5),
        'ev_sinks': nrm(ks[3], (N_EVEN, A_HEADS), 0.5),
        'ev_conv_w': nrm(ks[4], (N_EVEN, CONV_WIDTH, CONV_CH), CONV_WIDTH ** -0.5),
        'ev_conv_b': nrm(ks[5], (N_EVEN, CONV_CH), 0.02),
        'ev_conv_ln_g': 1.0 + nrm(ks[6], (N_EVEN, CONV_CH), 0.02),
        'ev_conv_ln_b': nrm(ks[7], (N_EVEN, CONV_CH), 0.02),
        'ev_w_out': nrm(ks[8], (N_EVEN, EVEN_OUT, D_MODEL), EVEN_OUT ** -0.5),
        'od_norm_g': 1.0 + nrm(ks[9], (N_ODD, D_MODEL), 0.02),
        'od_w_in': nrm(ks[10], (N_ODD, D_MODEL, ODD_IN), D_MODEL ** -0.5),
        'od_sgu_ln_g': 1.0 + nrm(ks[11], (N_ODD, D_CH), 0.02),
        'od_sgu_ln_b': nrm(ks[12], (N_ODD, D_CH), 0.02),
        'od_spatial_w': nrm(ks[13], (N_ODD, D_GROUPS, CHUNK, CHUNK), CHUNK ** -0.5),
        'od_spatial_b': 1.0 + nrm(ks[14], (N_ODD, D_GROUPS, CHUNK), 0.02),
        'od_w_out': nrm(ks[15], (N_ODD, ODD_OUT, D_MODEL), ODD_OUT ** -0.5),
        'ffn_norm_g': 1.0 + nrm(ks[16], (DEPTH, D_MODEL), 0.02),
        'ffn_w_gate': nrm(ks[17], (DEPTH, D_MODEL, D_FF), D_MODEL ** -0.5),
        'ffn_w_up': nrm(ks[18], (DEPTH, D_MODEL, D_FF), D_MODEL ** -0.5),
        'ffn_w_down': nrm(ks[19], (DEPTH, D_FF, D_MODEL), D_FF ** -0.5),
        'final_norm_g': 1.0 + nrm(ks[20], (D_MODEL,), 0.02),
    }

def second_block(x, ev_norm_g, ev_w_in, ev_sinks, ev_conv_w, ev_conv_b, ev_conv_ln_g,
              ev_conv_ln_b, ev_w_out, od_norm_g, od_w_in, od_sgu_ln_g, od_sgu_ln_b,
              od_spatial_w, od_spatial_b, od_w_out, ffn_norm_g, ffn_w_gate, ffn_w_up,
              ffn_w_down, final_norm_g):
    pos = jnp.arange(x.shape[1], dtype=jnp.int32)
    h = x
    for layer in range(DEPTH):
        i = layer // 2
        if layer % 2 == 0:
            h = h + even_mixer(rms_norm(h, ev_norm_g[i]), ev_w_in[i], ev_sinks[i],
                               ev_conv_w[i], ev_conv_b[i], ev_conv_ln_g[i],
                               ev_conv_ln_b[i], ev_w_out[i], pos)
        else:
            h = h + odd_mixer(rms_norm(h, od_norm_g[i]), od_w_in[i], od_sgu_ln_g[i],
                              od_sgu_ln_b[i], od_spatial_w[i], od_spatial_b[i],
                              od_w_out[i], pos)
        h = h + swiglu(rms_norm(h, ffn_norm_g[layer]), ffn_w_gate[layer],
                       ffn_w_up[layer], ffn_w_down[layer])
    return rms_norm(h, final_norm_g)


_first_inputs = second_inputs


def second_inputs(seed=0):
    import zlib

    import numpy as np

    out = dict(_first_inputs(seed))
    spreads = {}
    factors = {'ev_norm_g': 4.382,
     'ev_sinks': 7.141,
     'ev_conv_ln_g': 4.551,
     'ev_conv_ln_b': 5.368,
     'od_norm_g': 5.0,
     'od_sgu_ln_g': 41.425,
     'od_sgu_ln_b': 42.506,
     'od_spatial_b': 29.841,
     'ffn_norm_g': 2.979,
     'final_norm_g': 8.753,
     'ev_conv_b': 5.803}
    for name, (base, spread) in spreads.items():
        noise = np.random.default_rng([zlib.crc32(name.encode()), seed]).standard_normal(out[name].shape)
        drawn = base * np.exp(spread * noise) if base else spread * noise
        out[name] = jnp.asarray(drawn.astype(out[name].dtype))
    for name, factor in factors.items():
        out[name] = (out[name] * factor).astype(out[name].dtype)
    return out


_narrow_inputs = second_inputs


def second_inputs(seed=0):

    out = dict(_narrow_inputs(seed))
    wider = {'od_sgu_ln_g': 4.78, 'od_sgu_ln_b': 4.75, 'od_spatial_b': 4.58, 'final_norm_g': 3.33}
    for name, times in wider.items():
        mean = out[name].mean()
        out[name] = (mean + times * (out[name] - mean)).astype(out[name].dtype)
    return out


def setup_inputs(seed=0):
    out = dict(first_inputs(seed))
    for name, value in second_inputs(seed + 1).items():
        if name != "x":
            out[name + "_2"] = value
    return out


def reference(
    x, gla_w_in, gla_w_gate_up, gla_b_gate, gla_norm_g, gla_w_out, nsa_w_in, nsa_w_cmp_k1,
    nsa_w_cmp_k2, nsa_w_cmp_v1, nsa_w_cmp_v2, nsa_cmp_pe, nsa_w_out, moe_w_router, moe_b_router,
    moe_w_gate, moe_w_up, moe_w_down, ln_g, ln_b, ev_norm_g_2, ev_w_in_2, ev_sinks_2,
    ev_conv_w_2, ev_conv_b_2, ev_conv_ln_g_2, ev_conv_ln_b_2, ev_w_out_2, od_norm_g_2,
    od_w_in_2, od_sgu_ln_g_2, od_sgu_ln_b_2, od_spatial_w_2, od_spatial_b_2, od_w_out_2,
    ffn_norm_g_2, ffn_w_gate_2, ffn_w_up_2, ffn_w_down_2, final_norm_g_2,
):
    x = first_block(
        x, gla_w_in, gla_w_gate_up, gla_b_gate, gla_norm_g, gla_w_out, nsa_w_in, nsa_w_cmp_k1,
        nsa_w_cmp_k2, nsa_w_cmp_v1, nsa_w_cmp_v2, nsa_cmp_pe, nsa_w_out, moe_w_router,
        moe_b_router, moe_w_gate, moe_w_up, moe_w_down, ln_g, ln_b,
    )
    return second_block(
        x, ev_norm_g_2, ev_w_in_2, ev_sinks_2, ev_conv_w_2, ev_conv_b_2, ev_conv_ln_g_2,
        ev_conv_ln_b_2, ev_w_out_2, od_norm_g_2, od_w_in_2, od_sgu_ln_g_2, od_sgu_ln_b_2,
        od_spatial_w_2, od_spatial_b_2, od_w_out_2, ffn_norm_g_2, ffn_w_gate_2, ffn_w_up_2,
        ffn_w_down_2, final_norm_g_2,
    )


_drawn_inputs = setup_inputs


def setup_inputs(seed=0):
    import zlib

    import numpy as np

    out = dict(_drawn_inputs(seed))
    spreads = {}
    factors = {'ev_conv_ln_g_2': 2.704, 'ev_sinks_2': 4.95, 'ev_conv_ln_b_2': 4.643}
    for name, (base, spread) in spreads.items():
        noise = np.random.default_rng([zlib.crc32(name.encode()), seed]).standard_normal(out[name].shape)
        drawn = base * np.exp(spread * noise) if base else spread * noise
        out[name] = jnp.asarray(drawn.astype(out[name].dtype))
    for name, factor in factors.items():
        out[name] = (out[name] * factor).astype(out[name].dtype)
    return out
```

```python
from contextlib import ExitStack

import numpy as np
import concourse.bass as bass
from concourse import mybir

F32 = mybir.dt.float32
F32R = mybir.dt.float32r
U32 = mybir.dt.uint32
ALU = mybir.AluOpType
ACT = mybir.ActivationFunctionType
AX = mybir.AxisListType.X

P = 128
S = 512
NT = S // P
D = 1024
KC = D // P
NEG = -1e30
BIG = 3e38
LN_EPS = 1e-5
RMS_EPS = 1e-6
ALPHA = 4.0 ** 0.25

GH, GDK, GDV, GC, GR = 4, 128, 256, 64, 16
G_Q, G_K, G_V, G_G, G_R, G_IN = 0, 512, 1024, 2048, 2064, 3088
NCH = S // GC
HD = 64
NH, NG = 16, 4
N_KC, N_VC, N_KS, N_VS, N_KW, N_VW, N_GT, N_IN = 1024, 1280, 1536, 1792, 2048, 2304, 2560, 2608
NC = 32
CB = 32
CST = 16
NE, FF = 16, 256
DFF = 2816
E_K, E_V, E_GA, E_GB, E_IN = 512, 640, 768, 1280, 1792
TAPS = 31
O_K, O_V, O_U, O_G, O_IN = 512, 1024, 1536, 2048, 2560
UNIT = 2048
W2 = 512

CONSTS = {}
for _name, _width in (("ident", P), ("gla_mask", P), ("gla_sum", P), ("upper", P), ("causal", S), ("band", 2 * P),
                      ("dilated", S), ("cmp_mask", NT * NC), ("cmp_any", NT), ("cos", NT * 8), ("sin", NT * 8),
                      ("cmp_cos", 8), ("cmp_sin", 8), ("index4", 4), ("ones", NT * NE), ("minus_half", NT)):
    CONSTS[_name] = (sum(w for _, w in CONSTS.values()), _width)
CONST_W = sum(w for _, w in CONSTS.values())


def constants():
    f = np.float32
    t = np.zeros((P, CONST_W), f)

    def put(name, a):
        at, w = CONSTS[name]
        t[:, at:at + w] = np.asarray(a, f).reshape(P, w)

    p = np.arange(P)[:, None]
    q = np.arange(P)[None, :]
    put("ident", p == q)
    same = (p // GC == q // GC) & (p <= q)
    put("gla_mask", same)
    put("gla_sum", same / 16.0)
    put("upper", p <= q)
    d = p + 3 * P - np.arange(S)[None, :]
    put("causal", np.where(d >= 0, 0.0, NEG))
    db = p + P - np.arange(2 * P)[None, :]
    put("band", np.where((db >= 0) & (db <= P - 1), 0.0, NEG))
    n = (d <= 128).astype(int) + (d % 4 == 0) + (d % 16 == 0)
    put("dilated", np.where((d >= 0) & (n > 0), np.log(np.maximum(n, 1).astype(np.float64)), NEG))
    qpos = np.arange(NT)[None, :] * P + p
    c = np.arange(NC)
    ok = (c * CST + CB - 1 <= qpos[:, :, None]) & (c < NC - 1)
    put("cmp_mask", np.where(ok, 0.0, NEG))
    put("cmp_any", ok.any(-1))
    inv = np.power(f(500000.0), -np.arange(8, dtype=f) * f(2.0 / 16)).astype(f)
    ang = qpos.astype(f)[:, :, None] * inv
    put("cos", np.cos(ang))
    put("sin", np.sin(ang))
    cend = ((np.arange(P) % NC) * CST + CB - 1).astype(f)[:, None] * inv
    put("cmp_cos", np.cos(cend))
    put("cmp_sin", np.sin(cend))
    put("index4", np.broadcast_to(np.arange(4), (P, 4)))
    put("ones", np.ones((P, NT * NE)))
    put("minus_half", np.full((P, NT), -0.5))
    return t


class Chain:

    def __init__(self, eng, sem):
        self.eng, self.sem, self.n, self.turn = eng, sem, 0, None

    def after(self, ins):
        ins.then_inc(self.sem, 1)
        self.n += 1
        self.eng.wait_ge(self.sem, self.n if self.turn is None else self.turn + self.n)

    def enter(self, i, per):
        self.turn, self.base = i * per, self.n

    def leave(self, per, times):
        assert self.n - self.base == per, (self.n - self.base, per)
        self.turn, self.n = None, self.base + per * times


def build(nc, a, out):
    with ExitStack() as ctx:
        def sb(name, shape):
            return ctx.enter_context(nc.sbuf_tensor(name, shape, F32))

        sems = {}

        def S_(name):
            if name not in sems:
                sems[name] = ctx.enter_context(nc.semaphore(name))
            return sems[name]

        ps = [ctx.enter_context(nc.psum_tensor(f"ps{i}", [P, S], F32)) for i in range(8)]

        con = sb("con", [P, CONST_W])
        x = sb("x", [P, NT, D])
        cols_at = nc.sbuf_base
        cols = sb("cols", [P, KC, S])
        acc = sb("acc", [P, NT, D])
        proj = sb("proj", [P, NT, G_IN])
        raw = [sb(f"raw{i}", [P, UNIT]) for i in range(2)]
        whi = [ctx.enter_context(nc.sbuf_tensor(f"whi{i}", [P, UNIT], F32R)) for i in range(2)]
        wlo = [ctx.enter_context(nc.sbuf_tensor(f"wlo{i}", [P, UNIT], F32R)) for i in range(2)]
        work_at = nc.sbuf_base
        work = sb("work", [P, 4096])
        more_at = nc.sbuf_base
        more = sb("more", [P, 6144])
        chi = nc.alloc_sbuf_tensor_at("cols_high", [P, KC, S], F32R, offset=work_at)
        clo = nc.alloc_sbuf_tensor_at("cols_low", [P, KC, S], F32R, offset=cols_at)
        hhi = nc.alloc_sbuf_tensor_at("hidden_high", [P, 2, 2, S], F32R, offset=more_at + 8192)
        hlo = nc.alloc_sbuf_tensor_at("hidden_low", [P, 2, 2, S], F32R, offset=more_at + 16384)
        rowp = sb("rowp", [P, 2, D])
        colp = sb("colp", [P, 2, 9, KC])
        small = sb("small", [P, 1024])

        def cst(name, *shape):
            at, w = CONSTS[name]
            v = con[:, at:at + w]
            return v.rearrange("p (a b) -> p a b", a=shape[0]) if shape else v

        ident = cst("ident")

        hbuf = [more[:, i * 1024:(i + 1) * 1024].rearrange("p (c s) -> p c s", c=2) for i in range(2)]
        gate = small[:, 0:NT * NE].rearrange("p (t e) -> p t e", t=NT)
        bst = small[:, 64:64 + 48].rearrange("p (t a s) -> p t a s", t=NT, a=2)
        mv = small[:, 112:120].rearrange("p (t s) -> p t s", t=NT)
        rstd = small[:, 120:124]
        nmr = small[:, 124:128]
        vare = small[:, 128:132]
        rt = small[:, 160:160 + 6 * 64]
        gsc = small[:, 560:560 + 96]
        misc = small[:, 672:1024]

        raw_landed = [S_("raw_landed0"), S_("raw_landed1")]
        hi_done, lo_done = S_("weights_high"), S_("weights_low")

        TURNS = ["in", "gla_out", "n0", "n1", "nsa_out", "n2", "n4", "even_out", "n5", "n6", "odd_out", "n7"]
        turned, cols_act, cols_dve = S_("turned"), S_("cols_act"), S_("cols_dve")
        cols_hi, cols_lo = S_("cols_high"), S_("cols_low")

        WIDTHS = {"gla_in": G_IN, "gla_out": D, "nsa_in": N_IN, "nsa_out": D, "even_in": E_IN, "even_out": D,
                  "odd_in": O_IN, "odd_out": D}
        UNITS, READS, PIECES = {}, {}, {}
        units = reads = pieces = 0
        for name_, width_ in WIDTHS.items():
            UNITS[name_], READS[name_] = units, reads
            units += -(-width_ // S)
            reads += -(-width_ // S) if width_ != D else 0
        for name_, n_ in (("moe0", NE), ("moe1", NE), ("ffn0", DFF // FF), ("ffn1", DFF // FF)):
            PIECES[name_] = pieces
            pieces += n_
        READS_OF = ["gla_in", "nsa_in", "even_in", "odd_in"]
        OUTS = ["gla_out", "nsa_out", "even_out", "odd_out"]
        half_done, product = S_("half_done"), S_("product")
        read_act, read_dve, added = S_("read_act"), S_("read_dve"), S_("added")
        gate_ready, up_ready, silu = S_("gate_ready"), S_("up_ready"), S_("silu")
        h_whole, h_high, h_low = S_("hidden_whole"), S_("hidden_high"), S_("hidden_low")
        y_ready, y_added = S_("down"), S_("down_added")

        def val(at, per=0, i=None):
            return at if i is None or not per else i * per + at

        def linear_used(name, u, half):
            return (product, 4 * (UNITS[name] + u + 1), 4) if half else (half_done, UNITS[name] + u + 1, 1)

        def piece_used(name, e, what):
            e += PIECES[name] + 1
            return {"gate": (gate_ready, 2 * e, 2), "up": (up_ready, 2 * e, 2), "down": (y_ready, 8 * e, 8)}[what]

        class Count:

            def __init__(self):
                self.n = 0
                self.last = [None, None]

        def chunks(eng, n_cols, body):
            full, rest = divmod(n_cols, S)
            widths = [S] * full + ([rest] if rest else []) + [None]
            pairs = (full - 2) // 2
            body(0, None, widths[1])
            if pairs:
                with eng.Fori(0, pairs) as i:
                    for j in range(2):
                        body(1 + j, i, S)
            for u in range(1 + 2 * pairs, len(widths) - 1):
                body(u, None, widths[u + 1])

        def pieces_of(eng, n_exp, body):
            body(0, None)
            body(1, None)
            pairs = (n_exp - 3) // 2
            with eng.Fori(0, pairs) as i:
                for j in range(2):
                    body(2 + j, i)
            for e in range(2 + 2 * pairs, n_exp):
                body(e, None)

        def land(sp, n, per, i, dst, src):
            if n >= 2:
                sp.wait_ge(lo_done, val(n - 1, per, i))
            sp.dma_start(dst, src).then_inc(raw_landed[n % 2], 16)

        def piece(v, width):
            return v[:, :] if width == S else v[:, :].rearrange("p (k n) -> p k n", n=S)[:, :, 0:width]

        def high(act, n, per, i, used, width=S):
            act.wait_ge(raw_landed[n % 2], val(16 * (n // 2 + 1), 8 * per, i))
            if used:
                act.wait_ge(used[0], val(used[1], used[2], i))
            nc.scalar.copy(piece(whi[n % 2], width), piece(raw[n % 2], width)).then_inc(hi_done, 1)

        def low(dve, n, per, i, used, width=S):
            dve.wait_ge(hi_done, val(n + 1, per, i))
            nc.vector.tensor_tensor(piece(wlo[n % 2], width), piece(raw[n % 2], width),
                                    piece(whi[n % 2], width).bitcast(F32), ALU.subtract).then_inc(lo_done, 1)

        def twice(used):
            return used and (used[0], used[1], 2 * used[2])

        def three(out, lhs, rhs, first, last):
            (lh, ll), (rh, rl) = lhs, rhs
            nc.tensor.matmul(out, lh, rh, start=first, stop=False)
            nc.tensor.matmul(out, lh, rl, start=False, stop=False)
            return nc.tensor.matmul(out, ll, rh, start=False, stop=last)

        def load_linear(sp, c, name, w, n_cols):
            wv = w.rearrange("(k p) n -> p k n", p=P)

            def body(u, i, _):
                width = min(S, n_cols - u * S) if i is None else S
                for h in range(2):
                    n = c.n + 2 * u + h
                    cs = bass.ds(val(u * S, 2 * S, i), width)
                    dst = raw[n % 2][:, :].rearrange("p (k n) -> p k n", k=4)[:, :, 0:width]
                    land(sp, n, 4, i, dst, wv[:, 4 * h:4 * h + 4, cs])

            chunks(sp, n_cols, body)
            c.n += 2 * (-(-n_cols // S))

        def load_ff(sp, c, name, views, n_exp):
            def gate_up(e, i, w, n):
                dst = raw[n % 2][:, :].rearrange("p (k n) -> p k n", k=KC)
                land(sp, n, 6, i, dst, views(val(e, 2, i))[w])

            def body(e, i):
                n = c.n + 3 * e - 1 if e else c.n
                gate_up(e, i, 0, n)
                gate_up(e, i, 1, n + 1)
                if e:
                    down(e - 1, i, n + 2)

            def down(e, i, n):
                dst = raw[n % 2][:, :].rearrange("p (h n) -> p h n", h=2)
                land(sp, n, 6, i, dst, views(val(e, 2, i))[2])

            pieces_of(sp, n_exp, body)
            down(n_exp - 1, None, c.n + 3 * n_exp - 1)
            c.n += 3 * n_exp

        def load_cmp(sp, c):
            for w in ("nsa_w_cmp_k1", "nsa_w_cmp_v1"):
                wv = a[w][0].rearrange("(m p) n -> p m n", p=P)
                for h in range(2):
                    dst = raw[c.n % 2][:, :].rearrange("p (m n) -> p m n", m=8)
                    land(sp, c.n, 0, None, dst, wv[:, 8 * h:8 * h + 8])
                    c.n += 1

        def moe_views(layer):
            g, u, d = a["moe_w_gate"][layer], a["moe_w_up"][layer], a["moe_w_down"][layer]

            def at(e):
                pick = bass.ds(e, 1)
                return (g[pick].rearrange("e (k p) f -> p (e k) f", p=P), u[pick].rearrange("e (k p) f -> p (e k) f", p=P),
                        d[pick].rearrange("e (c p) n -> p (e c) n", p=P))
            return at

        def ffn_views(layer):
            g = a["ffn_w_gate_2"][layer].rearrange("(k p) f -> p k f", p=P)
            u = a["ffn_w_up_2"][layer].rearrange("(k p) f -> p k f", p=P)
            d = a["ffn_w_down_2"][layer].rearrange("(c p) n -> p c n", p=P)

            def at(e):
                cs = bass.ds(e * FF, FF)
                return g[:, :, cs], u[:, :, cs], d[:, bass.ds(e * 2, 2), :]
            return at

        def norm_rows(n):
            if n < 4:
                return a["ln_g"][n // 2, n % 2], a["ln_b"][n // 2, n % 2]
            return {4: a["ev_norm_g_2"][0], 5: a["ffn_norm_g_2"][0], 6: a["od_norm_g_2"][0],
                    7: a["ffn_norm_g_2"][1], 8: a["final_norm_g_2"]}[n], None

        def bcast(row, n):
            return row.rearrange("(o n) -> o n", o=1).broadcast_to((P, n))

        def split_chunk(split, eng, c, name, u, i, next_width, width):
            n = c.n + 2 * u
            before = twice(linear_used(name, u - 1, 1)) if u else c.last[1]
            split(eng, n + 1, 4, i, before, width)
            split(eng, n + 2, 4, i, twice(linear_used(name, u, 0)), next_width or S)

        def end_linear(c, name, n_cols):
            n = -(-n_cols // S)
            c.n += 2 * n
            c.last = [linear_used(name, n - 1, 0), linear_used(name, n - 1, 1)]

        def chunk_width(n_cols, u, i):
            return S if i is not None else min(S, n_cols - u * S)

        def linear_pe(pe, c, name, n_cols, turn):
            u0, v0 = UNITS[name], READS[name]

            def body(u, i, _):
                width = chunk_width(n_cols, u, i)
                for h in range(2):
                    n = c.n + 2 * u + h
                    if u == 0:
                        pe.wait_ge(cols_lo, KC * TURNS.index(turn) + 4 * h + 4)
                    pe.wait_ge(lo_done, val(n + 1, 4, i))
                    wv = [w[n % 2][:, :].rearrange("p (k n) -> p k n", k=4)[:, :, 0:width] for w in (whi, wlo)]
                    for t in range(NT):
                        bank = ps[4 - 4 * (u % 2) + t][:, 0:width]
                        if h == 0 and u >= 2 and name in READS_OF:
                            pe.wait_ge(read_act if t % 2 == 0 else read_dve, val(2 * (v0 + u) - 3 + t // 2, 4, i))
                        for k in range(4):
                            ts = slice(t * P, (t + 1) * P)
                            ins = three(bank, (chi[:, 4 * h + k, ts], clo[:, 4 * h + k, ts]), (wv[0][:, k], wv[1][:, k]),
                                        h == 0 and k == 0, h == 1 and k == 3)
                        if h == 1:
                            ins.then_inc(product, 1)
                    if h == 0:
                        ins.then_inc(half_done, 1)

            chunks(pe, n_cols, body)
            end_linear(c, name, n_cols)

        def linear_evac(eng, c, name, n_cols, which):
            u0 = UNITS[name]

            def body(u, i, next_width):
                width = chunk_width(n_cols, u, i)
                split_chunk(low if which else high, eng, c, name, u, i, next_width, width)
                for t in range(which, NT, 2):
                    eng.wait_ge(product, val(NT * (u0 + u) + t + 1, 2 * NT, i))
                    dst, src = proj[:, t, bass.ds(val(u * S, 2 * S, i), width)], ps[4 - 4 * (u % 2) + t][:, 0:width]
                    if which == 0:
                        nc.scalar.copy(dst, src).then_inc(read_act, 1)
                    else:
                        nc.vector.tensor_copy(dst, src).then_inc(read_dve, 1)

            chunks(eng, n_cols, body)
            end_linear(c, name, n_cols)

        def linear_done(name, n_cols):
            n = 2 * (READS[name] + -(-n_cols // S))
            return [(read_act, n), (read_dve, n)]

        def wait_alone(eng, sem, value):
            eng.wait_ge(sem, value)
            eng.sem_inc(S_("passed"), 1)

        def wait_all(eng, pairs):
            for s, v in pairs:
                eng.wait_ge(s, v)

        def out_pe(pe, c, name):
            linear_pe(pe, c, name, D, name)

        def out_act(act, c, name):
            chunks(act, D, lambda u, i, nxt: split_chunk(high, act, c, name, u, i, nxt, S))
            end_linear(c, name, D)

        def out_dve(dve, c, name, per_tile, first=()):
            u0, n0 = UNITS[name], 2 * NT * OUTS.index(name)

            def body(u, i, nxt):
                split_chunk(low, dve, c, name, u, i, nxt, S)
                if u == 0:
                    wait_all(dve, first)
                for t in range(NT):
                    dve.wait_ge(product, NT * (u0 + u) + t + 1)
                    xs = x[:, t, u * S:(u + 1) * S]
                    nc.vector.tensor_tensor(xs, xs, ps[4 - 4 * u + t][:, :], ALU.add).then_inc(added, 1)
                    if u == 1:
                        dve.wait_ge(added, n0 + NT * u + t + 1)
                        per_tile(t)

            chunks(dve, D, body)
            end_linear(c, name, D)


        def turn_pe(pe, name, src, waits):
            wait_all(pe, waits)
            n = TURNS.index(name)
            for k in range(KC):
                if k >= 4:
                    pe.wait_ge(cols_act if k % 2 == 0 else cols_dve, 4 * n + (k - 4) // 2 + 1)
                for t in range(NT):
                    ins = nc.tensor.transpose(ps[k % 4][:, t * P:(t + 1) * P], src[:, t, k * P:(k + 1) * P], ident)
                ins.then_inc(turned, 1)

        def turn_evac(eng, name, which, norm=None):
            base = TURNS.index(name)

            def out_of_psum(k):
                eng.wait_ge(turned, KC * base + k + 1)
                g = colp[:, 0, norm, k:k + 1] if norm is not None else 1.0
                b = colp[:, 1, norm, k:k + 1] if norm is not None and norm < 4 else 0.0
                dst, src = cols[:, k, :], ps[k % 4][:, :]
                if which == 0:
                    if norm is None:
                        ins = nc.scalar.copy(dst, src)
                    elif norm < 4:
                        ins = nc.scalar.activation(dst, src, ACT.Identity, bias=b, scale=g)
                    else:
                        ins = nc.scalar.activation(dst, src, ACT.Copy, scale=g)
                    ins.then_inc(cols_act, 1)
                else:
                    if norm is None:
                        ins = nc.vector.tensor_copy(dst, src)
                    elif norm < 4:
                        ins = nc.vector.tensor_scalar(dst, src, g, b, ALU.mult, ALU.add)
                    else:
                        ins = nc.vector.tensor_scalar(dst, src, g, None, ALU.mult)
                    ins.then_inc(cols_dve, 1)

            def parts(k):
                if which == 0:
                    eng.wait_ge(cols_act if k % 2 == 0 else cols_dve, 4 * base + k // 2 + 1)
                    nc.scalar.copy(chi[:, k, :], cols[:, k, :]).then_inc(cols_hi, 1)
                else:
                    eng.wait_ge(cols_hi, KC * base + k + 1)
                    nc.vector.tensor_tensor(clo[:, k, :], cols[:, k, :], chi[:, k, :].bitcast(F32), ALU.subtract)\
                        .then_inc(cols_lo, 1)

            for k in range(0, KC, 2):
                out_of_psum(k + which)
                if k >= 2:
                    parts(k - 2)
                    parts(k - 1)
            parts(KC - 2)
            parts(KC - 1)

        NORMS = [0, 1, 2, 3, 4, "conv", 5, 6, "sgu", 7, 8]

        def norm_count(n, tiles=NT):
            return NT * NORMS.index(n) + tiles

        def is_rms(n):
            return n in (4, 5, 6, 7, 8)

        def stats_dve(dve, ch, n, t, src=None, width=D):
            src = x[:, t, :] if src is None else src
            halves = width // 512
            for h in range(halves):
                ch.after(nc.vector.bn_stats(bst[:, t, h, :], src[:, h * 512:(h + 1) * 512]))
            ins = nc.vector.bn_aggr(mv[:, t, :], bst[:, t, 0:halves, :].rearrange("p a s -> p (a s)"))
            if is_rms(n):
                ch.after(ins)
                ins = nc.vector.scalar_tensor_tensor(out=mv[:, t, 1:2], in0=mv[:, t, 0:1], scalar=mv[:, t, 0:1],
                                                     in1=mv[:, t, 1:2], op0=ALU.mult, op1=ALU.add)
            ins.then_inc(S_("stats"), 1)

        def rstd_pool(pool, ch, n, t):
            pool.wait_ge(S_("stats"), norm_count(n, t + 1))
            eps = RMS_EPS if is_rms(n) else LN_EPS
            ch.after(nc.gpsimd.tensor_scalar(vare[:, t:t + 1], mv[:, t, 1:2], eps, None, ALU.add))
            nc.gpsimd.tensor_tensor(rstd[:, t:t + 1], vare[:, t:t + 1], cst("minus_half")[:, 0:1], ALU.pow)\
                .then_inc(S_("rstd"), 1)

        def scale_act(act, ch, n, t, dst, src):
            act.wait_ge(S_("rstd"), norm_count(n, t + 1))
            if not is_rms(n):
                ch.after(nc.scalar.activation(nmr[:, t:t + 1], mv[:, t, 0:1], ACT.Copy, scale=rstd[:, t:t + 1]))
                ch.after(nc.scalar.mul(nmr[:, t:t + 1], nmr[:, t:t + 1], -1.0))
                ins = nc.scalar.activation(dst, src, ACT.Identity, bias=nmr[:, t:t + 1], scale=rstd[:, t:t + 1])
            else:
                ins = nc.scalar.activation(dst, src, ACT.Copy, scale=rstd[:, t:t + 1])
            ins.then_inc(S_("scaled"), 1)

        def norm_pool(pool, ch, n):
            if n < 4:
                pool.wait_ge(S_("gain_rows"), 32 * n + 32)
                if n < 3:
                    ch.after(nc.gpsimd.tensor_scalar(rowp[:, :, :], rowp[:, :, :], ALPHA, None, ALU.mult))
            for t in range(NT):
                rstd_pool(pool, ch, n, t)
            if n < 4:
                for t in range(NT):
                    pool.wait_ge(S_("scaled"), norm_count(n, t + 1))
                    ch.after(nc.gpsimd.tensor_tensor(x[:, t, :], acc[:, t, :], rowp[:, 0, :], ALU.mult))
                    nc.gpsimd.tensor_tensor(x[:, t, :], x[:, t, :], rowp[:, 1, :], ALU.add)\
                        .then_inc(S_("x_rows"), 1)

        def norm_act(act, ch, n):
            for t in range(NT):
                scale_act(act, ch, n, t, acc[:, t, :], x[:, t, :])

        def ff_index(c, e, what):
            return c.n + {"gate": 3 * e - 1 if e else 0, "up": 3 * e if e else 1}.get(what, 3 * e + 4)

        def ff_split(split, eng, c, name, n_exp, e, i, what):
            n = c.n + 3 * n_exp - 1 if (what, e) == ("down", n_exp - 1) else ff_index(c, e, what)
            if n - c.n < 2:
                used = c.last[n - c.n]
            elif what == "up":
                used = piece_used(name, e - 2, "down") if e >= 2 else piece_used(name, 0, "up")
            elif what == "gate":
                used = piece_used(name, e - 1, "up" if e > 1 else "gate")
            else:
                used = piece_used(name, e, "up") if e == n_exp - 1 else piece_used(name, e + 1, "gate")
            split(eng, n, 6, i, twice(used))

        def end_ff(c, name, n_exp):
            c.n += 3 * n_exp
            c.last = [piece_used(name, n_exp - 2, "down"), piece_used(name, n_exp - 1, "down")]

        def ff_pe(pe, c, name, n_exp, turn):
            e0 = PIECES[name]

            def up_or_gate(e, i, w):
                n = ff_index(c, e, "up" if w else "gate")
                pe.wait_ge(lo_done, val(n + 1, 6, i))
                wv = [q[n % 2][:, :].rearrange("p (k n) -> p k n", k=KC) for q in (whi, wlo)]
                for h in range(2):
                    if e:
                        pe.wait_ge(h_whole if w else silu, val(2 * (e0 + e) - 1 + h, 4, i))
                    hs = slice(h * P, (h + 1) * P)
                    for k in range(KC):
                        if e == 0 and w == 0 and h == 0:
                            pe.wait_ge(cols_lo, KC * TURNS.index(turn) + k + 1)
                        ins = three(ps[4 + 2 * h + w][:, :], (wv[0][:, k, hs], wv[1][:, k, hs]), (chi[:, k, :], clo[:, k, :]),
                                    k == 0, k == KC - 1)
                    ins.then_inc(up_ready if w else gate_ready, 1)

            def down(e, i):
                n = c.n + 3 * n_exp - 1 if i is None and e == n_exp - 1 else ff_index(c, e, "down")
                pe.wait_ge(lo_done, val(n + 1, 6, i))
                pe.wait_ge(h_low, val(2 * (e0 + e) + 2, 4, i))
                wv = [q[n % 2][:, :].rearrange("p (h n) -> p h n", h=2) for q in (whi, wlo)]
                for m in range(8):
                    t, half = m // 2, m % 2
                    if m >= 4 or e:
                        pe.wait_ge(y_added, val(8 * (e0 + e) + m - 3, 16, i))
                    ts, ns = slice(t * P, (t + 1) * P), slice(half * S, (half + 1) * S)
                    for h in range(2):
                        ins = three(ps[m % 4][:, :], (hhi[:, e % 2, h, ts], hlo[:, e % 2, h, ts]),
                                    (wv[0][:, h, ns], wv[1][:, h, ns]), h == 0, h == 1)
                    ins.then_inc(y_ready, 1)

            def body(e, i):
                up_or_gate(e, i, 0)
                up_or_gate(e, i, 1)
                if e:
                    down(e - 1, i)

            pieces_of(pe, n_exp, body)
            down(n_exp - 1, None)
            end_ff(c, name, n_exp)

        def ff_act(act, c, name, n_exp):
            e0 = PIECES[name]

            def body(e, i):
                last = i is None and e == n_exp - 1
                ff_split(high, act, c, name, n_exp, e, i, "up")
                for h in range(2):
                    act.wait_ge(gate_ready, val(2 * (e0 + e) + h + 1, 4, i))
                    if e >= 2 and h == 0:
                        act.wait_ge(h_low, val(2 * (e0 + e) - 2, 4, i))
                    nc.scalar.activation(hbuf[e % 2][:, h, :], ps[4 + 2 * h][:, :], ACT.Silu).then_inc(silu, 1)
                if e:
                    ff_split(high, act, c, name, n_exp, e - 1, i, "down")
                ff_split(high, act, c, name, n_exp, *((e, i, "down") if last else (e + 1, i, "gate")))
                for h in range(2):
                    act.wait_ge(h_whole, val(2 * (e0 + e) + h + 1, 4, i))
                    if e >= 2 and h == 0:
                        act.wait_ge(y_ready, val(8 * (e0 + e) - 8, 16, i))
                    nc.scalar.copy(hhi[:, e % 2, h, :], hbuf[e % 2][:, h, :]).then_inc(h_high, 1)

            pieces_of(act, n_exp, body)
            end_ff(c, name, n_exp)
            if name != "ffn1":
                high(act, c.n, 0, None, c.last[0])

        def ff_dve(dve, c, name, n_exp, weight, per_tile, waits):
            e0 = PIECES[name]

            def hidden(e, i):
                for h in range(2):
                    dve.wait_ge(silu, val(2 * (e0 + e) + h + 1, 4, i))
                    dve.wait_ge(up_ready, val(2 * (e0 + e) + h + 1, 4, i))
                    nc.vector.tensor_tensor(hbuf[e % 2][:, h, :], hbuf[e % 2][:, h, :], ps[5 + 2 * h][:, :], ALU.mult)\
                        .then_inc(h_whole, 1)
                for h in range(2):
                    dve.wait_ge(h_high, val(2 * (e0 + e) + h + 1, 4, i))
                    nc.vector.tensor_tensor(hlo[:, e % 2, h, :], hbuf[e % 2][:, h, :],
                                            hhi[:, e % 2, h, :].bitcast(F32), ALU.subtract).then_inc(h_low, 1)

            def add(e, i, last):
                for m in range(8):
                    t, half = m // 2, m % 2
                    dve.wait_ge(y_ready, val(8 * (e0 + e) + m + 1, 16, i))
                    xs = x[:, t, half * S:(half + 1) * S]
                    if m == 0 and e:
                        dve.wait_ge(y_added, val(8 * (e0 + e), 16, i))
                    w = weight(t, val(e, 2, i))
                    if w is None:
                        nc.vector.tensor_tensor(xs, xs, ps[m % 4][:, :], ALU.add).then_inc(y_added, 1)
                    else:
                        nc.vector.scalar_tensor_tensor(out=xs, in0=ps[m % 4][:, :], scalar=w, in1=xs,
                                                       op0=ALU.mult, op1=ALU.add).then_inc(y_added, 1)
                    if last and half == 1:
                        dve.wait_ge(y_added, 8 * (e0 + e) + m + 1)
                        per_tile(t)

            def body(e, i):
                last = i is None and e == n_exp - 1
                ff_split(low, dve, c, name, n_exp, e, i, "up")
                if e:
                    ff_split(low, dve, c, name, n_exp, e - 1, i, "down")
                ff_split(low, dve, c, name, n_exp, *((e, i, "down") if last else (e + 1, i, "gate")))
                if e == 1:
                    wait_all(dve, waits)
                if e:
                    add(e - 1, i, False)
                hidden(e, i)

            pieces_of(dve, n_exp, body)
            end_ff(c, name, n_exp)
            if name != "ffn1":
                low(dve, c.n, 0, None, c.last[0])
            add(n_exp - 1, None, True)

        wr = sb("wr", [P, KC, NE])
        br = sb("br", [P, NE])

        wrh = ctx.enter_context(nc.sbuf_tensor("wrh", [P, KC, NE], F32R))
        wrl = ctx.enter_context(nc.sbuf_tensor("wrl", [P, KC, NE], F32R))

        def router_pe(pe, layer, turn):
            pe.wait_ge(S_("router_low"), 1)
            pe.wait_ge(cols_lo, KC * TURNS.index(turn) + KC)
            for t in range(NT):
                for k in range(KC):
                    ts = slice(t * P, (t + 1) * P)
                    ins = three(ps[0][:, t * NE:(t + 1) * NE], (chi[:, k, ts], clo[:, k, ts]), (wrh[:, k, :], wrl[:, k, :]),
                                k == 0, k == KC - 1)
            ins.then_inc(S_("router_logits"), 1)

        rview = [rt[:, i * 64:(i + 1) * 64].rearrange("p (t e) -> p t e", t=NT) for i in range(6)]

        def router_act(act, layer):
            act.wait_ge(S_("router_logits"), layer + 1)
            nc.scalar.activation(rt[:, 0:64], ps[0][:, 0:64], ACT.Sigmoid).then_inc(S_("router_scores"), 1)

        def router_dve(dve, ch, layer):
            dve.wait_ge(S_("router_scores"), layer + 1)
            sc, biased, rank, cmp_, top, sel = rview
            V = nc.vector

            def grp(v):
                return v.rearrange("p t (g k) -> p (t g) k", k=4)

            def ranks(v, r, tmp, n):
                i4 = cst("index4").rearrange("p (o k) -> p o k", o=1).broadcast_to((P, n, 4))
                ch.after(V.tensor_copy(r, i4))
                for d in (1, 2, 3):
                    ch.after(V.tensor_tensor(tmp[:, :, 0:4 - d], v[:, :, d:4], v[:, :, 0:4 - d], ALU.is_gt))
                    ch.after(V.tensor_tensor(r[:, :, 0:4 - d], r[:, :, 0:4 - d], tmp[:, :, 0:4 - d], ALU.add))
                    ch.after(V.tensor_tensor(r[:, :, d:4], r[:, :, d:4], tmp[:, :, 0:4 - d], ALU.subtract))

            brow_ = br[:, :].rearrange("p (o e) -> p o e", o=1).broadcast_to((P, NT, NE))
            ch.after(V.tensor_tensor(biased, sc, brow_, ALU.add))
            ranks(grp(biased), grp(rank), grp(cmp_), NT * 4)
            ch.after(V.tensor_scalar(top, rank, 2.0, None, ALU.is_lt))
            ch.after(V.tensor_tensor(cmp_, top, biased, ALU.mult))
            g4 = gsc[:, 0:16].rearrange("p (t g) -> p t g", t=NT)
            gr = gsc[:, 16:32].rearrange("p (t g) -> p t g", t=NT)
            gt = gsc[:, 32:48].rearrange("p (t g) -> p t g", t=NT)
            ch.after(V.tensor_reduce(gsc[:, 0:16], grp(cmp_), AX, ALU.add))
            ranks(g4, gr, gt, NT)
            ch.after(V.tensor_scalar(gt, gr, 0.5, None, ALU.is_lt))
            gb = gsc[:, 32:48].rearrange("p (q o) -> p q o", o=1).broadcast_to((P, 16, 4))
            ch.after(V.tensor_tensor(grp(sel), grp(top), gb, ALU.mult))
            ch.after(V.tensor_tensor(sel, sel, sc, ALU.mult))
            ch.after(V.tensor_reduce(gsc[:, 48:52], sel, AX, ALU.add))
            ch.after(V.reciprocal(gsc[:, 52:56], gsc[:, 48:52]))
            rb = gsc[:, 52:56].rearrange("p (t o) -> p t o", o=1).broadcast_to((P, NT, NE))
            ch.after(V.tensor_tensor(gate, sel, rb, ALU.mult))

        w_up = more[0:GR, 3840:4352]
        zb = work[:, 0:2048].rearrange("p (t c) -> p t c", t=NT)
        lb = work[:, 2048:4096].rearrange("p (t c) -> p t c", t=NT)
        g_sq, g_sk, g_sl, g_b, g_eb, g_enb, g_kd, g_p = (cols[:, i, :] for i in range(8))
        g_qd, g_ki = more[:, 0:512], more[:, 512:1024]
        g_sv = more[:, 1024:2048].rearrange("p (t c) -> p t c", t=NT)
        g_st = more[:, 2048:2048 + 7 * GDV].rearrange("p (c v) -> p c v", v=GDV)
        g_kdn = more[:, 3840:4352]
        g_sqr = more[:, 4352:4608]
        g_lowT = more[0:GR, 4608:5120]
        b_gate = more[:, 5120:5632]
        norm_g = more[:, 5632:5888]
        g_dec, g_ss, g_ms, g_rs = misc[:, 0:8], misc[:, 8:12], misc[:, 12:16], misc[:, 16:20]

        def by_tile(v):
            return v.rearrange("p (t c) -> p t c", t=NT)

        def half_bank(n):
            return (n % 2) * GDV, (n % 2 + 1) * GDV

        def kv_bank(c):
            lo, hi = half_bank(c // 2)
            return ps[2 * (c % 2) + c // 4][:, lo:hi]

        def gla_pe(pe):
            T = nc.tensor
            wait_all(pe, linear_done("gla_in", G_IN))
            for t in range(NT):
                ins = T.transpose(ps[4][0:GR, t * P:(t + 1) * P], proj[:, t, G_G:G_G + GR], ident)
            ins.then_inc(S_("g_low_turned"), 1)
            pe.wait_ge(S_("params"), PARAMS)
            pe.wait_ge(S_("g_low_cols"), 1)
            for t in range(NT):
                T.matmul(ps[t][:, :], g_lowT[:, t * P:(t + 1) * P], w_up, start=True, stop=True)\
                    .then_inc(S_("gate_logits"), 1)
            pe.sem_inc(S_("g_out"), 1)
            with pe.Fori(0, GH) as h:
                pe.wait_ge(S_("g_staged"), h + 1)
                for src, b in ((g_sq, 0), (g_sk, 1)):
                    for t in range(NT):
                        T.transpose(ps[b][:, t * P:(t + 1) * P], src[:, t * P:(t + 1) * P], ident)
                for t in range(NT):
                    ins = T.matmul(ps[2][:, t * P:(t + 1) * P], g_sl[:, t * P:(t + 1) * P], cst("gla_sum"),
                                   start=True, stop=True)
                ins.then_inc(S_("g_turned"), 1)
                pe.wait_ge(S_("g_qk_ready"), 2 * h + 2)
                for t in range(NT):
                    ins = T.matmul(ps[3][:, t * P:(t + 1) * P], g_ki[:, t * P:(t + 1) * P], g_qd[:, t * P:(t + 1) * P],
                                   start=True, stop=True)
                ins.then_inc(S_("g_scores"), 1)
                pe.wait_ge(S_("g_kd_ready"), h + 1)
                for t in range(NT):
                    ins = T.transpose(ps[4][:, t * P:(t + 1) * P], g_kd[:, t * P:(t + 1) * P], ident)
                ins.then_inc(S_("g_kd_turned"), 1)
                pe.wait_ge(S_("g_masked"), h + 1)
                pe.wait_ge(S_("g_kd_rows"), h + 1)
                for c in range(NCH - 1):
                    r0, t = (c % 2) * GC, c // 2
                    ins = T.matmul(kv_bank(c), g_kdn[r0:r0 + GC, t * P:(t + 1) * P], g_sv[r0:r0 + GC, t, :],
                                   start=True, stop=True)
                ins.then_inc(S_("g_kv"), 1)
                pe.wait_ge(S_("g_states"), h + 1)
                for t in range(NT):
                    lo, hi = half_bank(t)
                    o = ps[5 + t // 2]
                    T.matmul(o[:, lo:hi], g_p[:, t * P:(t + 1) * P], g_sv[:, t, :], start=True, stop=False,
                             skip_group_check=True)
                    for c in (2 * t, 2 * t + 1):
                        if c:
                            r0 = (c % 2) * GC
                            ins = T.matmul(o[r0:r0 + GC, lo:hi], g_qd[:, c * GC:(c + 1) * GC], g_st[:, c - 1, :],
                                           start=False, stop=True, skip_group_check=True)
                    ins.then_inc(S_("g_out"), 1)

        def gla_act(act, ch):
            A = nc.scalar
            act.wait_ge(S_("g_low_turned"), 1)
            A.copy(g_lowT, ps[4][0:GR, :]).then_inc(S_("g_low_cols"), 1)
            act.wait_ge(S_("gate_z"), NT)
            ch.after(A.activation(work[:, 2048:4096], work[:, 0:2048], ACT.Abs))
            ch.after(A.activation(work[:, 2048:4096], work[:, 2048:4096], ACT.Exp, scale=-1.0))
            A.activation(work[:, 2048:4096], work[:, 2048:4096], ACT.Ln, bias=1.0).then_inc(S_("gate_log"), 1)
            for t in range(NT):
                r = proj[:, t, G_R:G_R + D]
                A.activation(r, r, ACT.Silu).then_inc(S_("g_gate"), 1)
            act.wait_ge(S_("gate_decay"), 1)
            with act.Fori(0, GH) as h:
                act.wait_ge(S_("g_out"), 4 * h + 1)
                A.mul(by_tile(g_sq), proj[:, :, bass.ds(h * GDK + G_Q, GDK)], GDK ** -0.5).then_inc(S_("g_copied"), 1)
                A.copy(by_tile(g_sk), proj[:, :, bass.ds(h * GDK + G_K, GDK)]).then_inc(S_("g_copied"), 1)
                A.copy(g_sv, proj[:, :, bass.ds(h * GDV + G_V, GDV)]).then_inc(S_("g_copied"), 1)
                act.wait_ge(S_("g_copied"), 3 * h + 3)
                A.copy(by_tile(g_sl), zb[:, :, bass.ds(h * GDK, GDK)]).then_inc(S_("g_staged"), 1)
                act.wait_ge(S_("g_bsum"), h + 1)
                A.activation(g_eb, g_b, ACT.Exp).then_inc(S_("g_exp"), 1)
                A.activation(g_enb, g_b, ACT.Exp, scale=-1.0).then_inc(S_("g_exp"), 1)
                A.activation(g_dec, g_b[:, GC - 1:S:GC], ACT.Exp).then_inc(S_("g_exp"), 1)
                act.wait_ge(S_("g_rest"), h + 1)
                A.activation(g_kd, g_kd, ACT.Exp).then_inc(S_("g_exp"), 1)
                act.wait_ge(S_("g_kd_turned"), h + 1)
                A.copy(g_kdn, ps[4][:, :]).then_inc(S_("g_kd_rows"), 1)
                for t in range(NT):
                    lo, hi = half_bank(t)
                    act.wait_ge(S_("g_out"), 4 * h + 2 * (t // 2) + 3)
                    ins = A.activation(g_sqr, ps[5 + t // 2][:, lo:hi], ACT.Square, accum_out=g_ss[:, t:t + 1])
                    ins.then_inc(S_("g_squares"), 1)
                    act.wait_ge(S_("g_squares"), 4 * h + t + 1)
                A.activation(g_ms, g_ss, ACT.Copy, scale=1.0 / GDV, bias=LN_EPS).then_inc(S_("g_mean_square"), 1)

        def gla_pool(pool):
            with pool.Fori(0, GH) as h:
                pool.wait_ge(S_("g_mean_square"), h + 1)
                nc.gpsimd.tensor_tensor(g_rs, g_ms, cst("minus_half"), ALU.pow).then_inc(S_("g_rstd"), 1)

        def gla_dve(dve, ch):
            V = nc.vector
            for t in range(NT):
                dve.wait_ge(S_("gate_logits"), t + 1)
                V.tensor_tensor(zb[:, t, :], ps[t][:, :], b_gate, ALU.add).then_inc(S_("gate_z"), 1)
            dve.wait_ge(S_("gate_log"), 1)
            V.scalar_tensor_tensor(out=work[:, 0:2048], in0=work[:, 0:2048], scalar=0.0, in1=work[:, 2048:4096],
                                   op0=ALU.min, op1=ALU.subtract).then_inc(S_("gate_decay"), 1)
            dve.wait_ge(S_("g_gate"), NT)
            ch.after(V.memset(g_p, 0.0))
            mask4 = cst("gla_mask").bitcast(U32).rearrange("p (o j) -> p o j", o=1).broadcast_to((P, NT, P))
            with dve.Fori(0, GH) as h:
                ch.enter(h, 14)
                dve.wait_ge(S_("g_turned"), h + 1)
                V.tensor_copy(g_b, ps[2][:, :]).then_inc(S_("g_bsum"), 1)
                dve.wait_ge(S_("g_bsum"), h + 1)
                b3 = g_b.rearrange("p (c i) -> p c i", c=NCH)
                V.tensor_tensor(g_kd.rearrange("p (c i) -> p c i", c=NCH), b3[:, :, GC - 1:GC].broadcast_to((P, NCH, GC)),
                                b3, ALU.subtract).then_inc(S_("g_rest"), 1)
                dve.wait_ge(S_("g_exp"), 4 * h + 1)
                V.tensor_tensor(g_qd, ps[0][:, :], g_eb, ALU.mult).then_inc(S_("g_qk_ready"), 1)
                dve.wait_ge(S_("g_exp"), 4 * h + 2)
                V.tensor_tensor(g_ki, ps[1][:, :], g_enb, ALU.mult).then_inc(S_("g_qk_ready"), 1)
                dve.wait_ge(S_("g_exp"), 4 * h + 4)
                V.tensor_tensor(g_kd, g_kd, ps[1][:, :], ALU.mult).then_inc(S_("g_kd_ready"), 1)
                dve.wait_ge(S_("consts"), 16)
                dve.wait_ge(S_("g_scores"), h + 1)
                V.copy_predicated(by_tile(g_p), mask4, by_tile(ps[3][:, :])).then_inc(S_("g_masked"), 1)
                dve.wait_ge(S_("g_kv"), h + 1)
                for c in range(NCH - 1):
                    kv = kv_bank(c)
                    if c == 0:
                        ch.after(V.tensor_copy(g_st[:, 0, :], kv))
                        continue
                    ins = V.scalar_tensor_tensor(out=g_st[:, c, :], in0=g_st[:, c - 1, :], scalar=g_dec[:, c:c + 1],
                                                 in1=kv, op0=ALU.mult, op1=ALU.add)
                    if c < NCH - 2:
                        ch.after(ins)
                    else:
                        ins.then_inc(S_("g_states"), 1)
                dve.wait_ge(S_("g_rstd"), h + 1)
                for t in range(NT):
                    lo, hi = half_bank(t)
                    o = acc[:, t, bass.ds(h * GDV, GDV)]
                    ch.after(V.scalar_tensor_tensor(out=o, in0=ps[5 + t // 2][:, lo:hi], scalar=g_rs[:, t:t + 1],
                                                    in1=norm_g, op0=ALU.mult, op1=ALU.mult))
                for t in range(NT):
                    o = acc[:, t, bass.ds(h * GDV, GDV)]
                    ch.after(V.tensor_tensor(o, o, proj[:, t, bass.ds(h * GDV + G_R, GDV)], ALU.mult))
            ch.leave(14, GH)
            return [(ch.sem, ch.n)]

        def rope(dve, ch, src, heads, cos, sin, tiles, tmp):
            V = nc.vector
            v = src.rearrange("p t (h d) -> p t h d", d=HD)
            x1, x2 = v[:, :, :, 0:8], v[:, :, :, 8:16]
            n = tiles * heads * 8
            t4 = [tmp[:, i * 512:i * 512 + n].rearrange("p (t h d) -> p t h d", t=tiles, h=heads) for i in range(4)]
            cb = cos.rearrange("p (t o d) -> p t o d", t=tiles, o=1).broadcast_to((P, tiles, heads, 8))
            sb_ = sin.rearrange("p (t o d) -> p t o d", t=tiles, o=1).broadcast_to((P, tiles, heads, 8))
            V.tensor_tensor(t4[0], x1, cb, ALU.mult).then_inc(ch.sem, 1)
            V.tensor_tensor(t4[1], x2, sb_, ALU.mult).then_inc(ch.sem, 1)
            V.tensor_tensor(t4[2], x2, cb, ALU.mult).then_inc(ch.sem, 1)
            ch.n += 3
            ch.after(V.tensor_tensor(t4[3], x1, sb_, ALU.mult))
            ch.after(V.tensor_tensor(x1, t4[0], t4[1], ALU.subtract))
            ch.after(V.tensor_tensor(x2, t4[2], t4[3], ALU.add))

        t_qT = more[:, 0:2048].rearrange("p (j s) -> p j s", j=4)
        t_kT = more[:, 2048:3072].rearrange("p (j s) -> p j s", j=2)
        t_qs = more[:, 3072:4096].rearrange("p (t c) -> p t c", t=NT)
        t_ks = more[:, 4096:4608].rearrange("p (t c) -> p t c", t=NT)
        t_pT = [more[:, 4608 + 512 * i:5120 + 512 * i] for i in range(3)]
        t_p = [work[:, 512 * i:512 * i + 512] for i in range(3)]
        t_tmp = work[:, 1536:2048]
        t_l, t_nm = misc[:, 64:96], misc[:, 96:128]
        t_rl = misc[:, 128:136]
        t_sk, t_nsk, t_es = misc[:, 136:140], misc[:, 140:144], misc[:, 144:160]
        t_cl, t_cm, t_cw = misc[:, 160:176], misc[:, 176:192], misc[:, 192:208]
        c_p, c_pT = work[:, 2048:2560], work[:, 2560:3072]
        c_vblk, c_vrep, c_kT = work[:, 3072:3328], work[:, 3328:3584], work[0:HD, 3584:3712]
        c_w2 = proj[:, 0, N_IN:N_IN + 256].rearrange("p (w f d) -> p w f d", w=2, f=2)
        c_pe = misc[:, 32:48]
        c_hid, c_hT, c_row = work[:, 0:512], work[:, 512:768], work[:, 1024:1088]
        c_hTv = acc[:, 0, :].rearrange("p (f s) -> p f s", f=2)
        c_blk = [cols[:, 4 * n:4 * n + 4, :].rearrange("p a s -> p (a s)") for n in range(2)]
        sinks = misc[:, 208:216]

        class Attention:

            def __init__(self, name, turns, heads, k_slots, masks, values, q_of, k_of, band=False, sink=False,
                         cmp_=False):
                self.name, self.turns, self.heads, self.k_slots = name, turns, heads, k_slots
                self.values, self.q_of, self.k_of, self.sink, self.cmp = values, q_of, k_of, sink, cmp_
                kinds = 2 if cmp_ else 1
                self.per_head = kinds * NT
                self.units = []
                for j in range(heads):
                    for kind in range(kinds):
                        for t in range(NT):
                            k0 = max(0, t - 1) if band else 0
                            ks = kind if cmp_ else (j if k_slots == heads else 0)
                            at = (k0 - t + 1 if band else k0 - t + 3) * P
                            self.units.append((j, ks, t, k0, t + 1, masks[:, at:at + (t + 1 - k0) * P]))
                self.U = len(self.units)

            def sem(self, what):
                return S_(self.name + "_" + what)

            def last(self, j):
                return (j + 1) * self.per_head - 1

        def attn_pe(pe, c):
            T, U = nc.tensor, c.U
            with pe.Fori(0, c.turns) as i:
                wait_alone(pe, c.sem("staged"), i + 1)
                for j in range(c.heads):
                    b = ps[(7, 0, 1, 2)[j]]
                    for t in range(NT):
                        ins = T.transpose(b[0:HD, t * P:(t + 1) * P], t_qs[:, t, j * HD:(j + 1) * HD], ident)
                    ins.then_inc(c.sem("q_turned"), 1)
                for j in range(c.k_slots):
                    for t in range(NT):
                        ins = T.transpose(ps[3 + j][0:HD, t * P:(t + 1) * P], t_ks[:, t, j * HD:(j + 1) * HD], ident)
                    ins.then_inc(c.sem("k_turned"), 1)
                pe.wait_ge(c.sem("q_cols"), c.heads * i + c.heads)
                pe.wait_ge(c.sem("k_cols"), c.k_slots * i + c.k_slots)
                if c.cmp:
                    for t in range(NT):
                        for j in range(4):
                            at = (t * 4 + j) * NC
                            ins = T.matmul(ps[7][:, at:at + NC], t_qT[0:HD, j, t * P:(t + 1) * P],
                                           c_kT[:, bass.ds(i * NC, NC)], start=True, stop=True)
                    ins.then_inc(c.sem("cmp_scores"), 1)

                def scores(u):
                    j, ks, t, k0, k1, _ = c.units[u]
                    T.matmul(ps[u % 3][:, 0:(k1 - k0) * P], t_qT[0:HD, j, t * P:(t + 1) * P],
                             t_kT[0:HD, ks, k0 * P:k1 * P], start=True, stop=True).then_inc(c.sem("scores"), 1)

                def turn(u):
                    _, _, _, k0, k1, _ = c.units[u]
                    pe.wait_ge(c.sem("probs"), U * i + (u + 1))
                    for k in range(k1 - k0):
                        ins = T.transpose(ps[3 + u % 2][:, k * P:(k + 1) * P], t_p[u % 3][:, k * P:(k + 1) * P], ident)
                    ins.then_inc(c.sem("turned"), 1)

                def values(u):
                    j, ks, t, k0, k1, _ = c.units[u]
                    side = c.sem("keys_act" if u % 2 == 0 else "keys_dve")
                    pe.wait_ge(side, (U // 2) * i + (u // 2 + 1))
                    if u % c.per_head == 0:
                        pe.wait_ge(c.sem("head"), c.heads * i + max(j, 1))
                    at = (u % c.per_head) * HD
                    for k in range(k0, k1):
                        ins = T.matmul(ps[5 + j % 2][:, at:at + HD], t_pT[u % 3][:, (k - k0) * P:(k - k0 + 1) * P],
                                       proj[:, k, bass.ds(c.values(i, ks), HD)], start=(k == k0), stop=(k == k1 - 1))
                    ins.then_inc(c.sem("out"), 1)

                scores(0)
                scores(1)
                for u in range(U):
                    if u + 2 < U:
                        scores(u + 2)
                    turn(u)
                    if u:
                        values(u - 1)
                values(U - 1)
                if c.cmp:
                    pe.wait_ge(c.sem("cmp_probs"), i + 1)
                    for t in range(NT):
                        ins = T.transpose(ps[7][:, t * P:(t + 1) * P], c_p[:, t * P:(t + 1) * P], ident)
                    ins.then_inc(c.sem("cmp_turned"), 1)
                    pe.wait_ge(c.sem("cmp_keys"), i + 1)
                    for t in range(NT):
                        ins = T.matmul(ps[t // 2][:, (t % 2) * 256:(t % 2 + 1) * 256], c_pT[:, t * P:(t + 1) * P],
                                       c_vblk, start=True, stop=True)
                    ins.then_inc(c.sem("cmp_out"), 1)

        def attn_act(act, c):
            A, U = nc.scalar, c.U
            with act.Fori(0, c.turns) as i:
                act.wait_ge(c.sem("head"), c.heads * i + 1)
                if c.cmp:
                    act.wait_ge(c.sem("cmp_done"), i + 1)
                    for j in range(4):
                        A.copy(c_vblk[j * 32:(j + 1) * 32, j * HD:(j + 1) * HD],
                               c_vrep[j * 32:(j + 1) * 32, bass.ds(i * HD, HD)]).then_inc(c.sem("copied"), 1)
                if c.sink:
                    A.copy(t_sk, sinks[:, bass.ds(i * 4, 4)]).then_inc(c.sem("sink"), 1)
                    A.mul(t_nsk, sinks[:, bass.ds(i * 4, 4)], -1.0).then_inc(c.sem("sink"), 1)
                for n, (at, width, dst) in enumerate(c.k_of(i)):
                    A.copy(t_ks[:, :, dst:dst + width], proj[:, :, bass.ds(at, width)]).then_inc(c.sem("copied"), 1)
                n_copied = len(c.k_of(0)) + (4 if c.cmp else 0)
                act.wait_ge(c.sem("copied"), n_copied * i + n_copied)
                A.mul(t_qs[:, :, 0:c.heads * HD], proj[:, :, bass.ds(c.q_of(i), c.heads * HD)], HD ** -0.5)\
                    .then_inc(c.sem("staged"), 1)
                for j in range(c.heads):
                    act.wait_ge(c.sem("q_turned"), c.heads * i + (j + 1))
                    A.copy(t_qT[0:HD, j, :], ps[(7, 0, 1, 2)[j]][0:HD, :]).then_inc(c.sem("q_cols"), 1)
                if c.cmp:
                    act.wait_ge(c.sem("cmp_shifted"), i + 1)
                    A.activation(c_p, c_p, ACT.Exp).then_inc(c.sem("cmp_probs"), 1)

                def exps(u):
                    _, _, _, k0, k1, _ = c.units[u]
                    p = t_p[u % 3][:, 0:(k1 - k0) * P]
                    act.wait_ge(c.sem("masked"), U * i + (u + 1))
                    A.activation(p, p, ACT.Exp, bias=t_nm[:, u:u + 1], scale=-1.0, accum_out=t_l[:, u:u + 1])\
                        .then_inc(c.sem("probs"), 1)
                    if c.sink and u % c.per_head == c.per_head - 1:
                        j = u // c.per_head
                        act.wait_ge(c.sem("sink"), 2 * i + 2)
                        A.activation(t_es[:, 4 * j:4 * j + 4], t_nm[:, 4 * j:4 * j + 4], ACT.Exp, bias=t_sk[:, j:j + 1])\
                            .then_inc(c.sem("sink_exp"), 1)

                exps(0)
                for u in range(U):
                    if u + 1 < U:
                        exps(u + 1)
                    if u % 2 == 0:
                        _, _, _, k0, k1, _ = c.units[u]
                        act.wait_ge(c.sem("turned"), U * i + (u + 1))
                        if u >= 3:
                            act.wait_ge(c.sem("out"), U * i + (u - 2))
                        A.copy(t_pT[u % 3][:, 0:(k1 - k0) * P], ps[3 + u % 2][:, 0:(k1 - k0) * P])\
                            .then_inc(c.sem("keys_act"), 1)
                if c.cmp:
                    act.wait_ge(c.sem("cmp_turned"), i + 1)
                    A.copy(c_pT, ps[7][:, :]).then_inc(c.sem("cmp_keys"), 1)

        def attn_dve(dve, ch, c):
            V, U = nc.vector, c.U
            per = c.heads * (3 if c.cmp else 2 if c.sink else 1) + (10 if c.cmp else 0)
            dve.sem_inc(c.sem("head"), 1)
            if c.cmp:
                dve.sem_inc(c.sem("cmp_done"), 1)
            with dve.Fori(0, c.turns) as i:
                ch.enter(i, per)
                for j in range(c.k_slots):
                    dve.wait_ge(c.sem("k_turned"), c.k_slots * i + (j + 1))
                    V.tensor_copy(t_kT[0:HD, j, :], ps[3 + j][0:HD, :]).then_inc(c.sem("k_cols"), 1)

                def masked(u):
                    _, _, _, k0, k1, mask = c.units[u]
                    if u == 0 and c.sink:
                        wait_alone(dve, c.sem("sink"), 2 * i + 2)
                    if u >= 3:
                        wait_alone(dve, c.sem("turned"), U * i + (u - 2))
                    wait_alone(dve, c.sem("scores"), U * i + (u + 1))
                    first = t_nsk[:, u // c.per_head:u // c.per_head + 1] if c.sink else BIG
                    V.tensor_tensor_reduce(out=t_p[u % 3][:, 0:(k1 - k0) * P], in0=ps[u % 3][:, 0:(k1 - k0) * P],
                                           in1=mask, scale=-1.0, scalar=first, op0=ALU.add, op1=ALU.min,
                                           accum_out=t_nm[:, u:u + 1]).then_inc(c.sem("masked"), 1)

                def head(j):
                    u0, n = j * c.per_head, c.per_head
                    dve.wait_ge(c.sem("out"), U * i + (u0 + n))
                    o = ps[5 + j % 2][:, 0:n * HD].rearrange("p (u d) -> p u d", d=HD)
                    if c.sink:
                        dve.wait_ge(c.sem("sink_exp"), c.heads * i + (j + 1))
                        ch.after(V.tensor_tensor(t_l[:, u0:u0 + n], t_l[:, u0:u0 + n], t_es[:, 4 * j:4 * j + 4], ALU.add))
                    ch.after(V.reciprocal(t_rl[:, 0:n], t_l[:, u0:u0 + n]))
                    if c.cmp:
                        gates = proj[:, :, bass.ds(N_GT + 12 * i + 3 * j + 1, 2)].rearrange("p t k -> p k t")
                        ch.after(V.tensor_tensor(t_rl[:, 0:8].rearrange("p (k t) -> p k t", k=2),
                                                 t_rl[:, 0:8].rearrange("p (k t) -> p k t", k=2), gates, ALU.mult))
                    w = t_rl[:, 0:n].rearrange("p (u o) -> p u o", o=1).broadcast_to((P, n, HD))
                    hcol = acc[:, :, bass.ds((i * c.heads + j) * HD, HD)]
                    if c.cmp:
                        tmp = t_tmp.rearrange("p (u d) -> p u d", d=HD)
                        ch.after(V.tensor_tensor(tmp, o, w, ALU.mult))
                        V.tensor_tensor(hcol, tmp[:, 0:4, :], tmp[:, 4:8, :], ALU.add).then_inc(c.sem("head"), 1)
                    else:
                        V.tensor_tensor(hcol, o, w, ALU.mult).then_inc(c.sem("head"), 1)

                masked(0)
                masked(1)
                if c.cmp:
                    p3 = c_p.rearrange("p (q c) -> p q c", c=NC)
                    m4 = cst("cmp_mask", NT).rearrange("p t (o c) -> p t o c", o=1).broadcast_to((P, NT, 4, NC))
                    dve.wait_ge(c.sem("cmp_scores"), i + 1)
                    ch.after(V.tensor_tensor(c_p.rearrange("p (t j c) -> p t j c", t=NT, c=NC),
                                             ps[7][:, :].rearrange("p (t j c) -> p t j c", t=NT, c=NC), m4, ALU.add))
                    ch.after(V.tensor_reduce(t_cm, p3, AX, ALU.max))
                    V.tensor_tensor(p3, p3, t_cm.rearrange("p (q o) -> p q o", o=1).broadcast_to((P, 16, NC)),
                                    ALU.subtract).then_inc(c.sem("cmp_shifted"), 1)
                pending = []
                for u in range(U):
                    if u + 2 < U:
                        masked(u + 2)
                    if u % 2 == 1:
                        _, _, _, k0, k1, _ = c.units[u]
                        dve.wait_ge(c.sem("turned"), U * i + (u + 1))
                        if u >= 3:
                            dve.wait_ge(c.sem("out"), U * i + (u - 2))
                        V.tensor_copy(t_pT[u % 3][:, 0:(k1 - k0) * P], ps[3 + u % 2][:, 0:(k1 - k0) * P])\
                            .then_inc(c.sem("keys_dve"), 1)
                    for j in list(pending):
                        if u >= c.last(j) + 3:
                            head(j)
                            pending.remove(j)
                    if u % c.per_head == c.per_head - 1:
                        pending.append(u // c.per_head)
                for j in pending:
                    head(j)
                if c.cmp:
                    dve.wait_ge(c.sem("cmp_probs"), i + 1)
                    ch.after(V.tensor_reduce(t_cl, p3, AX, ALU.add))
                    ch.after(V.reciprocal(t_cw, t_cl))
                    cw = t_cw.rearrange("p (t j) -> p t j", t=NT)
                    gates = proj[:, :, bass.ds(N_GT + 12 * i, 12)].rearrange("p t (j w) -> p t j w", w=3)[:, :, :, 0]
                    ch.after(V.tensor_tensor(cw, cw, gates, ALU.mult))
                    ch.after(V.tensor_tensor(cw, cw, cst("cmp_any").rearrange("p (t o) -> p t o", o=1)
                                             .broadcast_to((P, NT, 4)), ALU.mult))
                    dve.wait_ge(c.sem("cmp_out"), i + 1)
                    dve.wait_ge(c.sem("head"), c.heads * i + (c.heads + 1))
                    for h in range(2):
                        wq = t_cw[:, 8 * h:8 * h + 8].rearrange("p (q o) -> p q o", o=1).broadcast_to((P, 8, HD))
                        ch.after(V.tensor_tensor(t_tmp.rearrange("p (q d) -> p q d", d=HD),
                                                 ps[h][:, :].rearrange("p (q d) -> p q d", d=HD), wq, ALU.mult))
                        o = acc[:, 2 * h:2 * h + 2, bass.ds(i * 256, 256)]
                        ch.after(V.tensor_tensor(o, o, t_tmp.rearrange("p (t d) -> p t d", t=2), ALU.add))
                    V.tensor_copy(misc[:, 216:217], t_cw[:, 0:1]).then_inc(c.sem("cmp_done"), 1)
            ch.leave(per, c.turns)

        nsa = Attention("nsa", NG, 4, 2, cst("causal"), lambda i, k: (N_VS if k == 0 else N_VW) + i * HD,
                        lambda i: i * 256, lambda i: [(N_KS + i * HD, HD, 0), (N_KW + i * HD, HD, HD)], cmp_=True)
        even = Attention("even", 2, 4, 1, cst("band"), lambda i, k: E_V + i * HD, lambda i: i * 256,
                         lambda i: [(E_K + i * HD, HD, 0)], band=True, sink=True)
        odd = Attention("odd", 4, 2, 2, cst("dilated"), lambda i, k: O_V + i * 128 + k * HD, lambda i: i * 128,
                        lambda i: [(O_K + i * 128, 128, 0)])

        def cmp_pe(pe, c):
            T = nc.tensor
            wait_all(pe, linear_done("nsa_in", N_IN))
            for w in range(2):
                pe.wait_ge(S_("cmp_twice"), 2 * w + 2)
                for g in range(NG):
                    for t in range(NT):
                        src = acc[:, t, (4 * w + g) * P:(4 * w + g + 1) * P]
                        ins = T.transpose(ps[4 * w + g][:, t * P:(t + 1) * P], src, ident)
                    ins.then_inc(S_("cmp_src"), 1)
            pe.wait_ge(S_("cmp_low"), 8)
            for w in range(2):
                for h in range(2):
                    pe.wait_ge(lo_done, c.n + 1)
                    wv = [q[c.n % 2][:, :].rearrange("p (m n) -> p m n", m=8) for q in (whi, wlo)]
                    for m in range(8):
                        k, at = 4 * w + 2 * h + m // 4, (m % 4) * P
                        ins = three(ps[w][:, 0:256], (chi[:, k, at:at + P], clo[:, k, at:at + P]), (wv[0][:, m], wv[1][:, m]),
                                    h == 0 and m == 0, h == 1 and m == 7)
                    ins.then_inc(S_("cmp_hidden"), 1)
                    c.n += 1
            pe.wait_ge(S_("cmp_silu"), 2)
            for n in range(4):
                ins = T.transpose(ps[2][:, n * P:(n + 1) * P], c_hid[:, n * P:(n + 1) * P], ident)
            ins.then_inc(S_("cmp_hid_turned"), 1)
            pe.wait_ge(S_("cmp_hid_cols"), 3)
            pe.wait_ge(S_("nsa_params"), 64)
            for f in range(2):
                ins = T.matmul(ps[3][:, 0:HD], c_hT[:, f * P:(f + 1) * P], c_w2[:, 0, f, :], start=(f == 0), stop=(f == 1))
            ins.then_inc(S_("cmp_k"), 1)
            for g in range(NG):
                for f in range(2):
                    src = c_hTv[:, f, g * P:(g + 1) * P]
                    ins = T.matmul(ps[4][:, g * HD:(g + 1) * HD], src, c_w2[:, 1, f, :], start=(f == 0), stop=(f == 1))
            ins.then_inc(S_("cmp_v"), 1)
            pe.wait_ge(S_("cmp_k_turning"), 1)
            T.transpose(ps[5][0:HD, 0:P], c_row, ident).then_inc(S_("cmp_k_turned"), 1)
            pe.wait_ge(S_("cmp_k_cols"), 1)

        def end_cmp(c):
            c.n += 4
            c.last = [(S_("cmp_hidden"), 3, 0), (S_("cmp_hidden"), 4, 0)]

        def cmp_act(act, c):
            A = nc.scalar
            wait_all(act, linear_done("nsa_in", N_IN))
            act.wait_ge(S_("x_rows"), 2 * NT)
            for w, off in enumerate((N_KC, N_VC)):
                src = proj[:, :, off:off + 256].rearrange("p t (g d) -> p t g d", d=HD)
                dst = acc[:, :, w * 512:(w + 1) * 512].rearrange("p t (g h d) -> p t g h d", h=2, d=HD)
                for half in range(2):
                    A.copy(dst[:, :, :, half, :], src).then_inc(S_("cmp_twice"), 1)
            g = proj[:, :, N_GT:N_GT + 48]
            A.activation(g, g, ACT.Sigmoid).then_inc(S_("nsa_gates"), 1)
            high(act, c.n + 1, 0, None, c.last[1])
            for k in range(KC):
                act.wait_ge(S_("cmp_blocks"), k // 4 + 1)
                A.copy(chi[:, k, :], cols[:, k, :]).then_inc(S_("cmp_high"), 1)
            for n in (2, 3, 4):
                high(act, c.n + n, 0, None, (S_("cmp_hidden"), n - 1, 0))
            end_cmp(c)
            for w in range(2):
                act.wait_ge(S_("cmp_hidden"), 2 * w + 2)
                A.activation(c_hid[:, w * 256:(w + 1) * 256], ps[w][:, 0:256], ACT.Silu).then_inc(S_("cmp_silu"), 1)
            act.wait_ge(S_("cmp_hid_turned"), 1)
            A.copy(c_hT, ps[2][:, 0:256]).then_inc(S_("cmp_hid_cols"), 1)
            for f in range(2):
                A.copy(c_hTv[:, f, :].rearrange("p (g j c) -> p g j c", g=NG, j=4),
                       ps[2][:, (2 + f) * P:(3 + f) * P].rearrange("p (g o c) -> p g o c", g=NG, o=1)
                       .broadcast_to((P, NG, 4, NC))).then_inc(S_("cmp_hid_cols"), 1)
            act.wait_ge(S_("cmp_v"), 1)
            A.copy(c_vrep, ps[4][:, 0:256]).then_inc(S_("cmp_v_rows"), 1)
            act.wait_ge(S_("cmp_v_rows"), 1)
            act.wait_ge(S_("cmp_k_turned"), 1)
            A.copy(c_kT, ps[5][0:HD, 0:P]).then_inc(S_("cmp_k_cols"), 1)
            act.wait_ge(S_("mixer_ready"), 2)

        def cmp_dve(dve, ch, c):
            V = nc.vector
            dve.wait_ge(S_("nsa_params"), 64)
            wait_all(dve, linear_done("nsa_in", N_IN))
            for w in range(2):
                ch.after(V.memset(c_blk[w], 0.0))
            for w in range(2):
                blk = c_blk[w].rearrange("p (m g c) -> p m g c", m=16, g=NG)
                for g in range(NG):
                    dve.wait_ge(S_("cmp_src"), 4 * w + g + 1)
                    for half in range(2):
                        rows = slice(half * HD, (half + 1) * HD)
                        for mh in range(2):
                            src = ps[4 * w + g][rows, :].rearrange("p (c r) -> p c r", r=CST)[:, mh:mh + NC - 1, half::2]
                            pe_ = c_pe[rows, mh * 8:mh * 8 + 8].rearrange("p (m o) -> p m o", o=1)\
                                .broadcast_to((HD, 8, NC - 1))
                            ins = V.tensor_tensor(blk[rows, mh * 8:mh * 8 + 8, g, 0:NC - 1],
                                                  src.rearrange("p c m -> p m c"), pe_, ALU.add)
                            if g < NG - 1 or half == 0 or mh == 0:
                                ch.after(ins)
                ins.then_inc(S_("cmp_blocks"), 1)
            low(dve, c.n + 1, 0, None, None)
            for k in range(KC):
                dve.wait_ge(S_("cmp_high"), k + 1)
                V.tensor_tensor(clo[:, k, :], cols[:, k, :], chi[:, k, :].bitcast(F32), ALU.subtract)\
                    .then_inc(S_("cmp_low"), 1)
            cos, sin = cst("cos"), cst("sin")
            rope(dve, ch, proj[:, :, 0:D], NH, cos, sin, NT, more)
            low(dve, c.n + 2, 0, None, None)
            rope(dve, ch, proj[:, :, N_KS:N_KS + 256], NG, cos, sin, NT, more)
            low(dve, c.n + 3, 0, None, None)
            low(dve, c.n + 4, 0, None, None)
            end_cmp(c)
            rope(dve, ch, proj[:, :, N_KW:N_KW + 256], NG, cos, sin, NT, more)
            dve.wait_ge(S_("cmp_k"), 1)
            ch.after(V.tensor_copy(c_row, ps[3][:, 0:HD]))
            rope(dve, ch, c_row.rearrange("p (t d) -> p t d", t=1), 1, cst("cmp_cos"), cst("cmp_sin"), 1, more)
            V.tensor_copy(misc[:, 217:218], c_row[:, 0:1]).then_inc(S_("cmp_k_turning"), 1)
            ch.after(V.memset(c_vblk, 0.0))
            V.memset(misc[:, 218:219], 0.0).then_inc(S_("mixer_ready"), 1)

        w_conv = misc[:, 220:348]
        conv_w = w_conv[:, 0:4 * TAPS].rearrange("p (c k) -> p c k", c=4)
        conv_b = w_conv[:, 4 * TAPS:4 * TAPS + 4]
        PAD = TAPS - 1
        cT = proj[:, :, E_IN:E_IN + PAD + S]
        conv_out = cols[:, 0:4, :]

        def even_pe(pe):
            T = nc.tensor
            pe.wait_ge(S_("even_glu"), 1)
            for k in range(4):
                for t in range(NT):
                    ins = T.transpose(ps[k][:, t * P:(t + 1) * P], proj[:, t, E_GA + k * P:E_GA + (k + 1) * P], ident)
                ins.then_inc(S_("glu_turned"), 1)

        def even_conv_back_pe(pe):
            T = nc.tensor
            pe.wait_ge(S_("conv_done"), 4)
            for t in range(NT):
                for k in range(4):
                    ins = T.transpose(ps[t][:, k * P:(k + 1) * P], conv_out[:, k, t * P:(t + 1) * P], ident)
                ins.then_inc(S_("conv_turned"), 1)

        def even_act(act):
            A = nc.scalar
            wait_all(act, linear_done("even_in", E_IN))
            A.activation(proj[:, :, E_GB:E_GB + W2], proj[:, :, E_GB:E_GB + W2], ACT.Sigmoid)\
                .then_inc(S_("even_sigmoid"), 1)
            for k in range(4):
                act.wait_ge(S_("glu_turned"), k + 1)
                A.copy(cT[:, k, PAD:PAD + S], ps[k][:, :]).then_inc(S_("glu_cols"), 1)

        def even_dve(dve, ch):
            V = nc.vector
            wait_all(dve, linear_done("even_in", E_IN))
            dve.wait_ge(S_("even_sigmoid"), 1)
            V.tensor_tensor(proj[:, :, E_GA:E_GA + W2], proj[:, :, E_GA:E_GA + W2], proj[:, :, E_GB:E_GB + W2], ALU.mult)\
                .then_inc(S_("even_glu"), 1)
            ch.after(V.memset(cT[:, :, 0:PAD], 0.0))
            rope(dve, ch, proj[:, :, 0:640], 10, cst("cos"), cst("sin"), NT, more)
            dve.wait_ge(S_("even_params"), 16 * 8)
            for k in range(4):
                dve.wait_ge(S_("glu_cols"), k + 1)
                o = conv_out[:, k, :]
                ch.after(V.tensor_scalar(o, cT[:, k, 0:S], conv_w[:, k, 0:1], conv_b[:, k:k + 1], ALU.mult, ALU.add))
                for n in range(1, TAPS):
                    ins = V.scalar_tensor_tensor(out=o, in0=cT[:, k, n:n + S], scalar=conv_w[:, k, n:n + 1], in1=o,
                                                 op0=ALU.mult, op1=ALU.add)
                    if n < TAPS - 1:
                        ch.after(ins)
                    else:
                        ins.then_inc(S_("conv_done"), 1)
            V.memset(misc[:, 218:219], 0.0).then_inc(S_("mixer_ready"), 1)

        def norm512_act(act, ch, tag, src, dst, silu):
            A = nc.scalar
            for t in range(NT):
                scale_act(act, ch, tag, t, dst(t), src(t))
            if silu:
                for t in range(NT):
                    act.wait_ge(S_(f"biased{tag}"), t + 1)
                    A.activation(dst(t), dst(t), ACT.Silu).then_inc(S_(f"done{tag}"), 1)

        def norm512_pool(pool, ch, tag, dst, last):
            for t in range(NT):
                rstd_pool(pool, ch, tag, t)
            for t in range(NT):
                pool.wait_ge(S_("scaled"), norm_count(tag, t + 1))
                ch.after(nc.gpsimd.tensor_tensor(dst(t), dst(t), rowp[:, 0, 0:W2], ALU.mult))
                nc.gpsimd.tensor_tensor(dst(t), dst(t), rowp[:, 1, 0:W2], ALU.add).then_inc(S_(last), 1)

        def conv_dst(t):
            return acc[:, t, W2:D]

        spat = proj[:, :, O_IN:O_IN + 256].rearrange("p a (b s) -> p a b s", b=2)
        spatT = cols[:, 0:2, :].rearrange("p a s -> p (a s)")
        spat_b = misc[:, 220:228]

        def sgu_dst(t):
            return proj[:, t, O_G:O_G + W2]

        def odd_pe(pe):
            T = nc.tensor
            wait_all(pe, linear_done("odd_in", O_IN))
            pe.wait_ge(S_("odd_params"), 16 * 7)
            for g in range(8):
                ins = T.transpose(ps[g // 4][:, (g % 4) * P:(g % 4 + 1) * P], spat[:, g // 2, g % 2, :], ident)
            ins.then_inc(S_("spatial_turned"), 1)
            pe.wait_ge(S_("spatial_cols"), 2)
            pe.wait_ge(S_("sgu_normed"), NT)
            for g in range(8):
                T.matmul(ps[2 + g // 2][:, (g % 2) * 256:(g % 2 + 1) * 256], spatT[:, g * P:(g + 1) * P],
                         proj[:, :, O_G + g * HD:O_G + (g + 1) * HD], start=True, stop=True).then_inc(S_("mixed"), 1)

        def odd_act(act, ch):
            A = nc.scalar
            wait_all(act, linear_done("odd_in", O_IN))
            for t in range(NT):
                z = proj[:, t, O_G:O_G + W2]
                A.activation(z, z, ACT.Gelu_apprx_tanh).then_inc(S_("gelu_g"), 1)
            z = proj[:, :, O_U:O_U + W2]
            A.activation(z, z, ACT.Gelu_apprx_tanh).then_inc(S_("gelu_u"), 1)
            norm512_act(act, ch, "sgu", sgu_dst, sgu_dst, False)

        def odd_dve(dve, ch):
            V = nc.vector
            for t in range(NT):
                dve.wait_ge(S_("gelu_g"), t + 1)
                stats_dve(dve, ch, "sgu", t, sgu_dst(t), W2)
            wait_all(dve, linear_done("odd_in", O_IN))
            rope(dve, ch, proj[:, :, 0:D], 16, cst("cos"), cst("sin"), NT, more)
            dve.wait_ge(S_("spatial_turned"), 1)
            up = cst("upper").rearrange("p (o t) -> p o t", o=1).broadcast_to((P, 4, P))
            for h in range(2):
                V.tensor_tensor(spatT[:, h * 512:(h + 1) * 512].rearrange("p (g t) -> p g t", g=4),
                                ps[h][:, :].rearrange("p (g t) -> p g t", g=4), up, ALU.mult)\
                    .then_inc(S_("spatial_cols"), 1)
            dve.wait_ge(S_("gelu_u"), 1)
            for g in range(8):
                dve.wait_ge(S_("mixed"), g + 1 if g % 2 else g + 2)
                V.scalar_tensor_tensor(out=acc[:, :, W2 + g * HD:W2 + (g + 1) * HD],
                                       in0=ps[2 + g // 2][:, (g % 2) * 256:(g % 2 + 1) * 256]
                                       .rearrange("p (t d) -> p t d", t=NT),
                                       scalar=spat_b[:, g:g + 1], in1=proj[:, :, O_U + g * HD:O_U + (g + 1) * HD],
                                       op0=ALU.add, op1=ALU.mult).then_inc(S_("gated"), 1)
            V.memset(misc[:, 218:219], 0.0).then_inc(S_("mixer_ready"), 1)

        PARAMS = 16 * 12
        ctx.enter_context(nc.allow_non_contiguous_dma(reason="a few small tables are read by columns"))
        block = ctx.enter_context(nc.Block())
        ffn_gate = lambda t, e: None
        moe_gate = lambda t, e: gate[:, t, bass.ds(e, 1)]

        @block.sync
        def _(sp):
            c = Count()
            sp.dma_start(con[:, :], a["consts"]).then_inc(S_("consts"), 16)
            sp.dma_start(x[:, :, :], a["x"][0].rearrange("(t p) d -> p t d", p=P)).then_inc(S_("x_landed"), 16)
            sp.dma_start(w_up, a["gla_w_gate_up"][0]).then_inc(S_("params"), 16)
            sp.dma_start(b_gate, bcast(a["gla_b_gate"][0], GH * GDK)).then_inc(S_("params"), 16)
            sp.dma_start(norm_g, bcast(a["gla_norm_g"][0], GDV)).then_inc(S_("params"), 16)
            sp.dma_start(wr[:, :, :], a["moe_w_router"].rearrange("(k p) e -> p k e", p=P)).then_inc(S_("params"), 16)
            sp.dma_start(br[:, :], bcast(a["moe_b_router"], NE)).then_inc(S_("params"), 16)
            sp.dma_start(colp[:, 0, 0:4, :], a["ln_g"].rearrange("l i (k p) -> p (l i) k", p=P)).then_inc(S_("params"), 16)
            sp.dma_start(colp[:, 1, 0:4, :], a["ln_b"].rearrange("l i (k p) -> p (l i) k", p=P)).then_inc(S_("params"), 16)
            for n in range(4, 9):
                sp.dma_start(colp[:, 0, n, :], norm_rows(n)[0].rearrange("(k p) -> p k", p=P)).then_inc(S_("params"), 16)
            load_linear(sp, c, "gla_in", a["gla_w_in"][0], G_IN)
            load_linear(sp, c, "gla_out", a["gla_w_out"][0], D)
            load_ff(sp, c, "moe0", moe_views(0), NE)
            load_linear(sp, c, "nsa_in", a["nsa_w_in"][0], N_IN)
            load_cmp(sp, c)
            load_linear(sp, c, "nsa_out", a["nsa_w_out"][0], D)
            load_ff(sp, c, "moe1", moe_views(1), NE)
            load_linear(sp, c, "even_in", a["ev_w_in_2"][0], E_IN)
            load_linear(sp, c, "even_out", a["ev_w_out_2"][0], D)
            load_ff(sp, c, "ffn0", ffn_views(0), DFF // FF)
            load_linear(sp, c, "odd_in", a["od_w_in_2"][0], O_IN)
            load_linear(sp, c, "odd_out", a["od_w_out_2"][0], D)
            load_ff(sp, c, "ffn1", ffn_views(1), DFF // FF)
            sp.wait_ge(S_("result"), NT)
            sp.dma_start(out[0].rearrange("(t p) d -> p t d", p=P), acc[:, :, :]).then_inc(S_("stored"), 16)
            sp.wait_ge(S_("stored"), 16)

        @block.tensor
        def _(pe):
            c = Count()
            turn_pe(pe, "in", x, [(S_("consts"), 16), (S_("x_landed"), 16)])
            linear_pe(pe, c, "gla_in", G_IN, "in")
            gla_pe(pe)
            turn_pe(pe, "gla_out", acc, [(S_("mixer_ready"), 1)])
            out_pe(pe, c, "gla_out")
            turn_pe(pe, "n0", acc, [(S_("scaled"), norm_count(0))])
            router_pe(pe, 0, "n0")
            ff_pe(pe, c, "moe0", NE, "n0")
            turn_pe(pe, "n1", acc, [(S_("scaled"), norm_count(1))])
            linear_pe(pe, c, "nsa_in", N_IN, "n1")
            cmp_pe(pe, c)
            attn_pe(pe, nsa)
            turn_pe(pe, "nsa_out", acc, [(nsa.sem("cmp_done"), NG + 1), (nsa.sem("head"), NH + 1)])
            out_pe(pe, c, "nsa_out")
            turn_pe(pe, "n2", acc, [(S_("scaled"), norm_count(2))])
            router_pe(pe, 1, "n2")
            ff_pe(pe, c, "moe1", NE, "n2")
            turn_pe(pe, "n4", acc, [(S_("scaled"), norm_count(4))])
            linear_pe(pe, c, "even_in", E_IN, "n4")
            even_pe(pe)
            attn_pe(pe, even)
            even_conv_back_pe(pe)
            turn_pe(pe, "even_out", acc, [(S_("doneconv"), NT), (even.sem("head"), 8 + 1)])
            out_pe(pe, c, "even_out")
            turn_pe(pe, "n5", acc, [(S_("scaled"), norm_count(5))])
            ff_pe(pe, c, "ffn0", DFF // FF, "n5")
            turn_pe(pe, "n6", acc, [(S_("scaled"), norm_count(6))])
            linear_pe(pe, c, "odd_in", O_IN, "n6")
            odd_pe(pe)
            attn_pe(pe, odd)
            turn_pe(pe, "odd_out", acc, [(S_("gated"), 8), (odd.sem("head"), 8 + 1)])
            out_pe(pe, c, "odd_out")
            turn_pe(pe, "n7", acc, [(S_("scaled"), norm_count(7))])
            ff_pe(pe, c, "ffn1", DFF // FF, "n7")

        @block.scalar
        def _(act):
            ch = Chain(act, S_("act"))
            c = Count()
            high(act, 0, 0, None, None)
            turn_evac(act, "in", 0)
            act.wait_ge(S_("params"), PARAMS)
            nc.scalar.copy(wrh[:, :, :], wr[:, :, :]).then_inc(S_("router_high"), 1)
            linear_evac(act, c, "gla_in", G_IN, 0)
            gla_act(act, ch)
            turn_evac(act, "gla_out", 0)
            out_act(act, c, "gla_out")
            norm_act(act, ch, 0)
            act.wait_ge(S_("params"), PARAMS)
            turn_evac(act, "n0", 0, 0)
            router_act(act, 0)
            ff_act(act, c, "moe0", NE)
            norm_act(act, ch, 1)
            turn_evac(act, "n1", 0, 1)
            linear_evac(act, c, "nsa_in", N_IN, 0)
            cmp_act(act, c)
            attn_act(act, nsa)
            turn_evac(act, "nsa_out", 0)
            out_act(act, c, "nsa_out")
            norm_act(act, ch, 2)
            turn_evac(act, "n2", 0, 2)
            router_act(act, 1)
            ff_act(act, c, "moe1", NE)
            norm_act(act, ch, 3)
            norm_act(act, ch, 4)
            turn_evac(act, "n4", 0, 4)
            linear_evac(act, c, "even_in", E_IN, 0)
            even_act(act)
            act.wait_ge(S_("mixer_ready"), 3)
            attn_act(act, even)
            act.wait_ge(S_("conv_turned"), NT)
            norm512_act(act, ch, "conv", lambda t: ps[t][:, :], conv_dst, True)
            turn_evac(act, "even_out", 0)
            out_act(act, c, "even_out")
            norm_act(act, ch, 5)
            turn_evac(act, "n5", 0, 5)
            ff_act(act, c, "ffn0", DFF // FF)
            norm_act(act, ch, 6)
            turn_evac(act, "n6", 0, 6)
            linear_evac(act, c, "odd_in", O_IN, 0)
            odd_act(act, ch)
            act.wait_ge(S_("mixer_ready"), 4)
            attn_act(act, odd)
            turn_evac(act, "odd_out", 0)
            out_act(act, c, "odd_out")
            norm_act(act, ch, 7)
            turn_evac(act, "n7", 0, 7)
            ff_act(act, c, "ffn1", DFF // FF)
            norm_act(act, ch, 8)

        @block.gpsimd
        def _(pool):
            ch = Chain(pool, S_("pool"))

            def load_rows(n):
                for i in range(2):
                    pool.dma_start(rowp[:, i, :], bcast(norm_rows(n)[i], D)).then_inc(S_("gain_rows"), 16)

            load_rows(0)
            pool.wait_ge(turned, KC)
            nc.gpsimd.tensor_scalar(x[:, :, :], x[:, :, :], ALPHA, None, ALU.mult).then_inc(S_("x_scaled"), 1)
            gla_pool(pool)
            norm_pool(pool, ch, 0)
            pool.wait_ge(S_("x_rows"), 1 * NT)
            load_rows(1)
            for w, name in enumerate(("nsa_w_cmp_k2", "nsa_w_cmp_v2")):
                pool.dma_start(c_w2[:, w, :, :], a[name][0].rearrange("(f p) d -> p f d", p=P)).then_inc(S_("nsa_params"), 16)
            for half in range(2):
                pool.dma_start(c_pe[half * HD:(half + 1) * HD, :], a["nsa_cmp_pe"][0]
                               .rearrange("(m h) d -> h d m", h=2)[half]).then_inc(S_("nsa_params"), 16)
            norm_pool(pool, ch, 1)
            pool.wait_ge(S_("x_rows"), 2 * NT)
            load_rows(2)
            norm_pool(pool, ch, 2)
            pool.wait_ge(S_("x_rows"), 3 * NT)
            load_rows(3)
            norm_pool(pool, ch, 3)
            pool.wait_ge(S_("x_rows"), 4 * NT)
            pool.dma_start(rowp[:, 0, 0:W2], bcast(a["ev_conv_ln_g_2"][0], W2)).then_inc(S_("even_params"), 16)
            pool.dma_start(rowp[:, 1, 0:W2], bcast(a["ev_conv_ln_b_2"][0], W2)).then_inc(S_("even_params"), 16)
            pool.dma_start(sinks, bcast(a["ev_sinks_2"][0], 8)).then_inc(S_("even_params"), 16)
            for k in range(4):
                pool.dma_start(conv_w[:, k, :], a["ev_conv_w_2"][0][:, k * P:(k + 1) * P].rearrange("n p -> p n"))\
                    .then_inc(S_("even_params"), 16)
            pool.dma_start(conv_b, a["ev_conv_b_2"][0].rearrange("(k p) -> p k", p=P)).then_inc(S_("even_params"), 16)
            norm_pool(pool, ch, 4)
            norm512_pool(pool, ch, "conv", conv_dst, "biasedconv")
            norm_pool(pool, ch, 5)
            pool.wait_ge(S_("biasedconv"), NT)
            pool.wait_ge(S_("stats"), norm_count(5))
            pool.dma_start(rowp[:, 0, 0:W2], bcast(a["od_sgu_ln_g_2"][0], W2)).then_inc(S_("odd_params"), 16)
            pool.dma_start(rowp[:, 1, 0:W2], bcast(a["od_sgu_ln_b_2"][0], W2)).then_inc(S_("odd_params"), 16)
            pool.dma_start(spat_b, a["od_spatial_b_2"][0].rearrange("g t -> t g")).then_inc(S_("odd_params"), 16)
            for n in range(4):
                pool.dma_start(spat[:, n, :, :], a["od_spatial_w_2"][0, 2 * n:2 * n + 2].rearrange("g t s -> t g s"))\
                    .then_inc(S_("odd_params"), 16)
            norm_pool(pool, ch, 6)
            pool.wait_ge(S_("odd_params"), 16 * 7)
            norm512_pool(pool, ch, "sgu", sgu_dst, "sgu_normed")
            norm_pool(pool, ch, 7)
            pool.wait_ge(S_("sgu_normed"), NT)
            pool.dma_start(rowp[:, 0, :], bcast(norm_rows(8)[0], D)).then_inc(S_("final_gain"), 16)
            norm_pool(pool, ch, 8)
            pool.wait_ge(S_("final_gain"), 16)
            for t in range(NT):
                pool.wait_ge(S_("scaled"), norm_count(8, t + 1))
                nc.gpsimd.tensor_tensor(acc[:, t, :], acc[:, t, :], rowp[:, 0, :], ALU.mult).then_inc(S_("result"), 1)

        @block.vector
        def _(dve):
            ch = Chain(dve, S_("dve"))
            c = Count()

            def stats(n):
                return lambda t: stats_dve(dve, ch, n, t)

            low(dve, 0, 0, None, None)
            turn_evac(dve, "in", 1)
            dve.wait_ge(S_("router_high"), 1)
            nc.vector.tensor_tensor(wrl[:, :, :], wr[:, :, :], wrh[:, :, :].bitcast(F32), ALU.subtract)\
                .then_inc(S_("router_low"), 1)
            linear_evac(dve, c, "gla_in", G_IN, 1)
            dve.wait_ge(S_("params"), PARAMS)
            gla_dve(dve, ch)
            nc.vector.memset(misc[:, 218:219], 0.0).then_inc(S_("mixer_ready"), 1)
            turn_evac(dve, "gla_out", 1)
            out_dve(dve, c, "gla_out", stats(0), [(S_("x_scaled"), 1)])
            turn_evac(dve, "n0", 1, 0)
            router_dve(dve, ch, 0)
            ff_dve(dve, c, "moe0", NE, moe_gate, stats(1), [(S_("x_rows"), 1 * NT)])
            turn_evac(dve, "n1", 1, 1)
            linear_evac(dve, c, "nsa_in", N_IN, 1)
            cmp_dve(dve, ch, c)
            dve.wait_ge(S_("nsa_gates"), 1)
            attn_dve(dve, ch, nsa)
            turn_evac(dve, "nsa_out", 1)
            out_dve(dve, c, "nsa_out", stats(2), [(S_("x_rows"), 2 * NT)])
            turn_evac(dve, "n2", 1, 2)
            router_dve(dve, ch, 1)
            ff_dve(dve, c, "moe1", NE, moe_gate, stats(3), [(S_("x_rows"), 3 * NT)])
            dve.wait_ge(S_("x_rows"), 4 * NT)
            for t in range(NT):
                stats_dve(dve, ch, 4, t)
            turn_evac(dve, "n4", 1, 4)
            linear_evac(dve, c, "even_in", E_IN, 1)
            even_dve(dve, ch)
            attn_dve(dve, ch, even)
            for t in range(NT):
                dve.wait_ge(S_("conv_turned"), t + 1)
                stats_dve(dve, ch, "conv", t, ps[t][:, :], W2)
            turn_evac(dve, "even_out", 1)
            out_dve(dve, c, "even_out", stats(5))
            turn_evac(dve, "n5", 1, 5)
            ff_dve(dve, c, "ffn0", DFF // FF, ffn_gate, stats(6), [])
            turn_evac(dve, "n6", 1, 6)
            linear_evac(dve, c, "odd_in", O_IN, 1)
            odd_dve(dve, ch)
            attn_dve(dve, ch, odd)
            turn_evac(dve, "odd_out", 1)
            out_dve(dve, c, "odd_out", stats(7))
            turn_evac(dve, "n7", 1, 7)
            ff_dve(dve, c, "ffn1", DFF // FF, ffn_gate, stats(8), [])


INPUTS = ["x", "gla_w_in", "gla_w_gate_up", "gla_b_gate", "gla_norm_g", "gla_w_out", "nsa_w_in", "nsa_w_cmp_k1",
          "nsa_w_cmp_k2", "nsa_w_cmp_v1", "nsa_w_cmp_v2", "nsa_cmp_pe", "nsa_w_out", "moe_w_router", "moe_b_router",
          "moe_w_gate", "moe_w_up", "moe_w_down", "ln_g", "ln_b", "ev_norm_g_2", "ev_w_in_2", "ev_sinks_2",
          "ev_conv_w_2", "ev_conv_b_2", "ev_conv_ln_g_2", "ev_conv_ln_b_2", "ev_w_out_2", "od_norm_g_2",
          "od_w_in_2", "od_sgu_ln_g_2", "od_sgu_ln_b_2", "od_spatial_w_2", "od_spatial_b_2", "od_w_out_2",
          "ffn_norm_g_2", "ffn_w_gate_2", "ffn_w_up_2", "ffn_w_down_2", "final_norm_g_2"]


def kernel(**inputs):
    import concourse.bacc as bacc
    from concourse.bass_utils import run_bass_kernel_spmd

    nc = bacc.Bacc("TRN2", target_bir_lowering=False, num_devices=1)
    arrays = {name: np.ascontiguousarray(inputs[name]) for name in INPUTS}
    arrays["consts"] = constants()
    tensors = {n: nc.dram_tensor("in_" + n, v.shape, F32, kind="ExternalInput").ap() for n, v in arrays.items()}
    out = nc.dram_tensor("out", (1, S, D), F32, kind="ExternalOutput").ap()
    build(nc, tensors, out)
    r = run_bass_kernel_spmd(nc, [{"in_" + n: v for n, v in arrays.items()}], core_ids=[0])
    return r.results[0]["out"]
```

```python
from contextlib import ExitStack

import numpy as np
import concourse.bass as bass
from concourse import mybir

F32 = mybir.dt.float32
F32R = mybir.dt.float32r
U32 = mybir.dt.uint32
ALU = mybir.AluOpType
ACT = mybir.ActivationFunctionType
AX = mybir.AxisListType.X

P = 128
S = 512
NT = S // P
D = 1024
KC = D // P
NEG = -1e30
BIG = 3e38
LN_EPS = 1e-5
RMS_EPS = 1e-6
ALPHA = 4.0 ** 0.25

GH, GDK, GDV, GC, GR = 4, 128, 256, 64, 16
G_Q, G_K, G_V, G_G, G_R, G_IN = 0, 512, 1024, 2048, 2064, 3088
NCH = S // GC
HD = 64
NH, NG = 16, 4
N_KC, N_VC, N_KS, N_VS, N_KW, N_VW, N_GT, N_IN = 1024, 1280, 1536, 1792, 2048, 2304, 2560, 2608
NC = 32
CB = 32
CST = 16
NE, FF = 16, 256
DFF = 2816
E_K, E_V, E_GA, E_GB, E_IN = 512, 640, 768, 1280, 1792
TAPS = 31
O_K, O_V, O_U, O_G, O_IN = 512, 1024, 1536, 2048, 2560
UNIT = 2048
W2 = 512

CONSTS = {}
for _name, _width in (("ident", P), ("gla_mask", P), ("gla_sum", P), ("upper", P), ("causal", S), ("band", 2 * P),
                      ("dilated", S), ("cmp_mask", NT * NC), ("cmp_any", NT), ("cos", NT * 8), ("sin", NT * 8),
                      ("cmp_cos", 8), ("cmp_sin", 8), ("index4", 4), ("ones", NT * NE), ("minus_half", NT)):
    CONSTS[_name] = (sum(w for _, w in CONSTS.values()), _width)
CONST_W = sum(w for _, w in CONSTS.values())


def constants():
    f = np.float32
    t = np.zeros((P, CONST_W), f)

    def put(name, a):
        at, w = CONSTS[name]
        t[:, at:at + w] = np.asarray(a, f).reshape(P, w)

    p = np.arange(P)[:, None]
    q = np.arange(P)[None, :]
    put("ident", p == q)
    same = (p // GC == q // GC) & (p <= q)
    put("gla_mask", same)
    put("gla_sum", same / 16.0)
    put("upper", p <= q)
    d = p + 3 * P - np.arange(S)[None, :]
    put("causal", np.where(d >= 0, 0.0, NEG))
    db = p + P - np.arange(2 * P)[None, :]
    put("band", np.where((db >= 0) & (db <= P - 1), 0.0, NEG))
    n = (d <= 128).astype(int) + (d % 4 == 0) + (d % 16 == 0)
    put("dilated", np.where((d >= 0) & (n > 0), np.log(np.maximum(n, 1).astype(np.float64)), NEG))
    qpos = np.arange(NT)[None, :] * P + p
    c = np.arange(NC)
    ok = (c * CST + CB - 1 <= qpos[:, :, None]) & (c < NC - 1)
    put("cmp_mask", np.where(ok, 0.0, NEG))
    put("cmp_any", ok.any(-1))
    inv = np.power(f(500000.0), -np.arange(8, dtype=f) * f(2.0 / 16)).astype(f)
    ang = qpos.astype(f)[:, :, None] * inv
    put("cos", np.cos(ang))
    put("sin", np.sin(ang))
    cend = ((np.arange(P) % NC) * CST + CB - 1).astype(f)[:, None] * inv
    put("cmp_cos", np.cos(cend))
    put("cmp_sin", np.sin(cend))
    put("index4", np.broadcast_to(np.arange(4), (P, 4)))
    put("ones", np.ones((P, NT * NE)))
    put("minus_half", np.full((P, NT), -0.5))
    return t


class Chain:

    def __init__(self, eng, sem):
        self.eng, self.sem, self.n, self.turn = eng, sem, 0, None

    def after(self, ins):
        ins.then_inc(self.sem, 1)
        self.n += 1
        self.eng.wait_ge(self.sem, self.n if self.turn is None else self.turn + self.n)

    def enter(self, i, per):
        self.turn, self.base = i * per, self.n

    def leave(self, per, times):
        assert self.n - self.base == per, (self.n - self.base, per)
        self.turn, self.n = None, self.base + per * times


def build(nc, a, out):
    with ExitStack() as ctx:
        def sb(name, shape):
            return ctx.enter_context(nc.sbuf_tensor(name, shape, F32))

        sems = {}

        def S_(name):
            if name not in sems:
                sems[name] = ctx.enter_context(nc.semaphore(name))
            return sems[name]

        ps = [ctx.enter_context(nc.psum_tensor(f"ps{i}", [P, S], F32)) for i in range(8)]

        con = sb("con", [P, CONST_W])
        x = sb("x", [P, NT, D])
        cols_at = nc.sbuf_base
        cols = sb("cols", [P, KC, S])
        acc = sb("acc", [P, NT, D])
        proj = sb("proj", [P, NT, G_IN])
        raw = [sb(f"raw{i}", [P, UNIT]) for i in range(2)]
        whi = [ctx.enter_context(nc.sbuf_tensor(f"whi{i}", [P, UNIT], F32R)) for i in range(2)]
        wlo = [ctx.enter_context(nc.sbuf_tensor(f"wlo{i}", [P, UNIT], F32R)) for i in range(2)]
        work_at = nc.sbuf_base
        work = sb("work", [P, 4096])
        more_at = nc.sbuf_base
        more = sb("more", [P, 6144])
        chi = nc.alloc_sbuf_tensor_at("cols_high", [P, KC, S], F32R, offset=work_at)
        clo = nc.alloc_sbuf_tensor_at("cols_low", [P, KC, S], F32R, offset=cols_at)
        hhi = nc.alloc_sbuf_tensor_at("hidden_high", [P, 2, 2, S], F32R, offset=more_at + 8192)
        hlo = nc.alloc_sbuf_tensor_at("hidden_low", [P, 2, 2, S], F32R, offset=more_at + 16384)
        rowp = sb("rowp", [P, 2, D])
        colp = sb("colp", [P, 2, 9, KC])
        small = sb("small", [P, 1024])

        def cst(name, *shape):
            at, w = CONSTS[name]
            v = con[:, at:at + w]
            return v.rearrange("p (a b) -> p a b", a=shape[0]) if shape else v

        ident = cst("ident")

        hbuf = [more[:, i * 1024:(i + 1) * 1024].rearrange("p (c s) -> p c s", c=2) for i in range(2)]
        gate = small[:, 0:NT * NE].rearrange("p (t e) -> p t e", t=NT)
        bst = small[:, 64:64 + 48].rearrange("p (t a s) -> p t a s", t=NT, a=2)
        mv = small[:, 112:120].rearrange("p (t s) -> p t s", t=NT)
        rstd = small[:, 120:124]
        nmr = small[:, 124:128]
        rt = small[:, 160:160 + 6 * 64]
        gsc = small[:, 560:560 + 96]
        misc = small[:, 672:1024]

        raw_landed = [S_("raw_landed0"), S_("raw_landed1")]
        hi_done, lo_done = S_("weights_high"), S_("weights_low")

        TURNS = ["in", "gla_out", "n0", "n1", "nsa_out", "n2", "n4", "even_out", "n5", "n6", "odd_out", "n7"]
        turned, cols_act, cols_dve = S_("turned"), S_("cols_act"), S_("cols_dve")
        cols_hi, cols_lo = S_("cols_high"), S_("cols_low")

        WIDTHS = {"gla_in": G_IN, "gla_out": D, "nsa_in": N_IN, "nsa_out": D, "even_in": E_IN, "even_out": D,
                  "odd_in": O_IN, "odd_out": D}
        UNITS, READS, PIECES = {}, {}, {}
        units = reads = pieces = 0
        for name_, width_ in WIDTHS.items():
            UNITS[name_], READS[name_] = units, reads
            units += -(-width_ // S)
            reads += -(-width_ // S) if width_ != D else 0
        for name_, n_ in (("moe0", NE), ("moe1", NE), ("ffn0", DFF // FF), ("ffn1", DFF // FF)):
            PIECES[name_] = pieces
            pieces += n_
        READS_OF = ["gla_in", "nsa_in", "even_in", "odd_in"]
        OUTS = ["gla_out", "nsa_out", "even_out", "odd_out"]
        half_done, product = S_("half_done"), S_("product")
        read_act, read_dve, added = S_("read_act"), S_("read_dve"), S_("added")
        gate_ready, up_ready, silu = S_("gate_ready"), S_("up_ready"), S_("silu")
        h_whole, h_high, h_low = S_("hidden_whole"), S_("hidden_high"), S_("hidden_low")
        y_ready, y_added = S_("down"), S_("down_added")

        def val(at, per=0, i=None):
            return at if i is None or not per else i * per + at

        def linear_used(name, u, half):
            return (product, 4 * (UNITS[name] + u + 1), 4) if half else (half_done, UNITS[name] + u + 1, 1)

        def piece_used(name, e, what):
            e += PIECES[name] + 1
            return {"gate": (gate_ready, 2 * e, 2), "up": (up_ready, 2 * e, 2), "down": (y_ready, 8 * e, 8)}[what]

        PARAMS = 16 * 13
        NSA_PARAMS = 16 * 4
        EVEN_PARAMS = NSA_PARAMS + 16 * 8
        ODD_PARAMS = EVEN_PARAMS + 16 * 7
        FINAL_PARAMS = ODD_PARAMS + 16

        class Count:

            def __init__(self):
                self.n = 0
                self.last = [None, None]

        def chunks(eng, n_cols, body):
            full, rest = divmod(n_cols, S)
            widths = [S] * full + ([rest] if rest else []) + [None]
            pairs = (full - 2) // 2
            body(0, None, widths[1])
            if pairs:
                with eng.Fori(0, pairs) as i:
                    for j in range(2):
                        body(1 + j, i, S)
            for u in range(1 + 2 * pairs, len(widths) - 1):
                body(u, None, widths[u + 1])

        def pieces_of(eng, n_exp, body):
            body(0, None)
            body(1, None)
            pairs = (n_exp - 3) // 2
            with eng.Fori(0, pairs) as i:
                for j in range(2):
                    body(2 + j, i)
            for e in range(2 + 2 * pairs, n_exp):
                body(e, None)

        def land(sp, n, per, i, dst, src):
            if n >= 2:
                sp.wait_ge(lo_done, val(n - 1, per, i))
            sp.dma_start(dst, src).then_inc(raw_landed[n % 2], 16)

        def piece(v, width):
            return v[:, :] if width == S else v[:, :].rearrange("p (k n) -> p k n", n=S)[:, :, 0:width]

        def high(act, n, per, i, used, width=S):
            act.wait_ge(raw_landed[n % 2], val(16 * (n // 2 + 1), 8 * per, i))
            if used:
                act.wait_ge(used[0], val(used[1], used[2], i))
            nc.scalar.copy(piece(whi[n % 2], width), piece(raw[n % 2], width)).then_inc(hi_done, 1)

        def low(dve, n, per, i, used, width=S):
            dve.wait_ge(hi_done, val(n + 1, per, i))
            nc.vector.tensor_tensor(piece(wlo[n % 2], width), piece(raw[n % 2], width),
                                    piece(whi[n % 2], width).bitcast(F32), ALU.subtract).then_inc(lo_done, 1)

        def twice(used):
            return used and (used[0], used[1], 2 * used[2])

        def three(out, lhs, rhs, first, last):
            (lh, ll), (rh, rl) = lhs, rhs
            nc.tensor.matmul(out, lh, rh, start=first, stop=False)
            nc.tensor.matmul(out, lh, rl, start=False, stop=False)
            return nc.tensor.matmul(out, ll, rh, start=False, stop=last)

        def load_linear(sp, c, name, w, n_cols, after_first=lambda: None):
            wv = w.rearrange("(k p) n -> p k n", p=P)

            def body(u, i, _):
                width = min(S, n_cols - u * S) if i is None else S
                for h in range(2):
                    n = c.n + 2 * u + h
                    cs = bass.ds(val(u * S, 2 * S, i), width)
                    dst = raw[n % 2][:, :].rearrange("p (k n) -> p k n", k=4)[:, :, 0:width]
                    land(sp, n, 4, i, dst, wv[:, 4 * h:4 * h + 4, cs])
                if u == 0:
                    after_first()

            chunks(sp, n_cols, body)
            c.n += 2 * (-(-n_cols // S))

        def load_ff(sp, c, name, views, n_exp):
            def gate_up(e, i, w, n):
                dst = raw[n % 2][:, :].rearrange("p (k n) -> p k n", k=KC)
                land(sp, n, 6, i, dst, views(val(e, 2, i))[w])

            def body(e, i):
                n = c.n + 3 * e - 1 if e else c.n
                gate_up(e, i, 0, n)
                gate_up(e, i, 1, n + 1)
                if e:
                    down(e - 1, i, n + 2)

            def down(e, i, n):
                dst = raw[n % 2][:, :].rearrange("p (h n) -> p h n", h=2)
                land(sp, n, 6, i, dst, views(val(e, 2, i))[2])

            pieces_of(sp, n_exp, body)
            down(n_exp - 1, None, c.n + 3 * n_exp - 1)
            c.n += 3 * n_exp

        def load_cmp(sp, c):
            for w in ("nsa_w_cmp_k1", "nsa_w_cmp_v1"):
                wv = a[w][0].rearrange("(m p) n -> p m n", p=P)
                for h in range(2):
                    dst = raw[c.n % 2][:, :].rearrange("p (m n) -> p m n", m=8)
                    land(sp, c.n, 0, None, dst, wv[:, 8 * h:8 * h + 8])
                    c.n += 1

        def moe_views(layer):
            g, u, d = a["moe_w_gate"][layer], a["moe_w_up"][layer], a["moe_w_down"][layer]

            def at(e):
                pick = bass.ds(e, 1)
                return (g[pick].rearrange("e (k p) f -> p (e k) f", p=P), u[pick].rearrange("e (k p) f -> p (e k) f", p=P),
                        d[pick].rearrange("e (c p) n -> p (e c) n", p=P))
            return at

        def ffn_views(layer):
            g = a["ffn_w_gate_2"][layer].rearrange("(k p) f -> p k f", p=P)
            u = a["ffn_w_up_2"][layer].rearrange("(k p) f -> p k f", p=P)
            d = a["ffn_w_down_2"][layer].rearrange("(c p) n -> p c n", p=P)

            def at(e):
                cs = bass.ds(e * FF, FF)
                return g[:, :, cs], u[:, :, cs], d[:, bass.ds(e * 2, 2), :]
            return at

        def norm_rows(n):
            if n < 4:
                return a["ln_g"][n // 2, n % 2], a["ln_b"][n // 2, n % 2]
            return {4: a["ev_norm_g_2"][0], 5: a["ffn_norm_g_2"][0], 6: a["od_norm_g_2"][0],
                    7: a["ffn_norm_g_2"][1], 8: a["final_norm_g_2"]}[n], None

        def bcast(row, n):
            return row.rearrange("(o n) -> o n", o=1).broadcast_to((P, n))

        def split_chunk(split, eng, c, name, u, i, next_width, width):
            n = c.n + 2 * u
            before = twice(linear_used(name, u - 1, 1)) if u else c.last[1]
            split(eng, n + 1, 4, i, before, width)
            split(eng, n + 2, 4, i, twice(linear_used(name, u, 0)), next_width or S)

        def end_linear(c, name, n_cols):
            n = -(-n_cols // S)
            c.n += 2 * n
            c.last = [linear_used(name, n - 1, 0), linear_used(name, n - 1, 1)]

        def chunk_width(n_cols, u, i):
            return S if i is not None else min(S, n_cols - u * S)

        def linear_pe(pe, c, name, n_cols, turn):
            v0 = READS[name]

            def body(u, i, _):
                width = chunk_width(n_cols, u, i)
                for h in range(2):
                    n = c.n + 2 * u + h
                    if u == 0:
                        pe.wait_ge(cols_lo, KC * TURNS.index(turn) + 4 * h + 4)
                    pe.wait_ge(lo_done, val(n + 1, 4, i))
                    wv = [w[n % 2][:, :].rearrange("p (k n) -> p k n", k=4)[:, :, 0:width] for w in (whi, wlo)]
                    for t in range(NT):
                        bank = ps[4 - 4 * (u % 2) + t][:, 0:width]
                        if h == 0 and u >= 2 and name in READS_OF:
                            pe.wait_ge(read_act if t % 2 == 0 else read_dve, val(2 * (v0 + u) - 3 + t // 2, 4, i))
                        for k in range(4):
                            ts = slice(t * P, (t + 1) * P)
                            ins = three(bank, (chi[:, 4 * h + k, ts], clo[:, 4 * h + k, ts]), (wv[0][:, k], wv[1][:, k]),
                                        h == 0 and k == 0, h == 1 and k == 3)
                        if h == 1:
                            ins.then_inc(product, 1)
                    if h == 0:
                        ins.then_inc(half_done, 1)

            chunks(pe, n_cols, body)
            end_linear(c, name, n_cols)

        def linear_evac(eng, c, name, n_cols, which):
            u0 = UNITS[name]

            def body(u, i, next_width):
                width = chunk_width(n_cols, u, i)
                split_chunk(low if which else high, eng, c, name, u, i, next_width, width)
                for t in range(which, NT, 2):
                    eng.wait_ge(product, val(NT * (u0 + u) + t + 1, 2 * NT, i))
                    dst, src = proj[:, t, bass.ds(val(u * S, 2 * S, i), width)], ps[4 - 4 * (u % 2) + t][:, 0:width]
                    if which == 0:
                        nc.scalar.copy(dst, src).then_inc(read_act, 1)
                    else:
                        nc.vector.tensor_copy(dst, src).then_inc(read_dve, 1)

            chunks(eng, n_cols, body)
            end_linear(c, name, n_cols)

        def linear_done(name, n_cols):
            n = 2 * (READS[name] + -(-n_cols // S))
            return [(read_act, n), (read_dve, n)]

        def wait_alone(eng, sem, value):
            eng.wait_ge(sem, value)
            eng.sem_inc(S_("passed"), 1)

        def wait_all(eng, pairs):
            for s, v in pairs:
                eng.wait_ge(s, v)

        def out_pe(pe, c, name):
            linear_pe(pe, c, name, D, name)

        def out_act(act, c, name):
            chunks(act, D, lambda u, i, nxt: split_chunk(high, act, c, name, u, i, nxt, S))
            end_linear(c, name, D)

        def out_dve(dve, c, name, per_tile, first=()):
            u0, n0 = UNITS[name], 2 * NT * OUTS.index(name)

            def body(u, i, nxt):
                split_chunk(low, dve, c, name, u, i, nxt, S)
                if u == 0:
                    wait_all(dve, first)
                for t in range(NT):
                    dve.wait_ge(product, NT * (u0 + u) + t + 1)
                    xs = x[:, t, u * S:(u + 1) * S]
                    nc.vector.tensor_tensor(xs, xs, ps[4 - 4 * u + t][:, :], ALU.add).then_inc(added, 1)
                    if u == 1:
                        dve.wait_ge(added, n0 + NT * u + t + 1)
                        per_tile(t)

            chunks(dve, D, body)
            end_linear(c, name, D)


        def turn_pe(pe, name, src, waits, norm=None):
            wait_all(pe, waits)
            if norm is not None:
                for t in range(NT):
                    pe.wait_ge(S_("scaled"), norm_count(norm, t + 1))
                    for k in range(4):
                        ins = nc.tensor.transpose(ps[4 + k][:, t * P:(t + 1) * P], src[:, t, k * P:(k + 1) * P], ident)
                        if t == NT - 1:
                            ins.then_inc(turned, 1)
            for k in range(0 if norm is None else 4, KC):
                for t in range(NT):
                    ins = nc.tensor.transpose(ps[(k + 4) % 8][:, t * P:(t + 1) * P], src[:, t, k * P:(k + 1) * P], ident)
                ins.then_inc(turned, 1)

        def turn_evac(eng, name, which, norm=None, midway=lambda: None):
            base = TURNS.index(name)

            def out_of_psum(k):
                eng.wait_ge(turned, KC * base + k + 1)
                g = colp[:, 0, norm, k:k + 1] if norm is not None else 1.0
                b = colp[:, 1, norm, k:k + 1] if norm is not None and norm < 4 else 0.0
                dst, src = cols[:, k, :], ps[(k + 4) % 8][:, :]
                if which == 0:
                    if norm is None:
                        ins = nc.scalar.copy(dst, src)
                    elif norm < 4:
                        ins = nc.scalar.activation(dst, src, ACT.Identity, bias=b, scale=g)
                    else:
                        ins = nc.scalar.activation(dst, src, ACT.Copy, scale=g)
                    ins.then_inc(cols_act, 1)
                else:
                    if norm is None:
                        ins = nc.vector.tensor_copy(dst, src)
                    elif norm < 4:
                        ins = nc.vector.tensor_scalar(dst, src, g, b, ALU.mult, ALU.add)
                    else:
                        ins = nc.vector.tensor_scalar(dst, src, g, None, ALU.mult)
                    ins.then_inc(cols_dve, 1)

            def parts(k):
                if which == 0:
                    eng.wait_ge(cols_act if k % 2 == 0 else cols_dve, 4 * base + k // 2 + 1)
                    nc.scalar.copy(chi[:, k, :], cols[:, k, :]).then_inc(cols_hi, 1)
                else:
                    eng.wait_ge(cols_hi, KC * base + k + 1)
                    nc.vector.tensor_tensor(clo[:, k, :], cols[:, k, :], chi[:, k, :].bitcast(F32), ALU.subtract)\
                        .then_inc(cols_lo, 1)

            for k in range(0, KC, 2):
                if k == 4:
                    midway()
                out_of_psum(k + which)
                if k >= 2:
                    parts(k - 2)
                    parts(k - 1)
            parts(KC - 2)
            parts(KC - 1)

        NORMS = [0, 1, 2, 3, 4, "conv", 5, 6, "sgu", 7, 8]

        def norm_count(n, tiles=NT):
            return NT * NORMS.index(n) + tiles

        def is_rms(n):
            return n in (4, 5, 6, 7, 8)

        def stats_dve(dve, ch, n, t, src=None, width=D):
            src = x[:, t, :] if src is None else src
            halves = width // 512
            for h in range(halves):
                ch.after(nc.vector.bn_stats(bst[:, t, h, :], src[:, h * 512:(h + 1) * 512]))
            ch.after(nc.vector.bn_aggr(mv[:, t, :], bst[:, t, 0:halves, :].rearrange("p a s -> p (a s)")))
            mean, var = mv[:, t, 0:1], mv[:, t, 1:2]
            if is_rms(n):
                ch.after(nc.vector.scalar_tensor_tensor(out=var, in0=mean, scalar=mean, in1=var, op0=ALU.mult, op1=ALU.add))
            else:
                ch.after(nc.vector.tensor_scalar(mean, mean, -1.0, None, ALU.mult))
            nc.vector.tensor_scalar(var, var, RMS_EPS if is_rms(n) else LN_EPS, None, ALU.add).then_inc(S_("stats"), 1)

        def rstd_pool(pool, n, t):
            pool.wait_ge(S_("stats"), norm_count(n, t + 1))
            nc.gpsimd.tensor_tensor(rstd[:, t:t + 1], mv[:, t, 1:2], cst("minus_half")[:, 0:1], ALU.pow)\
                .then_inc(S_("rstd"), 1)

        def scale_act(act, ch, n, t, dst, src):
            act.wait_ge(S_("rstd"), norm_count(n, t + 1))
            if not is_rms(n):
                ch.after(nc.scalar.activation(nmr[:, t:t + 1], mv[:, t, 0:1], ACT.Copy, scale=rstd[:, t:t + 1]))
                ins = nc.scalar.activation(dst, src, ACT.Identity, bias=nmr[:, t:t + 1], scale=rstd[:, t:t + 1])
            else:
                ins = nc.scalar.activation(dst, src, ACT.Copy, scale=rstd[:, t:t + 1])
            ins.then_inc(S_("scaled"), 1)

        def norm_pool(pool, ch, n):
            if n < 4:
                pool.wait_ge(S_("gain_rows"), 32 * n + 32)
                if n < 3:
                    ch.after(nc.gpsimd.tensor_scalar(rowp[:, :, :], rowp[:, :, :], ALPHA, None, ALU.mult))
            for t in range(NT):
                rstd_pool(pool, n, t)
            if n < 4:
                for t in range(NT) if n < 3 else (NT - 1,):
                    pool.wait_ge(S_("scaled"), norm_count(n, t + 1))
                    ch.after(nc.gpsimd.tensor_tensor(x[:, t, :], acc[:, t, :], rowp[:, 0, :], ALU.mult))
                    nc.gpsimd.tensor_tensor(x[:, t, :], x[:, t, :], rowp[:, 1, :], ALU.add)\
                        .then_inc(S_("x_rows"), 1)

        def norm34_dve(dve, ch):
            dve.wait_ge(S_("gain_rows"), 128)
            for t in range(NT):
                if t < NT - 1:
                    dve.wait_ge(S_("scaled"), norm_count(3, t + 1))
                    ch.after(nc.vector.tensor_tensor(x[:, t, :], acc[:, t, :], rowp[:, 0, :], ALU.mult))
                    ch.after(nc.vector.tensor_tensor(x[:, t, :], x[:, t, :], rowp[:, 1, :], ALU.add))
                else:
                    dve.wait_ge(S_("x_rows"), 3 * NT + 1)
                stats_dve(dve, ch, 4, t)

        def norm_act(act, ch, n):
            for t in range(NT):
                scale_act(act, ch, n, t, acc[:, t, :], x[:, t, :])

        def ff_index(c, e, what):
            return c.n + {"gate": 3 * e - 1 if e else 0, "up": 3 * e if e else 1}.get(what, 3 * e + 4)

        def ff_split(split, eng, c, name, n_exp, e, i, what):
            n = c.n + 3 * n_exp - 1 if (what, e) == ("down", n_exp - 1) else ff_index(c, e, what)
            if n - c.n < 2:
                used = c.last[n - c.n]
            elif what == "up":
                used = piece_used(name, e - 2, "down") if e >= 2 else piece_used(name, 0, "up")
            elif what == "gate":
                used = piece_used(name, e - 1, "up" if e > 1 else "gate")
            else:
                used = piece_used(name, e, "up") if e == n_exp - 1 else piece_used(name, e + 1, "gate")
            split(eng, n, 6, i, twice(used))

        def end_ff(c, name, n_exp):
            c.n += 3 * n_exp
            c.last = [piece_used(name, n_exp - 2, "down"), piece_used(name, n_exp - 1, "down")]

        def ff_pe(pe, c, name, n_exp, turn, router=lambda: None):
            e0 = PIECES[name]

            def up_or_gate(e, i, w):
                n = ff_index(c, e, "up" if w else "gate")
                pe.wait_ge(lo_done, val(n + 1, 6, i))
                wv = [q[n % 2][:, :].rearrange("p (k n) -> p k n", k=KC) for q in (whi, wlo)]
                for h in range(2):
                    if e:
                        pe.wait_ge(h_whole if w else silu, val(2 * (e0 + e) - 1 + h, 4, i))
                    hs = slice(h * P, (h + 1) * P)
                    for k in range(KC):
                        if e == 0 and w == 0 and h == 0:
                            pe.wait_ge(cols_lo, KC * TURNS.index(turn) + k + 1)
                        ins = three(ps[4 + 2 * h + w][:, :], (wv[0][:, k, hs], wv[1][:, k, hs]), (chi[:, k, :], clo[:, k, :]),
                                    k == 0, k == KC - 1)
                    ins.then_inc(up_ready if w else gate_ready, 1)

            def down(e, i):
                n = c.n + 3 * n_exp - 1 if i is None and e == n_exp - 1 else ff_index(c, e, "down")
                pe.wait_ge(lo_done, val(n + 1, 6, i))
                pe.wait_ge(h_low, val(2 * (e0 + e) + 2, 4, i))
                wv = [q[n % 2][:, :].rearrange("p (h n) -> p h n", h=2) for q in (whi, wlo)]
                for m in range(8):
                    t, half = m // 2, m % 2
                    if m >= 4 or e:
                        pe.wait_ge(y_added, val(8 * (e0 + e) + m - 3, 16, i))
                    ts, ns = slice(t * P, (t + 1) * P), slice(half * S, (half + 1) * S)
                    for h in range(2):
                        ins = three(ps[m % 4][:, :], (hhi[:, e % 2, h, ts], hlo[:, e % 2, h, ts]),
                                    (wv[0][:, h, ns], wv[1][:, h, ns]), h == 0, h == 1)
                    ins.then_inc(y_ready, 1)

            def body(e, i):
                up_or_gate(e, i, 0)
                if e == 0:
                    router()
                up_or_gate(e, i, 1)
                if e:
                    down(e - 1, i)

            pieces_of(pe, n_exp, body)
            down(n_exp - 1, None)
            end_ff(c, name, n_exp)

        def ff_act(act, c, name, n_exp, router=lambda: None):
            e0 = PIECES[name]

            def body(e, i):
                last = i is None and e == n_exp - 1
                ff_split(high, act, c, name, n_exp, e, i, "up")
                for h in range(2):
                    act.wait_ge(gate_ready, val(2 * (e0 + e) + h + 1, 4, i))
                    if e >= 2 and h == 0:
                        act.wait_ge(h_low, val(2 * (e0 + e) - 2, 4, i))
                    nc.scalar.activation(hbuf[e % 2][:, h, :], ps[4 + 2 * h][:, :], ACT.Silu).then_inc(silu, 1)
                if e == 0:
                    router()
                if e:
                    ff_split(high, act, c, name, n_exp, e - 1, i, "down")
                ff_split(high, act, c, name, n_exp, *((e, i, "down") if last else (e + 1, i, "gate")))
                for h in range(2):
                    act.wait_ge(h_whole, val(2 * (e0 + e) + h + 1, 4, i))
                    if e >= 2 and h == 0:
                        act.wait_ge(y_ready, val(8 * (e0 + e) - 8, 16, i))
                    nc.scalar.copy(hhi[:, e % 2, h, :], hbuf[e % 2][:, h, :]).then_inc(h_high, 1)

            pieces_of(act, n_exp, body)
            end_ff(c, name, n_exp)
            if name != "ffn1":
                high(act, c.n, 0, None, c.last[0])

        def ff_dve(dve, c, name, n_exp, weight, per_tile, waits, router=lambda: None):
            e0 = PIECES[name]

            def hidden(e, i):
                hidden_whole(e, i)
                hidden_low(e, i)

            def hidden_whole(e, i):
                for h in range(2):
                    dve.wait_ge(silu, val(2 * (e0 + e) + h + 1, 4, i))
                    dve.wait_ge(up_ready, val(2 * (e0 + e) + h + 1, 4, i))
                    nc.vector.tensor_tensor(hbuf[e % 2][:, h, :], hbuf[e % 2][:, h, :], ps[5 + 2 * h][:, :], ALU.mult)\
                        .then_inc(h_whole, 1)

            def hidden_low(e, i):
                for h in range(2):
                    dve.wait_ge(h_high, val(2 * (e0 + e) + h + 1, 4, i))
                    nc.vector.tensor_tensor(hlo[:, e % 2, h, :], hbuf[e % 2][:, h, :],
                                            hhi[:, e % 2, h, :].bitcast(F32), ALU.subtract).then_inc(h_low, 1)

            def add(e, i, last):
                for m in range(8):
                    t, half = m // 2, m % 2
                    dve.wait_ge(y_ready, val(8 * (e0 + e) + m + 1, 16, i))
                    xs = x[:, t, half * S:(half + 1) * S]
                    if m == 0 and e:
                        dve.wait_ge(y_added, val(8 * (e0 + e), 16, i))
                    w = weight(t, val(e, 2, i))
                    if w is None:
                        nc.vector.tensor_tensor(xs, xs, ps[m % 4][:, :], ALU.add).then_inc(y_added, 1)
                    else:
                        nc.vector.scalar_tensor_tensor(out=xs, in0=ps[m % 4][:, :], scalar=w, in1=xs,
                                                       op0=ALU.mult, op1=ALU.add).then_inc(y_added, 1)
                    if last and half == 1:
                        dve.wait_ge(y_added, 8 * (e0 + e) + m + 1)
                        per_tile(t)

            def body(e, i):
                last = i is None and e == n_exp - 1
                ff_split(low, dve, c, name, n_exp, e, i, "up")
                if e:
                    ff_split(low, dve, c, name, n_exp, e - 1, i, "down")
                if last:
                    hidden_whole(e, i)
                    ff_split(low, dve, c, name, n_exp, e, i, "down")
                    hidden_low(e, i)
                    add(e - 1, i, False)
                    return
                ff_split(low, dve, c, name, n_exp, e + 1, i, "gate")
                if e == 0:
                    router()
                if e == 1:
                    wait_all(dve, waits)
                if e:
                    add(e - 1, i, False)
                hidden(e, i)

            pieces_of(dve, n_exp, body)
            end_ff(c, name, n_exp)
            if name != "ffn1":
                low(dve, c.n, 0, None, c.last[0])
            add(n_exp - 1, None, True)

        wr = sb("wr", [P, KC, NE])
        br = sb("br", [P, NE])

        wrh = ctx.enter_context(nc.sbuf_tensor("wrh", [P, KC, NE], F32R))
        wrl = ctx.enter_context(nc.sbuf_tensor("wrl", [P, KC, NE], F32R))

        def router_pe(pe, layer, turn):
            pe.wait_ge(S_("small_low"), 1)
            pe.wait_ge(cols_lo, KC * TURNS.index(turn) + KC)
            for t in range(NT):
                for k in range(KC):
                    ts = slice(t * P, (t + 1) * P)
                    ins = three(ps[0][:, t * NE:(t + 1) * NE], (chi[:, k, ts], clo[:, k, ts]), (wrh[:, k, :], wrl[:, k, :]),
                                k == 0, k == KC - 1)
            ins.then_inc(S_("router_logits"), 1)

        rview = [rt[:, i * 64:(i + 1) * 64].rearrange("p (t e) -> p t e", t=NT) for i in range(6)]

        def router_act(act, layer):
            act.wait_ge(S_("router_logits"), layer + 1)
            nc.scalar.activation(rt[:, 0:64], ps[0][:, 0:64], ACT.Sigmoid).then_inc(S_("router_scores"), 1)

        def router_dve(dve, ch, layer):
            dve.wait_ge(S_("router_scores"), layer + 1)
            sc, biased, rank, cmp_, top, sel = rview
            V = nc.vector

            def grp(v):
                return v.rearrange("p t (g k) -> p (t g) k", k=4)

            def ranks(v, r, tmp, n):
                i4 = cst("index4").rearrange("p (o k) -> p o k", o=1).broadcast_to((P, n, 4))
                ch.after(V.tensor_copy(r, i4))
                for d in (1, 2, 3):
                    ch.after(V.tensor_tensor(tmp[:, :, 0:4 - d], v[:, :, d:4], v[:, :, 0:4 - d], ALU.is_gt))
                    ch.after(V.tensor_tensor(r[:, :, 0:4 - d], r[:, :, 0:4 - d], tmp[:, :, 0:4 - d], ALU.add))
                    ch.after(V.tensor_tensor(r[:, :, d:4], r[:, :, d:4], tmp[:, :, 0:4 - d], ALU.subtract))

            brow_ = br[:, :].rearrange("p (o e) -> p o e", o=1).broadcast_to((P, NT, NE))
            ch.after(V.tensor_tensor(biased, sc, brow_, ALU.add))
            ranks(grp(biased), grp(rank), grp(cmp_), NT * 4)
            ch.after(V.tensor_scalar(top, rank, 2.0, None, ALU.is_lt))
            ch.after(V.tensor_tensor(cmp_, top, biased, ALU.mult))
            g4 = gsc[:, 0:16].rearrange("p (t g) -> p t g", t=NT)
            gr = gsc[:, 16:32].rearrange("p (t g) -> p t g", t=NT)
            gt = gsc[:, 32:48].rearrange("p (t g) -> p t g", t=NT)
            ch.after(V.tensor_reduce(gsc[:, 0:16], grp(cmp_), AX, ALU.add))
            ranks(g4, gr, gt, NT)
            ch.after(V.tensor_scalar(gt, gr, 0.5, None, ALU.is_lt))
            gb = gsc[:, 32:48].rearrange("p (q o) -> p q o", o=1).broadcast_to((P, 16, 4))
            ch.after(V.tensor_tensor(grp(sel), grp(top), gb, ALU.mult))
            ch.after(V.tensor_tensor(sel, sel, sc, ALU.mult))
            ch.after(V.tensor_reduce(gsc[:, 48:52], sel, AX, ALU.add))
            ch.after(V.reciprocal(gsc[:, 52:56], gsc[:, 48:52]))
            rb = gsc[:, 52:56].rearrange("p (t o) -> p t o", o=1).broadcast_to((P, NT, NE))
            ch.after(V.tensor_tensor(gate, sel, rb, ALU.mult))

        w_up = more[0:GR, 3840:4352]
        zb = work[:, 0:2048].rearrange("p (t c) -> p t c", t=NT)
        g_sq, g_sk, g_sl, g_b, g_eb, g_enb, g_kd, g_p = (cols[:, i, :] for i in range(8))
        g_qd, g_ki = more[:, 0:512], more[:, 512:1024]
        g_sv = more[:, 1024:2048].rearrange("p (t c) -> p t c", t=NT)
        g_st = more[:, 2048:2048 + 7 * GDV].rearrange("p (c v) -> p c v", v=GDV)
        g_kdn = more[:, 3840:4352]
        g_sqr = more[:, 4352:4608]
        g_lowT = more[0:GR, 4608:5120]
        b_gate = more[:, 5120:5632]
        norm_g = more[:, 5632:5888]
        g_dec, g_ss, g_ms, g_rs = misc[:, 0:8], misc[:, 8:12], misc[:, 12:16], misc[:, 16:20]

        def by_tile(v):
            return v.rearrange("p (t c) -> p t c", t=NT)

        def half_bank(n):
            return (n % 2) * GDV, (n % 2 + 1) * GDV

        def kv_bank(c):
            lo, hi = half_bank(c // 2)
            return ps[2 * (c % 2) + c // 4][:, lo:hi]

        def gla_pe(pe):
            T = nc.tensor
            wait_all(pe, linear_done("gla_in", G_IN))
            for t in range(NT):
                ins = T.transpose(ps[4][0:GR, t * P:(t + 1) * P], proj[:, t, G_G:G_G + GR], ident)
            ins.then_inc(S_("g_low_turned"), 1)
            pe.wait_ge(S_("params"), PARAMS)
            pe.wait_ge(S_("g_low_cols"), 1)
            for t in range(NT):
                T.matmul(ps[t][:, :], g_lowT[:, t * P:(t + 1) * P], w_up, start=True, stop=True)\
                    .then_inc(S_("gate_logits"), 1)
            pe.sem_inc(S_("g_out"), 1)
            with pe.Fori(0, GH) as h:
                pe.wait_ge(S_("g_staged"), h + 1)
                for src, b in ((g_sq, 0), (g_sk, 1)):
                    for t in range(NT):
                        T.transpose(ps[b][:, t * P:(t + 1) * P], src[:, t * P:(t + 1) * P], ident)
                for t in range(NT):
                    ins = T.matmul(ps[2][:, t * P:(t + 1) * P], g_sl[:, t * P:(t + 1) * P], cst("gla_sum"),
                                   start=True, stop=True)
                ins.then_inc(S_("g_turned"), 1)
                pe.wait_ge(S_("g_qk_ready"), 2 * h + 2)
                for t in range(NT):
                    ins = T.matmul(ps[3][:, t * P:(t + 1) * P], g_ki[:, t * P:(t + 1) * P], g_qd[:, t * P:(t + 1) * P],
                                   start=True, stop=True)
                ins.then_inc(S_("g_scores"), 1)
                pe.wait_ge(S_("g_kd_ready"), h + 1)
                for t in range(NT):
                    ins = T.transpose(ps[4][:, t * P:(t + 1) * P], g_kd[:, t * P:(t + 1) * P], ident)
                ins.then_inc(S_("g_kd_turned"), 1)
                pe.wait_ge(S_("g_masked"), h + 1)
                pe.wait_ge(S_("g_kd_rows"), h + 1)
                pe.wait_ge(S_("g_values"), h + 1)
                for c in range(NCH - 1):
                    r0, t = (c % 2) * GC, c // 2
                    ins = T.matmul(kv_bank(c), g_kdn[r0:r0 + GC, t * P:(t + 1) * P], g_sv[r0:r0 + GC, t, :],
                                   start=True, stop=True)
                ins.then_inc(S_("g_kv"), 1)
                pe.wait_ge(S_("g_states"), h + 1)
                for t in range(NT):
                    lo, hi = half_bank(t)
                    o = ps[5 + t // 2]
                    T.matmul(o[:, lo:hi], g_p[:, t * P:(t + 1) * P], g_sv[:, t, :], start=True, stop=False,
                             skip_group_check=True)
                    for c in (2 * t, 2 * t + 1):
                        if c:
                            r0 = (c % 2) * GC
                            ins = T.matmul(o[r0:r0 + GC, lo:hi], g_qd[:, c * GC:(c + 1) * GC], g_st[:, c - 1, :],
                                           start=False, stop=True, skip_group_check=True)
                    ins.then_inc(S_("g_out"), 1)

        def gla_act(act, ch):
            A = nc.scalar
            act.wait_ge(S_("g_low_turned"), 1)
            A.copy(g_lowT, ps[4][0:GR, :]).then_inc(S_("g_low_cols"), 1)
            for t in range(NT):
                r = proj[:, t, G_R:G_R + D]
                A.activation(r, r, ACT.Silu).then_inc(S_("g_gate"), 1)
            act.wait_ge(S_("gate_z"), NT)
            ch.after(A.activation(work[:, 2048:4096], work[:, 0:2048], ACT.Abs))
            ch.after(A.activation(work[:, 2048:4096], work[:, 2048:4096], ACT.Exp, scale=-1.0))
            A.activation(work[:, 2048:4096], work[:, 2048:4096], ACT.Ln, bias=1.0).then_inc(S_("gate_log"), 1)

            def stage(h, copied):
                A.mul(by_tile(g_sq), proj[:, :, bass.ds(h * GDK + G_Q, GDK)], GDK ** -0.5).then_inc(S_("g_copied"), 1)
                A.copy(by_tile(g_sk), proj[:, :, bass.ds(h * GDK + G_K, GDK)]).then_inc(S_("g_copied"), 1)
                act.wait_ge(S_("g_copied"), copied)
                A.copy(by_tile(g_sl), zb[:, :, bass.ds(h * GDK, GDK)]).then_inc(S_("g_staged"), 1)

            act.wait_ge(S_("gate_decay"), 1)
            stage(0, 2)

            def head(h, last):
                A.copy(g_sv, proj[:, :, bass.ds(h * GDV + G_V, GDV)]).then_inc(S_("g_values"), 1)
                act.wait_ge(S_("g_bsum"), h + 1)
                A.activation(g_eb, g_b, ACT.Exp).then_inc(S_("g_exp"), 1)
                A.activation(g_enb, g_b, ACT.Exp, scale=-1.0).then_inc(S_("g_exp"), 1)
                A.activation(g_dec, g_b[:, GC - 1:S:GC], ACT.Exp).then_inc(S_("g_exp"), 1)
                act.wait_ge(S_("g_rest"), h + 1)
                A.activation(g_kd, g_kd, ACT.Exp).then_inc(S_("g_exp"), 1)
                act.wait_ge(S_("g_kd_turned"), h + 1)
                A.copy(g_kdn, ps[4][:, :]).then_inc(S_("g_kd_rows"), 1)
                if not last:
                    stage(h + 1, 2 * h + 4)
                for t in range(NT):
                    lo, hi = half_bank(t)
                    act.wait_ge(S_("g_out"), 4 * h + 2 * (t // 2) + 3)
                    ins = A.activation(g_sqr, ps[5 + t // 2][:, lo:hi], ACT.Square, accum_out=g_ss[:, t:t + 1])
                    ins.then_inc(S_("g_squares"), 1)
                    act.wait_ge(S_("g_squares"), 4 * h + t + 1)
                A.activation(g_ms, g_ss, ACT.Copy, scale=1.0 / GDV, bias=LN_EPS).then_inc(S_("g_mean_square"), 1)

            with act.Fori(0, GH - 1) as h:
                head(h, False)
            head(GH - 1, True)

        def gla_pool(pool):
            with pool.Fori(0, GH) as h:
                pool.wait_ge(S_("g_mean_square"), h + 1)
                nc.gpsimd.tensor_tensor(g_rs, g_ms, cst("minus_half"), ALU.pow).then_inc(S_("g_rstd"), 1)

        def gla_dve(dve, ch):
            V = nc.vector
            for t in range(NT):
                dve.wait_ge(S_("gate_logits"), t + 1)
                V.tensor_tensor(zb[:, t, :], ps[t][:, :], b_gate, ALU.add).then_inc(S_("gate_z"), 1)
            dve.wait_ge(S_("gate_log"), 1)
            V.scalar_tensor_tensor(out=work[:, 0:2048], in0=work[:, 0:2048], scalar=0.0, in1=work[:, 2048:4096],
                                   op0=ALU.min, op1=ALU.subtract).then_inc(S_("gate_decay"), 1)
            dve.wait_ge(S_("g_gate"), NT)
            ch.after(V.memset(g_p, 0.0))
            mask4 = cst("gla_mask").bitcast(U32).rearrange("p (o j) -> p o j", o=1).broadcast_to((P, NT, P))
            def begin(h):
                dve.wait_ge(S_("g_turned"), h + 1)
                V.tensor_copy(g_b, ps[2][:, :]).then_inc(S_("g_bsum"), 1)
                dve.wait_ge(S_("g_bsum"), h + 1)
                b3 = g_b.rearrange("p (c i) -> p c i", c=NCH)
                V.tensor_tensor(g_kd.rearrange("p (c i) -> p c i", c=NCH), b3[:, :, GC - 1:GC].broadcast_to((P, NCH, GC)),
                                b3, ALU.subtract).then_inc(S_("g_rest"), 1)
                dve.wait_ge(S_("g_exp"), 4 * h + 1)
                V.tensor_tensor(g_qd, ps[0][:, :], g_eb, ALU.mult).then_inc(S_("g_qk_ready"), 1)
                dve.wait_ge(S_("g_exp"), 4 * h + 2)
                V.tensor_tensor(g_ki, ps[1][:, :], g_enb, ALU.mult).then_inc(S_("g_qk_ready"), 1)
                dve.wait_ge(S_("g_exp"), 4 * h + 4)
                V.tensor_tensor(g_kd, g_kd, ps[1][:, :], ALU.mult).then_inc(S_("g_kd_ready"), 1)

            def masked(h):
                wait_alone(dve, S_("g_scores"), h + 1)
                V.copy_predicated(by_tile(g_p), mask4, by_tile(ps[3][:, :])).then_inc(S_("g_masked"), 1)

            def states(h):
                dve.wait_ge(S_("g_kv"), h + 1)
                for c in range(NCH - 1):
                    kv = kv_bank(c)
                    if c == 0:
                        ch.after(V.tensor_copy(g_st[:, 0, :], kv))
                        continue
                    ins = V.scalar_tensor_tensor(out=g_st[:, c, :], in0=g_st[:, c - 1, :], scalar=g_dec[:, c:c + 1],
                                                 in1=kv, op0=ALU.mult, op1=ALU.add)
                    if c < NCH - 2:
                        ch.after(ins)
                    else:
                        ins.then_inc(S_("g_states"), 1)

            def finish(h):
                dve.wait_ge(S_("g_rstd"), h + 1)
                for t in range(NT):
                    lo, hi = half_bank(t)
                    o = acc[:, t, bass.ds(h * GDV, GDV)]
                    ch.after(V.scalar_tensor_tensor(out=o, in0=ps[5 + t // 2][:, lo:hi], scalar=g_rs[:, t:t + 1],
                                                    in1=norm_g, op0=ALU.mult, op1=ALU.mult))
                for t in range(NT):
                    o = acc[:, t, bass.ds(h * GDV, GDV)]
                    ch.after(V.tensor_tensor(o, o, proj[:, t, bass.ds(h * GDV + G_R, GDV)], ALU.mult))

            dve.wait_ge(S_("params"), PARAMS)
            begin(0)
            masked(0)
            states(0)
            with dve.Fori(0, GH - 1) as i:
                ch.enter(i, 14)
                begin(i + 1)
                masked(i + 1)
                finish(i)
                states(i + 1)
            ch.leave(14, GH - 1)
            finish(GH - 1)

        def rope(dve, ch, src, heads, cos, sin, tiles, tmp):
            V = nc.vector
            v = src.rearrange("p t (h d) -> p t h d", d=HD)
            x1, x2 = v[:, :, :, 0:8], v[:, :, :, 8:16]
            n = tiles * heads * 8
            t4 = [tmp[:, i * 512:i * 512 + n].rearrange("p (t h d) -> p t h d", t=tiles, h=heads) for i in range(4)]
            cb = cos.rearrange("p (t o d) -> p t o d", t=tiles, o=1).broadcast_to((P, tiles, heads, 8))
            sb_ = sin.rearrange("p (t o d) -> p t o d", t=tiles, o=1).broadcast_to((P, tiles, heads, 8))
            V.tensor_tensor(t4[0], x1, cb, ALU.mult).then_inc(ch.sem, 1)
            V.tensor_tensor(t4[1], x2, sb_, ALU.mult).then_inc(ch.sem, 1)
            V.tensor_tensor(t4[2], x2, cb, ALU.mult).then_inc(ch.sem, 1)
            ch.n += 3
            ch.after(V.tensor_tensor(t4[3], x1, sb_, ALU.mult))
            ch.after(V.tensor_tensor(x1, t4[0], t4[1], ALU.subtract))
            ch.after(V.tensor_tensor(x2, t4[2], t4[3], ALU.add))

        t_qT = more[:, 0:2048].rearrange("p (j s) -> p j s", j=4)
        t_kT = more[:, 2048:3072].rearrange("p (j s) -> p j s", j=2)
        t_qs = more[:, 3072:4096].rearrange("p (t c) -> p t c", t=NT)
        t_ks = more[:, 4096:4608].rearrange("p (t c) -> p t c", t=NT)
        t_vs = cols[:, 4, :].rearrange("p (t c) -> p t c", t=NT)
        t_oT = [cols[0:HD, 5 + n, :] for n in range(2)]
        t_pT = [more[:, 4608 + 512 * i:5120 + 512 * i] for i in range(3)]
        t_p = [work[:, 512 * i:512 * i + 512] for i in range(3)]
        t_tmp = work[:, 1536:2048]
        t_l, t_nm = misc[:, 64:96], misc[:, 96:128]
        t_rl = misc[:, 128:136]
        t_sk, t_nsk, t_es = misc[:, 136:140], misc[:, 140:144], misc[:, 144:160]
        t_cl, t_cm, t_cw = misc[:, 160:176], misc[:, 176:192], misc[:, 192:208]
        c_p, c_pT = work[:, 2048:2560], work[:, 2560:3072]
        c_vblk, c_vrep, c_kT = work[:, 3072:3328], work[:, 3328:3584], work[0:HD, 3584:3712]
        c_w2 = proj[:, 0, N_IN:N_IN + 256].rearrange("p (w f d) -> p w f d", w=2, f=2)
        c_pe = misc[:, 32:48]
        c_hid, c_hT, c_row = work[:, 0:512], work[:, 512:768], work[:, 1024:1088]
        c_hTv = acc[:, 0, :].rearrange("p (f s) -> p f s", f=2)
        c_blk = [cols[:, 4 * n:4 * n + 4, :].rearrange("p a s -> p (a s)") for n in range(2)]
        sinks = misc[:, 208:216]

        class Attention:

            def __init__(self, name, turns, heads, k_slots, masks, values, q_of, k_of, band=False, sink=False,
                         cmp_=False):
                self.name, self.turns, self.heads, self.k_slots = name, turns, heads, k_slots
                self.values, self.q_of, self.k_of, self.sink, self.cmp = values, q_of, k_of, sink, cmp_
                kinds = 2 if cmp_ else 1
                self.kinds, self.per_head = kinds, kinds * NT
                self.units = []
                for j in range(heads):
                    for kind in range(kinds):
                        for t in range(NT):
                            k0 = max(0, t - 1) if band else 0
                            ks = kind if cmp_ else (j if k_slots == heads else 0)
                            at = (k0 - t + 1 if band else k0 - t + 3) * P
                            self.units.append((j, ks, t, k0, t + 1, masks[:, at:at + (t + 1 - k0) * P]))
                self.U = len(self.units)

            def sem(self, what):
                return S_(self.name + "_" + what)

            def last(self, j):
                return (j + 1) * self.per_head - 1

        Q_BANKS = (5, 6, 2, 0)

        def attn_pe(pe, c):
            T, U = nc.tensor, c.U
            with pe.Fori(0, c.turns) as i:
                wait_alone(pe, c.sem("staged"), i + 1)
                for j in range(c.k_slots):
                    for t in range(NT):
                        ins = T.transpose(ps[3 + j][0:HD, t * P:(t + 1) * P], t_ks[:, t, j * HD:(j + 1) * HD], ident)
                    ins.then_inc(c.sem("k_turned"), 1)
                for j in range(c.heads):
                    if c.cmp and j == 3:
                        wait_alone(pe, c.sem("cmp_done"), i + 1)
                    for t in range(NT):
                        ins = T.transpose(ps[Q_BANKS[j]][0:HD, t * P:(t + 1) * P], t_qs[:, t, j * HD:(j + 1) * HD], ident)
                    ins.then_inc(c.sem("q_turned"), 1)
                pe.wait_ge(c.sem("q_cols"), c.heads * i + c.heads)
                pe.wait_ge(c.sem("k_cols"), c.k_slots * i + c.k_slots)
                if c.cmp:
                    wait_alone(pe, c.sem("head"), c.heads * i + 1)
                    for t in range(NT):
                        for j in range(4):
                            at = (t * 4 + j) * NC
                            ins = T.matmul(ps[7][:, at:at + NC], t_qT[0:HD, j, t * P:(t + 1) * P],
                                           c_kT[:, bass.ds(i * NC, NC)], start=True, stop=True)
                    ins.then_inc(c.sem("cmp_scores"), 1)

                def scores(u):
                    j, ks, t, k0, k1, _ = c.units[u]
                    T.matmul(ps[u % 3][:, 0:(k1 - k0) * P], t_qT[0:HD, j, t * P:(t + 1) * P],
                             t_kT[0:HD, ks, k0 * P:k1 * P], start=True, stop=True).then_inc(c.sem("scores"), 1)

                def turn(u):
                    _, _, _, k0, k1, _ = c.units[u]
                    pe.wait_ge(c.sem("probs"), U * i + (u + 1))
                    for k in range(k1 - k0):
                        ins = T.transpose(ps[3 + u % 2][:, k * P:(k + 1) * P], t_p[u % 3][:, k * P:(k + 1) * P], ident)
                    ins.then_inc(c.sem("turned"), 1)

                def values(u):
                    j, ks, t, k0, k1, _ = c.units[u]
                    side = c.sem("keys_act" if u % 2 == 0 else "keys_dve")
                    wait_alone(pe, side, (U // 2) * i + (u // 2 + 1))
                    for k in range(k0, k1):
                        ins = T.matmul(ps[5 + u // NT % 2][0:HD, t * P:(t + 1) * P], t_vs[:, k, ks * HD:(ks + 1) * HD],
                                       t_pT[u % 3][:, (k - k0) * P:(k - k0 + 1) * P], start=(k == k0), stop=(k == k1 - 1))
                    ins.then_inc(c.sem("out"), 1)

                def back(n):
                    if n % c.kinds == 0:
                        wait_alone(pe, c.sem("head"), c.heads * i + (n // c.kinds + 1))
                    if c.cmp and n == 0:
                        wait_alone(pe, c.sem("cmp_shifted"), i + 1)
                    wait_alone(pe, c.sem("o_cols"), (U // NT) * i + (n + 1))
                    for t in range(NT):
                        at = ((n % c.kinds) * NT + t) * HD
                        ins = T.transpose(ps[7][:, at:at + HD], t_oT[n % 2][:, t * P:(t + 1) * P], ident[0:HD, 0:HD])
                    ins.then_inc(c.sem("o_rows"), 1)

                scores(0)
                scores(1)
                for u in range(U):
                    if u + 2 < U:
                        scores(u + 2)
                    turn(u)
                    if u:
                        values(u - 1)
                    if u >= NT + 2 and (u - 2) % NT == 0:
                        back((u - 2) // NT - 1)
                values(U - 1)
                back(U // NT - 1)
                if c.cmp:
                    pe.wait_ge(c.sem("cmp_probs"), i + 1)
                    for t in range(NT):
                        ins = T.transpose(ps[5][:, t * P:(t + 1) * P], c_p[:, t * P:(t + 1) * P], ident)
                    ins.then_inc(c.sem("cmp_turned"), 1)
                    pe.wait_ge(c.sem("cmp_keys"), i + 1)
                    for t in range(NT):
                        ins = T.matmul(ps[t // 2][:, (t % 2) * 256:(t % 2 + 1) * 256], c_pT[:, t * P:(t + 1) * P],
                                       c_vblk, start=True, stop=True)
                    ins.then_inc(c.sem("cmp_out"), 1)

        def attn_act(act, c, staged=lambda: None):
            A, U = nc.scalar, c.U
            n_k, n_v = len(c.k_of(0)), c.k_slots + (4 if c.cmp else 0)

            def stage(i, copied):
                for at, width, dst in c.k_of(i):
                    A.copy(t_ks[:, :, dst:dst + width], proj[:, :, bass.ds(at, width)]).then_inc(c.sem("copied"), 1)
                act.wait_ge(c.sem("copied"), copied)
                A.mul(t_qs[:, :, 0:c.heads * HD], proj[:, :, bass.ds(c.q_of(i), c.heads * HD)], HD ** -0.5)\
                    .then_inc(c.sem("staged"), 1)

            stage(0, n_k)
            staged()
            with act.Fori(0, c.turns) as i:
                for j in range(c.heads):
                    act.wait_ge(c.sem("q_turned"), c.heads * i + (j + 1))
                    A.copy(t_qT[0:HD, j, :], ps[Q_BANKS[j]][0:HD, :]).then_inc(c.sem("q_cols"), 1)
                if c.cmp:
                    act.wait_ge(c.sem("cmp_done"), i + 1)
                    for j in range(4):
                        A.copy(c_vblk[j * 32:(j + 1) * 32, j * HD:(j + 1) * HD],
                               c_vrep[j * 32:(j + 1) * 32, bass.ds(i * HD, HD)]).then_inc(c.sem("copied"), 1)
                act.wait_ge(c.sem("head"), c.heads * i + 1)
                for n in range(c.k_slots):
                    A.copy(t_vs[:, :, n * HD:(n + 1) * HD], proj[:, :, bass.ds(c.values(i, n), HD)])\
                        .then_inc(c.sem("copied"), 1)
                if c.sink:
                    A.copy(t_sk, sinks[:, bass.ds(i * 4, 4)]).then_inc(c.sem("sink"), 1)
                    A.mul(t_nsk, sinks[:, bass.ds(i * 4, 4)], -1.0).then_inc(c.sem("sink"), 1)
                if c.cmp:
                    act.wait_ge(c.sem("cmp_shifted"), i + 1)
                    A.activation(c_p, c_p, ACT.Exp).then_inc(c.sem("cmp_probs"), 1)

                def exps(u):
                    _, _, _, k0, k1, _ = c.units[u]
                    p = t_p[u % 3][:, 0:(k1 - k0) * P]
                    act.wait_ge(c.sem("masked"), U * i + (u + 1))
                    A.activation(p, p, ACT.Exp, bias=t_nm[:, u:u + 1], scale=-1.0, accum_out=t_l[:, u:u + 1])\
                        .then_inc(c.sem("probs"), 1)
                    if c.sink and u % c.per_head == c.per_head - 1:
                        j = u // c.per_head
                        act.wait_ge(c.sem("sink"), 2 * i + 2)
                        A.activation(t_es[:, 4 * j:4 * j + 4], t_nm[:, 4 * j:4 * j + 4], ACT.Exp, bias=t_sk[:, j:j + 1])\
                            .then_inc(c.sem("sink_exp"), 1)

                def result(n):
                    act.wait_ge(c.sem("out"), U * i + NT * (n + 1))
                    if n >= 2:
                        act.wait_ge(c.sem("o_rows"), (U // NT) * i + (n - 1))
                    A.copy(t_oT[n % 2], ps[5 + n % 2][0:HD, :]).then_inc(c.sem("o_cols"), 1)

                exps(0)
                for u in range(U):
                    if u + 1 < U:
                        exps(u + 1)
                    if u > NT and u % NT == 1:
                        result(u // NT - 1)
                    if u == 2:
                        act.wait_ge(c.sem("k_turned"), c.k_slots * i + c.k_slots)
                        stage(i + 1, (n_k + n_v) * (i + 1) + n_k)
                    if u % 2 == 0:
                        _, _, _, k0, k1, _ = c.units[u]
                        act.wait_ge(c.sem("turned"), U * i + (u + 1))
                        if u >= 3:
                            act.wait_ge(c.sem("out"), U * i + (u - 2))
                        A.copy(t_pT[u % 3][:, 0:(k1 - k0) * P], ps[3 + u % 2][:, 0:(k1 - k0) * P])\
                            .then_inc(c.sem("keys_act"), 1)
                result(U // NT - 1)
                if c.cmp:
                    act.wait_ge(c.sem("cmp_turned"), i + 1)
                    A.copy(c_pT, ps[5][:, :]).then_inc(c.sem("cmp_keys"), 1)

        def attn_dve(dve, ch, c):
            V, U = nc.vector, c.U
            per = c.heads * (3 if c.cmp else 2 if c.sink else 1) + (10 if c.cmp else 0)
            dve.sem_inc(c.sem("head"), 1)
            if c.cmp:
                dve.sem_inc(c.sem("cmp_done"), 1)
            with dve.Fori(0, c.turns) as i:
                ch.enter(i, per)
                for j in range(c.k_slots):
                    dve.wait_ge(c.sem("k_turned"), c.k_slots * i + (j + 1))
                    V.tensor_copy(t_kT[0:HD, j, :], ps[3 + j][0:HD, :]).then_inc(c.sem("k_cols"), 1)

                def masked(u):
                    _, _, _, k0, k1, mask = c.units[u]
                    if u == 0 and c.sink:
                        wait_alone(dve, c.sem("sink"), 2 * i + 2)
                    if u >= 3:
                        wait_alone(dve, c.sem("turned"), U * i + (u - 2))
                    wait_alone(dve, c.sem("scores"), U * i + (u + 1))
                    first = t_nsk[:, u // c.per_head:u // c.per_head + 1] if c.sink else BIG
                    V.tensor_tensor_reduce(out=t_p[u % 3][:, 0:(k1 - k0) * P], in0=ps[u % 3][:, 0:(k1 - k0) * P],
                                           in1=mask, scale=-1.0, scalar=first, op0=ALU.add, op1=ALU.min,
                                           accum_out=t_nm[:, u:u + 1]).then_inc(c.sem("masked"), 1)

                def head(j):
                    u0, n = j * c.per_head, c.per_head
                    dve.wait_ge(c.sem("o_rows"), (U // NT) * i + c.kinds * (j + 1))
                    o = ps[7][:, 0:n * HD].rearrange("p (u d) -> p u d", d=HD)
                    if c.sink:
                        dve.wait_ge(c.sem("sink_exp"), c.heads * i + (j + 1))
                        ch.after(V.tensor_tensor(t_l[:, u0:u0 + n], t_l[:, u0:u0 + n], t_es[:, 4 * j:4 * j + 4], ALU.add))
                    ch.after(V.reciprocal(t_rl[:, 0:n], t_l[:, u0:u0 + n]))
                    if c.cmp:
                        gates = proj[:, :, bass.ds(N_GT + 12 * i + 3 * j + 1, 2)].rearrange("p t k -> p k t")
                        ch.after(V.tensor_tensor(t_rl[:, 0:8].rearrange("p (k t) -> p k t", k=2),
                                                 t_rl[:, 0:8].rearrange("p (k t) -> p k t", k=2), gates, ALU.mult))
                    w = t_rl[:, 0:n].rearrange("p (u o) -> p u o", o=1).broadcast_to((P, n, HD))
                    hcol = acc[:, :, bass.ds((i * c.heads + j) * HD, HD)]
                    if c.cmp:
                        tmp = t_tmp.rearrange("p (u d) -> p u d", d=HD)
                        ch.after(V.tensor_tensor(tmp, o, w, ALU.mult))
                        V.tensor_tensor(hcol, tmp[:, 0:4, :], tmp[:, 4:8, :], ALU.add).then_inc(c.sem("head"), 1)
                    else:
                        V.tensor_tensor(hcol, o, w, ALU.mult).then_inc(c.sem("head"), 1)

                masked(0)
                masked(1)
                if c.cmp:
                    p3 = c_p.rearrange("p (q c) -> p q c", c=NC)
                    m4 = cst("cmp_mask", NT).rearrange("p t (o c) -> p t o c", o=1).broadcast_to((P, NT, 4, NC))
                    dve.wait_ge(c.sem("cmp_scores"), i + 1)
                    ch.after(V.tensor_tensor(c_p.rearrange("p (t j c) -> p t j c", t=NT, c=NC),
                                             ps[7][:, :].rearrange("p (t j c) -> p t j c", t=NT, c=NC), m4, ALU.add))
                    ch.after(V.tensor_reduce(t_cm, p3, AX, ALU.max))
                    V.tensor_tensor(p3, p3, t_cm.rearrange("p (q o) -> p q o", o=1).broadcast_to((P, 16, NC)),
                                    ALU.subtract).then_inc(c.sem("cmp_shifted"), 1)
                pending = []
                for u in range(U):
                    if u + 2 < U:
                        masked(u + 2)
                    if u % 2 == 1:
                        _, _, _, k0, k1, _ = c.units[u]
                        dve.wait_ge(c.sem("turned"), U * i + (u + 1))
                        if u >= 3:
                            dve.wait_ge(c.sem("out"), U * i + (u - 2))
                        V.tensor_copy(t_pT[u % 3][:, 0:(k1 - k0) * P], ps[3 + u % 2][:, 0:(k1 - k0) * P])\
                            .then_inc(c.sem("keys_dve"), 1)
                    for j in list(pending):
                        if u >= c.last(j) + 4:
                            head(j)
                            pending.remove(j)
                    if u % c.per_head == c.per_head - 1:
                        pending.append(u // c.per_head)
                for j in pending:
                    head(j)
                if c.cmp:
                    dve.wait_ge(c.sem("cmp_probs"), i + 1)
                    ch.after(V.tensor_reduce(t_cl, p3, AX, ALU.add))
                    ch.after(V.reciprocal(t_cw, t_cl))
                    cw = t_cw.rearrange("p (t j) -> p t j", t=NT)
                    gates = proj[:, :, bass.ds(N_GT + 12 * i, 12)].rearrange("p t (j w) -> p t j w", w=3)[:, :, :, 0]
                    ch.after(V.tensor_tensor(cw, cw, gates, ALU.mult))
                    ch.after(V.tensor_tensor(cw, cw, cst("cmp_any").rearrange("p (t o) -> p t o", o=1)
                                             .broadcast_to((P, NT, 4)), ALU.mult))
                    dve.wait_ge(c.sem("cmp_out"), i + 1)
                    dve.wait_ge(c.sem("head"), c.heads * i + (c.heads + 1))
                    for h in range(2):
                        wq = t_cw[:, 8 * h:8 * h + 8].rearrange("p (q o) -> p q o", o=1).broadcast_to((P, 8, HD))
                        ch.after(V.tensor_tensor(t_tmp.rearrange("p (q d) -> p q d", d=HD),
                                                 ps[h][:, :].rearrange("p (q d) -> p q d", d=HD), wq, ALU.mult))
                        o = acc[:, 2 * h:2 * h + 2, bass.ds(i * 256, 256)]
                        ch.after(V.tensor_tensor(o, o, t_tmp.rearrange("p (t d) -> p t d", t=2), ALU.add))
                    V.tensor_copy(misc[:, 216:217], t_cw[:, 0:1]).then_inc(c.sem("cmp_done"), 1)
            ch.leave(per, c.turns)

        nsa = Attention("nsa", NG, 4, 2, cst("causal"), lambda i, k: (N_VS if k == 0 else N_VW) + i * HD,
                        lambda i: i * 256, lambda i: [(N_KS + i * HD, HD, 0), (N_KW + i * HD, HD, HD)], cmp_=True)
        even = Attention("even", 2, 4, 1, cst("band"), lambda i, k: E_V + i * HD, lambda i: i * 256,
                         lambda i: [(E_K + i * HD, HD, 0)], band=True, sink=True)
        odd = Attention("odd", 4, 2, 2, cst("dilated"), lambda i, k: O_V + i * 128 + k * HD, lambda i: i * 128,
                        lambda i: [(O_K + i * 128, 128, 0)])

        def cmp_pe(pe, c):
            T = nc.tensor
            wait_all(pe, linear_done("nsa_in", N_IN))
            for w in range(2):
                pe.wait_ge(S_("cmp_twice"), 2 * w + 2)
                for g in range(NG):
                    for t in range(NT):
                        src = acc[:, t, (4 * w + g) * P:(4 * w + g + 1) * P]
                        ins = T.transpose(ps[4 * w + g][:, t * P:(t + 1) * P], src, ident)
                    ins.then_inc(S_("cmp_src"), 1)
            pe.wait_ge(S_("cmp_low"), 8)
            for w in range(2):
                for h in range(2):
                    pe.wait_ge(lo_done, c.n + 1)
                    wv = [q[c.n % 2][:, :].rearrange("p (m n) -> p m n", m=8) for q in (whi, wlo)]
                    for m in range(8):
                        k, at = 4 * w + 2 * h + m // 4, (m % 4) * P
                        ins = three(ps[w][:, 0:256], (chi[:, k, at:at + P], clo[:, k, at:at + P]), (wv[0][:, m], wv[1][:, m]),
                                    h == 0 and m == 0, h == 1 and m == 7)
                    ins.then_inc(S_("cmp_hidden"), 1)
                    c.n += 1
            pe.wait_ge(S_("cmp_silu"), 2)
            for n in range(4):
                ins = T.transpose(ps[2][:, n * P:(n + 1) * P], c_hid[:, n * P:(n + 1) * P], ident)
            ins.then_inc(S_("cmp_hid_turned"), 1)
            pe.wait_ge(S_("cmp_hid_cols"), 3)
            pe.wait_ge(S_("mixer_params"), NSA_PARAMS)
            for f in range(2):
                ins = T.matmul(ps[3][:, 0:HD], c_hT[:, f * P:(f + 1) * P], c_w2[:, 0, f, :], start=(f == 0), stop=(f == 1))
            ins.then_inc(S_("cmp_k"), 1)
            for g in range(NG):
                for f in range(2):
                    src = c_hTv[:, f, g * P:(g + 1) * P]
                    ins = T.matmul(ps[4][:, g * HD:(g + 1) * HD], src, c_w2[:, 1, f, :], start=(f == 0), stop=(f == 1))
            ins.then_inc(S_("cmp_v"), 1)
            pe.wait_ge(S_("cmp_k_turning"), 1)
            T.transpose(ps[5][0:HD, 0:P], c_row, ident).then_inc(S_("cmp_k_turned"), 1)
            pe.wait_ge(S_("cmp_k_cols"), 1)

        def end_cmp(c):
            c.n += 4
            c.last = [(S_("cmp_hidden"), 3, 0), (S_("cmp_hidden"), 4, 0)]

        def cmp_act(act, c):
            A = nc.scalar
            wait_all(act, linear_done("nsa_in", N_IN))
            act.wait_ge(S_("x_rows"), 2 * NT)
            for w, off in enumerate((N_KC, N_VC)):
                src = proj[:, :, off:off + 256].rearrange("p t (g d) -> p t g d", d=HD)
                dst = acc[:, :, w * 512:(w + 1) * 512].rearrange("p t (g h d) -> p t g h d", h=2, d=HD)
                for half in range(2):
                    A.copy(dst[:, :, :, half, :], src).then_inc(S_("cmp_twice"), 1)
            g = proj[:, :, N_GT:N_GT + 48]
            A.activation(g, g, ACT.Sigmoid).then_inc(S_("nsa_gates"), 1)
            high(act, c.n + 1, 0, None, c.last[1])
            for k in range(KC):
                act.wait_ge(S_("cmp_blocks"), k // 4 + 1)
                A.copy(chi[:, k, :], cols[:, k, :]).then_inc(S_("cmp_high"), 1)
            for n in (2, 3, 4):
                high(act, c.n + n, 0, None, (S_("cmp_hidden"), n - 1, 0))
            end_cmp(c)
            for w in range(2):
                act.wait_ge(S_("cmp_hidden"), 2 * w + 2)
                A.activation(c_hid[:, w * 256:(w + 1) * 256], ps[w][:, 0:256], ACT.Silu).then_inc(S_("cmp_silu"), 1)
            act.wait_ge(S_("cmp_hid_turned"), 1)
            A.copy(c_hT, ps[2][:, 0:256]).then_inc(S_("cmp_hid_cols"), 1)
            for f in range(2):
                A.copy(c_hTv[:, f, :].rearrange("p (g j c) -> p g j c", g=NG, j=4),
                       ps[2][:, (2 + f) * P:(3 + f) * P].rearrange("p (g o c) -> p g o c", g=NG, o=1)
                       .broadcast_to((P, NG, 4, NC))).then_inc(S_("cmp_hid_cols"), 1)
            act.wait_ge(S_("cmp_v"), 1)
            A.copy(c_vrep, ps[4][:, 0:256]).then_inc(S_("cmp_v_rows"), 1)
            act.wait_ge(S_("cmp_v_rows"), 1)
            act.wait_ge(S_("cmp_k_turned"), 1)
            A.copy(c_kT, ps[5][0:HD, 0:P]).then_inc(S_("cmp_k_cols"), 1)
            act.wait_ge(S_("mixer_ready"), 2)

        def cmp_dve(dve, ch, c):
            V = nc.vector
            dve.wait_ge(S_("mixer_params"), NSA_PARAMS)
            wait_all(dve, linear_done("nsa_in", N_IN))
            for w in range(2):
                ch.after(V.memset(c_blk[w], 0.0))
            for w in range(2):
                blk = c_blk[w].rearrange("p (m g c) -> p m g c", m=16, g=NG)
                for g in range(NG):
                    dve.wait_ge(S_("cmp_src"), 4 * w + g + 1)
                    for half in range(2):
                        rows = slice(half * HD, (half + 1) * HD)
                        for mh in range(2):
                            src = ps[4 * w + g][rows, :].rearrange("p (c r) -> p c r", r=CST)[:, mh:mh + NC - 1, half::2]
                            pe_ = c_pe[rows, mh * 8:mh * 8 + 8].rearrange("p (m o) -> p m o", o=1)\
                                .broadcast_to((HD, 8, NC - 1))
                            ins = V.tensor_tensor(blk[rows, mh * 8:mh * 8 + 8, g, 0:NC - 1],
                                                  src.rearrange("p c m -> p m c"), pe_, ALU.add)
                            if g < NG - 1 or half == 0 or mh == 0:
                                ch.after(ins)
                ins.then_inc(S_("cmp_blocks"), 1)
            low(dve, c.n + 1, 0, None, None)
            for k in range(KC):
                dve.wait_ge(S_("cmp_high"), k + 1)
                V.tensor_tensor(clo[:, k, :], cols[:, k, :], chi[:, k, :].bitcast(F32), ALU.subtract)\
                    .then_inc(S_("cmp_low"), 1)
            cos, sin = cst("cos"), cst("sin")
            rope(dve, ch, proj[:, :, 0:D], NH, cos, sin, NT, more)
            low(dve, c.n + 2, 0, None, None)
            rope(dve, ch, proj[:, :, N_KS:N_KS + 256], NG, cos, sin, NT, more)
            low(dve, c.n + 3, 0, None, None)
            low(dve, c.n + 4, 0, None, None)
            end_cmp(c)
            rope(dve, ch, proj[:, :, N_KW:N_KW + 256], NG, cos, sin, NT, more)
            dve.wait_ge(S_("cmp_k"), 1)
            ch.after(V.tensor_copy(c_row, ps[3][:, 0:HD]))
            rope(dve, ch, c_row.rearrange("p (t d) -> p t d", t=1), 1, cst("cmp_cos"), cst("cmp_sin"), 1, more)
            V.tensor_copy(misc[:, 217:218], c_row[:, 0:1]).then_inc(S_("cmp_k_turning"), 1)
            ch.after(V.memset(c_vblk, 0.0))
            V.memset(misc[:, 218:219], 0.0).then_inc(S_("mixer_ready"), 1)

        w_conv = misc[:, 220:348]
        conv_w = w_conv[:, 0:4 * TAPS].rearrange("p (c k) -> p c k", c=4)
        conv_b = w_conv[:, 4 * TAPS:4 * TAPS + 4]
        PAD = TAPS - 1
        cT = proj[:, :, E_IN:E_IN + PAD + S]
        conv_out = cols[:, 0:4, :]
        PE_CHUNKS, TAP_SLOTS = (2, 3), 8
        c_hi = nc.alloc_sbuf_tensor_at("conv_high", [P, 2, PAD + S], F32R, offset=work_at)
        c_lo = nc.alloc_sbuf_tensor_at("conv_low", [P, 2, PAD + S], F32R, offset=work_at + 8192)
        diag = nc.alloc_sbuf_tensor_at("tap_diagonals", [P, TAP_SLOTS, 2, P], F32R, offset=more_at + 16384)
        tap_hi = ctx.enter_context(nc.sbuf_tensor("tap_high", [P, 2, TAPS], F32R))
        tap_lo = sb("tap_low", [P, 2, TAPS])

        def even_pe(pe):
            T = nc.tensor
            pe.wait_ge(S_("even_glu"), 1)
            for k in range(4):
                for t in range(NT):
                    ins = T.transpose(ps[k][:, t * P:(t + 1) * P], proj[:, t, E_GA + k * P:E_GA + (k + 1) * P], ident)
                ins.then_inc(S_("glu_turned"), 1)
            pe.wait_ge(S_("small_low"), 3)
            for k in range(2):
                for n in range(TAPS):
                    g = TAPS * k + n
                    pe.wait_ge(S_("taps_ready"), 2 * g + 2)
                    d = diag[:, g % TAP_SLOTS]
                    three(ps[4 + k][:, :], (d[:, 0], d[:, 1]), (c_hi[:, k, n:n + S], c_lo[:, k, n:n + S]),
                          n == 0, n == TAPS - 1).then_inc(S_("taps_used"), 1)

        def even_conv_back_pe(pe):
            T = nc.tensor
            pe.wait_ge(S_("conv_done"), 4)
            for t in range(NT):
                for k in range(4):
                    ins = T.transpose(ps[t][:, k * P:(k + 1) * P], conv_out[:, k, t * P:(t + 1) * P], ident)
                ins.then_inc(S_("conv_turned"), 1)

        def even_act(act):
            A = nc.scalar
            wait_all(act, linear_done("even_in", E_IN))
            A.activation(proj[:, :, E_GB:E_GB + W2], proj[:, :, E_GB:E_GB + W2], ACT.Sigmoid)\
                .then_inc(S_("even_sigmoid"), 1)
            for k in range(4):
                act.wait_ge(S_("glu_turned"), k + 1)
                A.copy(cT[:, k, PAD:PAD + S], ps[k][:, :]).then_inc(S_("glu_cols"), 1)
            act.wait_ge(S_("mixer_params"), EVEN_PARAMS)
            A.copy(tap_hi[:, :, :], conv_w[:, 2:4, :]).then_inc(S_("small_high"), 1)
            act.wait_ge(S_("glu_cols"), 4)
            A.copy(c_hi[:, :, :], cT[:, 2:4, :]).then_inc(S_("small_high"), 1)
            act.wait_ge(S_("small_low"), 2)
            for k in range(2):
                for n in range(TAPS):
                    g = TAPS * k + n
                    if g >= TAP_SLOTS:
                        act.wait_ge(S_("taps_used"), g - TAP_SLOTS + 1)
                    d = diag[:, g % TAP_SLOTS]
                    A.mul(d[:, 0], ident, conv_w[:, 2 + k, n:n + 1]).then_inc(S_("taps_ready"), 1)
                    A.mul(d[:, 1], ident, tap_lo[:, k, n:n + 1]).then_inc(S_("taps_ready"), 1)
            for k in range(2):
                act.wait_ge(S_("taps_used"), TAPS * (k + 1))
                A.activation(conv_out[:, 2 + k, :], ps[4 + k][:, :], ACT.Identity, bias=conv_b[:, 2 + k:3 + k])\
                    .then_inc(S_("conv_done"), 1)

        def even_dve(dve, ch):
            V = nc.vector
            wait_all(dve, linear_done("even_in", E_IN))
            ch.after(V.memset(cT[:, :, 0:PAD], 0.0))
            dve.wait_ge(S_("even_sigmoid"), 1)
            V.tensor_tensor(proj[:, :, E_GA:E_GA + W2], proj[:, :, E_GA:E_GA + W2], proj[:, :, E_GB:E_GB + W2], ALU.mult)\
                .then_inc(S_("even_glu"), 1)
            dve.wait_ge(S_("small_high"), 2)
            V.tensor_tensor(tap_lo[:, :, :], conv_w[:, 2:4, :], tap_hi[:, :, :].bitcast(F32), ALU.subtract)\
                .then_inc(S_("small_low"), 1)
            dve.wait_ge(S_("small_high"), 3)
            V.tensor_tensor(c_lo[:, :, :], cT[:, 2:4, :], c_hi[:, :, :].bitcast(F32), ALU.subtract)\
                .then_inc(S_("small_low"), 1)
            rope(dve, ch, proj[:, :, 0:640], 10, cst("cos"), cst("sin"), NT, more)
            dve.wait_ge(S_("mixer_params"), EVEN_PARAMS)
            for k in range(2):
                dve.wait_ge(S_("glu_cols"), k + 1)
                o = conv_out[:, k, :]
                ch.after(V.tensor_scalar(o, cT[:, k, 0:S], conv_w[:, k, 0:1], conv_b[:, k:k + 1], ALU.mult, ALU.add))
                for n in range(1, TAPS):
                    ins = V.scalar_tensor_tensor(out=o, in0=cT[:, k, n:n + S], scalar=conv_w[:, k, n:n + 1], in1=o,
                                                 op0=ALU.mult, op1=ALU.add)
                    if n < TAPS - 1:
                        ch.after(ins)
                    else:
                        ins.then_inc(S_("conv_done"), 1)
            V.memset(misc[:, 218:219], 0.0).then_inc(S_("mixer_ready"), 1)

        def norm512_act(act, ch, tag, src, dst):
            for t in range(NT):
                scale_act(act, ch, tag, t, dst(t), src(t))

        def norm512_pool(pool, ch, tag, dst):
            for t in range(NT):
                rstd_pool(pool, tag, t)
            for t in range(NT):
                pool.wait_ge(S_("scaled"), norm_count(tag, t + 1))
                ch.after(nc.gpsimd.tensor_tensor(dst(t), dst(t), rowp[:, 0, 0:W2], ALU.mult))
                nc.gpsimd.tensor_tensor(dst(t), dst(t), rowp[:, 1, 0:W2], ALU.add).then_inc(S_("biased"), 1)

        def conv_dst(t):
            return acc[:, t, W2:D]

        spat = proj[:, :, O_IN:O_IN + 256].rearrange("p a (b s) -> p a b s", b=2)
        spatT = cols[:, 0:2, :].rearrange("p a s -> p (a s)")
        spat_b = misc[:, 220:228]

        def sgu_dst(t):
            return proj[:, t, O_G:O_G + W2]

        def odd_pe(pe):
            T = nc.tensor
            wait_all(pe, linear_done("odd_in", O_IN))
            pe.wait_ge(S_("mixer_params"), ODD_PARAMS)
            for g in range(8):
                ins = T.transpose(ps[g // 4][:, (g % 4) * P:(g % 4 + 1) * P], spat[:, g // 2, g % 2, :], ident)
            ins.then_inc(S_("spatial_turned"), 1)
            pe.wait_ge(S_("spatial_cols"), 2)

        MIX_BANKS = (0, 1, 2, 5)

        def odd_mix_pe(pe):
            T = nc.tensor
            pe.wait_ge(S_("biased"), 2 * NT)
            for g in range(8):
                T.matmul(ps[MIX_BANKS[g // 2]][:, (g % 2) * 256:(g % 2 + 1) * 256], spatT[:, g * P:(g + 1) * P],
                         proj[:, :, O_G + g * HD:O_G + (g + 1) * HD], start=True, stop=True).then_inc(S_("mixed"), 1)

        def odd_act(act, ch):
            A = nc.scalar
            wait_all(act, linear_done("odd_in", O_IN))
            for t in range(NT):
                z = proj[:, t, O_G:O_G + W2]
                A.activation(z, z, ACT.Gelu_apprx_tanh).then_inc(S_("gelu"), 1)
            z = proj[:, :, O_U:O_U + W2]
            A.activation(z, z, ACT.Gelu_apprx_tanh).then_inc(S_("gelu"), 1)

        def odd_dve(dve, ch):
            V = nc.vector
            wait_all(dve, linear_done("odd_in", O_IN))
            rope(dve, ch, proj[:, :, 0:D], 16, cst("cos"), cst("sin"), NT, more)
            dve.wait_ge(S_("spatial_turned"), 1)
            up = cst("upper").rearrange("p (o t) -> p o t", o=1).broadcast_to((P, 4, P))
            for h in range(2):
                V.tensor_tensor(spatT[:, h * 512:(h + 1) * 512].rearrange("p (g t) -> p g t", g=4),
                                ps[h][:, :].rearrange("p (g t) -> p g t", g=4), up, ALU.mult)\
                    .then_inc(S_("spatial_cols"), 1)
            V.memset(misc[:, 218:219], 0.0).then_inc(S_("mixer_ready"), 1)
            for t in range(NT):
                dve.wait_ge(S_("gelu"), t + 1)
                stats_dve(dve, ch, "sgu", t, sgu_dst(t), W2)

        def odd_gate_dve(dve):
            V = nc.vector
            dve.wait_ge(S_("gelu"), NT + 1)
            for g in range(8):
                dve.wait_ge(S_("mixed"), g + 1 if g % 2 else g + 2)
                V.scalar_tensor_tensor(out=acc[:, :, W2 + g * HD:W2 + (g + 1) * HD],
                                       in0=ps[MIX_BANKS[g // 2]][:, (g % 2) * 256:(g % 2 + 1) * 256]
                                       .rearrange("p (t d) -> p t d", t=NT),
                                       scalar=spat_b[:, g:g + 1], in1=proj[:, :, O_U + g * HD:O_U + (g + 1) * HD],
                                       op0=ALU.add, op1=ALU.mult).then_inc(S_("gated"), 1)

        ctx.enter_context(nc.allow_non_contiguous_dma(reason="a few small tables are read by columns"))
        block = ctx.enter_context(nc.Block())
        ffn_gate = lambda t, e: None
        moe_gate = lambda t, e: gate[:, t, bass.ds(e, 1)]

        @block.sync
        def _(sp):
            c = Count()
            sp.dma_start(ident, a["consts"][:, 0:P]).then_inc(S_("x_landed"), 16)
            sp.dma_start(x[:, :, :], a["x"][0].rearrange("(t p) d -> p t d", p=P)).then_inc(S_("x_landed"), 16)

            def params():
                sp.dma_start(con[:, P:CONST_W], a["consts"][:, P:CONST_W]).then_inc(S_("params"), 16)
                sp.dma_start(w_up, a["gla_w_gate_up"][0]).then_inc(S_("params"), 16)
                sp.dma_start(b_gate, bcast(a["gla_b_gate"][0], GH * GDK)).then_inc(S_("params"), 16)
                sp.dma_start(norm_g, bcast(a["gla_norm_g"][0], GDV)).then_inc(S_("params"), 16)
                sp.dma_start(wr[:, :, :], a["moe_w_router"].rearrange("(k p) e -> p k e", p=P)).then_inc(S_("params"), 16)
                sp.dma_start(br[:, :], bcast(a["moe_b_router"], NE)).then_inc(S_("params"), 16)
                sp.dma_start(colp[:, 0, 0:4, :], a["ln_g"].rearrange("l i (k p) -> p (l i) k", p=P)).then_inc(S_("params"), 16)
                sp.dma_start(colp[:, 1, 0:4, :], a["ln_b"].rearrange("l i (k p) -> p (l i) k", p=P)).then_inc(S_("params"), 16)
                for n in range(4, 9):
                    sp.dma_start(colp[:, 0, n, :], norm_rows(n)[0].rearrange("(k p) -> p k", p=P)).then_inc(S_("params"), 16)

            load_linear(sp, c, "gla_in", a["gla_w_in"][0], G_IN, params)
            load_linear(sp, c, "gla_out", a["gla_w_out"][0], D)
            load_ff(sp, c, "moe0", moe_views(0), NE)
            load_linear(sp, c, "nsa_in", a["nsa_w_in"][0], N_IN)
            load_cmp(sp, c)
            load_linear(sp, c, "nsa_out", a["nsa_w_out"][0], D)
            load_ff(sp, c, "moe1", moe_views(1), NE)
            load_linear(sp, c, "even_in", a["ev_w_in_2"][0], E_IN)
            load_linear(sp, c, "even_out", a["ev_w_out_2"][0], D)
            load_ff(sp, c, "ffn0", ffn_views(0), DFF // FF)
            load_linear(sp, c, "odd_in", a["od_w_in_2"][0], O_IN)
            load_linear(sp, c, "odd_out", a["od_w_out_2"][0], D)
            load_ff(sp, c, "ffn1", ffn_views(1), DFF // FF)
            for t in range(NT):
                sp.wait_ge(S_("result_pool") if t < 2 else S_("result_dve"), t % 2 + 1)
                sp.dma_start(out[0, t * P:(t + 1) * P, :], acc[:, t, :]).then_inc(S_("stored"), 16)
            sp.wait_ge(S_("stored"), 16 * NT)

        @block.tensor
        def _(pe):
            c = Count()
            turn_pe(pe, "in", x, [(S_("x_landed"), 32)])
            linear_pe(pe, c, "gla_in", G_IN, "in")
            gla_pe(pe)
            turn_pe(pe, "gla_out", acc, [(S_("mixer_ready"), 1)])
            out_pe(pe, c, "gla_out")
            turn_pe(pe, "n0", acc, [], 0)
            ff_pe(pe, c, "moe0", NE, "n0", lambda: router_pe(pe, 0, "n0"))
            turn_pe(pe, "n1", acc, [], 1)
            linear_pe(pe, c, "nsa_in", N_IN, "n1")
            cmp_pe(pe, c)
            attn_pe(pe, nsa)
            turn_pe(pe, "nsa_out", acc, [(nsa.sem("cmp_done"), NG + 1), (nsa.sem("head"), NH + 1)])
            out_pe(pe, c, "nsa_out")
            turn_pe(pe, "n2", acc, [], 2)
            ff_pe(pe, c, "moe1", NE, "n2", lambda: router_pe(pe, 1, "n2"))
            turn_pe(pe, "n4", acc, [], 4)
            linear_pe(pe, c, "even_in", E_IN, "n4")
            even_pe(pe)
            even_conv_back_pe(pe)
            pe.wait_ge(S_("scaled"), norm_count("conv"))
            attn_pe(pe, even)
            turn_pe(pe, "even_out", acc, [(S_("doneconv"), NT), (even.sem("head"), 8 + 1)])
            out_pe(pe, c, "even_out")
            turn_pe(pe, "n5", acc, [], 5)
            ff_pe(pe, c, "ffn0", DFF // FF, "n5")
            turn_pe(pe, "n6", acc, [], 6)
            linear_pe(pe, c, "odd_in", O_IN, "n6")
            odd_pe(pe)
            attn_pe(pe, odd)
            odd_mix_pe(pe)
            turn_pe(pe, "odd_out", acc, [(S_("gated"), 8), (odd.sem("head"), 8 + 1)])
            out_pe(pe, c, "odd_out")
            turn_pe(pe, "n7", acc, [], 7)
            ff_pe(pe, c, "ffn1", DFF // FF, "n7")

        @block.scalar
        def _(act):
            ch = Chain(act, S_("act"))
            c = Count()
            turn_evac(act, "in", 0, midway=lambda: high(act, 0, 0, None, None))
            linear_evac(act, c, "gla_in", G_IN, 0)
            gla_act(act, ch)
            turn_evac(act, "gla_out", 0)
            out_act(act, c, "gla_out")
            act.wait_ge(S_("params"), PARAMS)
            nc.scalar.copy(wrh[:, :, :], wr[:, :, :]).then_inc(S_("small_high"), 1)
            norm_act(act, ch, 0)
            turn_evac(act, "n0", 0, 0)
            ff_act(act, c, "moe0", NE, lambda: router_act(act, 0))
            norm_act(act, ch, 1)
            turn_evac(act, "n1", 0, 1)
            linear_evac(act, c, "nsa_in", N_IN, 0)
            cmp_act(act, c)
            attn_act(act, nsa)
            turn_evac(act, "nsa_out", 0)
            out_act(act, c, "nsa_out")
            norm_act(act, ch, 2)
            turn_evac(act, "n2", 0, 2)
            ff_act(act, c, "moe1", NE, lambda: router_act(act, 1))
            norm_act(act, ch, 3)
            norm_act(act, ch, 4)
            turn_evac(act, "n4", 0, 4)
            linear_evac(act, c, "even_in", E_IN, 0)
            even_act(act)
            act.wait_ge(S_("mixer_ready"), 3)
            attn_act(act, even, lambda: norm512_act(act, ch, "conv", lambda t: ps[t][:, :], conv_dst))
            for t in range(NT):
                act.wait_ge(S_("biased"), t + 1)
                nc.scalar.activation(conv_dst(t), conv_dst(t), ACT.Silu).then_inc(S_("doneconv"), 1)
            turn_evac(act, "even_out", 0)
            out_act(act, c, "even_out")
            norm_act(act, ch, 5)
            turn_evac(act, "n5", 0, 5)
            ff_act(act, c, "ffn0", DFF // FF)
            norm_act(act, ch, 6)
            turn_evac(act, "n6", 0, 6)
            linear_evac(act, c, "odd_in", O_IN, 0)
            odd_act(act, ch)
            act.wait_ge(S_("mixer_ready"), 4)
            attn_act(act, odd, lambda: norm512_act(act, ch, "sgu", sgu_dst, sgu_dst))
            turn_evac(act, "odd_out", 0)
            out_act(act, c, "odd_out")
            norm_act(act, ch, 7)
            turn_evac(act, "n7", 0, 7)
            ff_act(act, c, "ffn1", DFF // FF)
            norm_act(act, ch, 8)

        @block.gpsimd
        def _(pool):
            ch = Chain(pool, S_("pool"))

            def load_rows(n):
                for i in range(2):
                    pool.dma_start(rowp[:, i, :], bcast(norm_rows(n)[i], D)).then_inc(S_("gain_rows"), 16)

            load_rows(0)
            pool.wait_ge(turned, KC)
            nc.gpsimd.tensor_scalar(x[:, :, :], x[:, :, :], ALPHA, None, ALU.mult).then_inc(S_("x_scaled"), 1)
            gla_pool(pool)
            norm_pool(pool, ch, 0)
            pool.wait_ge(S_("x_rows"), 1 * NT)
            load_rows(1)
            for w, name in enumerate(("nsa_w_cmp_k2", "nsa_w_cmp_v2")):
                pool.dma_start(c_w2[:, w, :, :], a[name][0].rearrange("(f p) d -> p f d", p=P)).then_inc(S_("mixer_params"), 16)
            for half in range(2):
                pool.dma_start(c_pe[half * HD:(half + 1) * HD, :], a["nsa_cmp_pe"][0]
                               .rearrange("(m h) d -> h d m", h=2)[half]).then_inc(S_("mixer_params"), 16)
            norm_pool(pool, ch, 1)
            pool.wait_ge(S_("x_rows"), 2 * NT)
            load_rows(2)
            norm_pool(pool, ch, 2)
            pool.wait_ge(S_("x_rows"), 3 * NT)
            load_rows(3)
            norm_pool(pool, ch, 3)
            norm_pool(pool, ch, 4)
            pool.dma_start(rowp[:, 0, 0:W2], bcast(a["ev_conv_ln_g_2"][0], W2)).then_inc(S_("mixer_params"), 16)
            pool.dma_start(rowp[:, 1, 0:W2], bcast(a["ev_conv_ln_b_2"][0], W2)).then_inc(S_("mixer_params"), 16)
            pool.dma_start(sinks, bcast(a["ev_sinks_2"][0], 8)).then_inc(S_("mixer_params"), 16)
            for k in range(4):
                pool.dma_start(conv_w[:, k, :], a["ev_conv_w_2"][0][:, k * P:(k + 1) * P].rearrange("n p -> p n"))\
                    .then_inc(S_("mixer_params"), 16)
            pool.dma_start(conv_b, a["ev_conv_b_2"][0].rearrange("(k p) -> p k", p=P)).then_inc(S_("mixer_params"), 16)
            norm512_pool(pool, ch, "conv", conv_dst)
            norm_pool(pool, ch, 5)
            pool.wait_ge(S_("biased"), NT)
            pool.wait_ge(S_("stats"), norm_count(5))
            pool.dma_start(rowp[:, 0, 0:W2], bcast(a["od_sgu_ln_g_2"][0], W2)).then_inc(S_("mixer_params"), 16)
            pool.dma_start(rowp[:, 1, 0:W2], bcast(a["od_sgu_ln_b_2"][0], W2)).then_inc(S_("mixer_params"), 16)
            pool.dma_start(spat_b, a["od_spatial_b_2"][0].rearrange("g t -> t g")).then_inc(S_("mixer_params"), 16)
            for n in range(4):
                pool.dma_start(spat[:, n, :, :], a["od_spatial_w_2"][0, 2 * n:2 * n + 2].rearrange("g t s -> t g s"))\
                    .then_inc(S_("mixer_params"), 16)
            norm_pool(pool, ch, 6)
            pool.wait_ge(S_("mixer_params"), ODD_PARAMS)
            norm512_pool(pool, ch, "sgu", sgu_dst)
            norm_pool(pool, ch, 7)
            pool.wait_ge(S_("biased"), 2 * NT)
            pool.dma_start(rowp[:, 0, :], bcast(norm_rows(8)[0], D)).then_inc(S_("mixer_params"), 16)
            norm_pool(pool, ch, 8)
            pool.wait_ge(S_("mixer_params"), FINAL_PARAMS)
            for t in (0, 1):
                pool.wait_ge(S_("scaled"), norm_count(8, t + 1))
                nc.gpsimd.tensor_tensor(acc[:, t, :], acc[:, t, :], rowp[:, 0, :], ALU.mult).then_inc(S_("result_pool"), 1)

        @block.vector
        def _(dve):
            ch = Chain(dve, S_("dve"))
            c = Count()

            def stats(n):
                return lambda t: stats_dve(dve, ch, n, t)

            turn_evac(dve, "in", 1, midway=lambda: low(dve, 0, 0, None, None))
            linear_evac(dve, c, "gla_in", G_IN, 1)
            dve.wait_ge(S_("params"), PARAMS)
            gla_dve(dve, ch)
            nc.vector.memset(misc[:, 218:219], 0.0).then_inc(S_("mixer_ready"), 1)
            turn_evac(dve, "gla_out", 1)
            out_dve(dve, c, "gla_out", stats(0), [(S_("x_scaled"), 1)])
            dve.wait_ge(S_("small_high"), 1)
            nc.vector.tensor_tensor(wrl[:, :, :], wr[:, :, :], wrh[:, :, :].bitcast(F32), ALU.subtract)\
                .then_inc(S_("small_low"), 1)
            turn_evac(dve, "n0", 1, 0)
            ff_dve(dve, c, "moe0", NE, moe_gate, stats(1), [(S_("x_rows"), 1 * NT)],
                   lambda: router_dve(dve, ch, 0))
            turn_evac(dve, "n1", 1, 1)
            linear_evac(dve, c, "nsa_in", N_IN, 1)
            cmp_dve(dve, ch, c)
            dve.wait_ge(S_("nsa_gates"), 1)
            attn_dve(dve, ch, nsa)
            turn_evac(dve, "nsa_out", 1)
            out_dve(dve, c, "nsa_out", stats(2), [(S_("x_rows"), 2 * NT)])
            turn_evac(dve, "n2", 1, 2)
            ff_dve(dve, c, "moe1", NE, moe_gate, stats(3), [(S_("x_rows"), 3 * NT)],
                   lambda: router_dve(dve, ch, 1))
            norm34_dve(dve, ch)
            turn_evac(dve, "n4", 1, 4)
            linear_evac(dve, c, "even_in", E_IN, 1)
            even_dve(dve, ch)
            for t in range(NT):
                dve.wait_ge(S_("conv_turned"), t + 1)
                stats_dve(dve, ch, "conv", t, ps[t][:, :], W2)
            attn_dve(dve, ch, even)
            turn_evac(dve, "even_out", 1)
            out_dve(dve, c, "even_out", stats(5))
            turn_evac(dve, "n5", 1, 5)
            ff_dve(dve, c, "ffn0", DFF // FF, ffn_gate, stats(6), [])
            turn_evac(dve, "n6", 1, 6)
            linear_evac(dve, c, "odd_in", O_IN, 1)
            odd_dve(dve, ch)
            attn_dve(dve, ch, odd)
            odd_gate_dve(dve)
            turn_evac(dve, "odd_out", 1)
            out_dve(dve, c, "odd_out", stats(7))
            turn_evac(dve, "n7", 1, 7)
            ff_dve(dve, c, "ffn1", DFF // FF, ffn_gate, stats(8), [])
            dve.wait_ge(S_("mixer_params"), FINAL_PARAMS)
            for t in (2, 3):
                dve.wait_ge(S_("scaled"), norm_count(8, t + 1))
                nc.vector.tensor_tensor(acc[:, t, :], acc[:, t, :], rowp[:, 0, :], ALU.mult).then_inc(S_("result_dve"), 1)


INPUTS = ["x", "gla_w_in", "gla_w_gate_up", "gla_b_gate", "gla_norm_g", "gla_w_out", "nsa_w_in", "nsa_w_cmp_k1",
          "nsa_w_cmp_k2", "nsa_w_cmp_v1", "nsa_w_cmp_v2", "nsa_cmp_pe", "nsa_w_out", "moe_w_router", "moe_b_router",
          "moe_w_gate", "moe_w_up", "moe_w_down", "ln_g", "ln_b", "ev_norm_g_2", "ev_w_in_2", "ev_sinks_2",
          "ev_conv_w_2", "ev_conv_b_2", "ev_conv_ln_g_2", "ev_conv_ln_b_2", "ev_w_out_2", "od_norm_g_2",
          "od_w_in_2", "od_sgu_ln_g_2", "od_sgu_ln_b_2", "od_spatial_w_2", "od_spatial_b_2", "od_w_out_2",
          "ffn_norm_g_2", "ffn_w_gate_2", "ffn_w_up_2", "ffn_w_down_2", "final_norm_g_2"]


def kernel(**inputs):
    import concourse.bacc as bacc
    from concourse.bass_utils import run_bass_kernel_spmd

    nc = bacc.Bacc("TRN2", target_bir_lowering=False, num_devices=1)
    arrays = {name: np.ascontiguousarray(inputs[name]) for name in INPUTS}
    arrays["consts"] = constants()
    tensors = {n: nc.dram_tensor("in_" + n, v.shape, F32, kind="ExternalInput").ap() for n, v in arrays.items()}
    out = nc.dram_tensor("out", (1, S, D), F32, kind="ExternalOutput").ap()
    build(nc, tensors, out)
    r = run_bass_kernel_spmd(nc, [{"in_" + n: v for n, v in arrays.items()}], core_ids=[0])
    return r.results[0]["out"]
```
